# Optimizing a Trainium2 kernel written in Bass

```python
import math
import jax, jax.numpy as jnp
from jax import lax
import numpy as np

D_MODEL = 1024
BATCH = 1
SEQ = 256
DEPTH = 2

HYENA_WIDTH = D_MODEL // 2
HYENA_ORDER = 2
SHORT_CONV = 3
FILTER_EMB = 33
FILTER_HIDDEN = 64
HYENA_TARGET = 1e-2
FAST_DECAY_PCT = 0.3
SLOW_DECAY_PCT = 1.5
N_DIFF_HEADS = 4
DIFF_HEAD_DIM = 64
DIFF_V_DIM = 2 * DIFF_HEAD_DIM
QK_WIDTH = N_DIFF_HEADS * 2 * DIFF_HEAD_DIM
ATTN_WIDTH = N_DIFF_HEADS * DIFF_V_DIM
ROPE_THETA = 10000.0
Q_BLOCK = 128
N_BRANCHES = 2
IN_WIDTH = 3 * HYENA_WIDTH + 2 * QK_WIDTH + ATTN_WIDTH + N_BRANCHES * D_MODEL
D_FF = 2752
N_EXPERTS = 8
TOP_K = 2
MOE_BLOCK = 128
N_DENSE = (DEPTH + 1) // 2
N_MOE = DEPTH // 2
RMS_EPS = 1e-6

kernel_name = "hybrid_hyena_diffattn_moe_encoder"

F32 = jnp.float32

def rms_norm(x, g):
    xf = x.astype(F32)
    y = xf * lax.rsqrt(jnp.mean(xf * xf, axis=-1, keepdims=True) + RMS_EPS)
    return (y * g.astype(F32)).astype(x.dtype)

def rope_tables(L, dim):
    inv = 1.0 / (ROPE_THETA ** (jnp.arange(0, dim, 2, dtype=F32) / dim))
    ang = jnp.arange(L, dtype=F32)[:, None] * inv[None, :]
    return jnp.cos(ang), jnp.sin(ang)

def apply_rope(x, cos, sin):
    xf = x.astype(F32)
    x1, x2 = jnp.split(xf, 2, axis=-1)
    c = cos[None, :, None, None, :]
    s = sin[None, :, None, None, :]
    return jnp.concatenate([x1 * c - x2 * s, x1 * s + x2 * c], axis=-1).astype(x.dtype)

def centred_short_conv(u, w):
    L = u.shape[1]
    pad = SHORT_CONV // 2
    up = jnp.pad(u, ((0, 0), (pad, SHORT_CONV - 1 - pad), (0, 0)))
    out = up[:, 0:L] * w[0]
    for i in range(1, SHORT_CONV):
        out = out + up[:, i:i + L] * w[i]
    return out

def hyena_filters(L, w_f1, b_f1, freq1, w_f2, b_f2, freq2, w_f3):
    bands = (FILTER_EMB - 1) // 2
    t = jnp.linspace(0.0, 1.0, L, dtype=F32)[:, None]
    w = 2.0 * math.pi * jnp.arange(L, dtype=F32)[:, None] / L
    f = jnp.linspace(1e-4, bands - 1, bands, dtype=F32)[None, :]
    z = jnp.concatenate([t, jnp.cos(f * w), -jnp.sin(f * w)], axis=-1)
    hdn = jnp.sin(freq1.astype(F32) * (z @ w_f1.astype(F32) + b_f1.astype(F32)))
    hdn = jnp.sin(freq2.astype(F32) * (hdn @ w_f2.astype(F32) + b_f2.astype(F32)))
    hf = hdn @ w_f3.astype(F32)
    max_decay = math.log(HYENA_TARGET) / FAST_DECAY_PCT
    min_decay = math.log(HYENA_TARGET) / SLOW_DECAY_PCT
    deltas = jnp.linspace(min_decay, max_decay, HYENA_WIDTH, dtype=F32)
    decay = jnp.exp(-t * jnp.abs(deltas)[None, :])
    hf = hf.reshape(L, HYENA_ORDER, 2, HYENA_WIDTH) * decay[:, None, None, :]
    fwd = hf[:, :, 0]
    bwd = hf[:, :, 1]
    kern = jnp.concatenate([fwd, jnp.zeros_like(fwd[:1]), bwd[1:][::-1]], axis=0)
    return jnp.fft.rfft(kern, axis=0)

def bidir_long_conv(z, kf, bias):
    L = z.shape[1]
    zf32 = z.astype(F32)
    zf = jnp.fft.rfft(zf32, n=2 * L, axis=1)
    y = jnp.fft.irfft(zf * kf[None], n=2 * L, axis=1)[:, :L]
    return (y + zf32 * bias.astype(F32)).astype(z.dtype)

def hyena_mixer(u, conv_w, filt, hy_bias):
    u = centred_short_conv(u, conv_w)
    x1, x2, v = jnp.split(u, 3, axis=-1)
    z = x1 * bidir_long_conv(v, filt[:, 0], hy_bias[0])
    return x2 * bidir_long_conv(z, filt[:, 1], hy_bias[1])

def diff_attention(q, k, v, lam, lambda_init, subln_g):
    B, L = q.shape[0], q.shape[1]
    nb = L // Q_BLOCK
    qb = q.reshape(B, nb, Q_BLOCK, N_DIFF_HEADS, 2, DIFF_HEAD_DIM).transpose(1, 0, 2, 3, 4, 5)
    scale = DIFF_HEAD_DIM ** -0.5

    def block(qblk):
        s = jnp.einsum('bqhcd,bkhcd->bhcqk', qblk, k, preferred_element_type=F32) * scale
        p = jax.nn.softmax(s, axis=-1)
        a = p[:, :, 0] - lam * p[:, :, 1]
        return jnp.einsum('bhqk,bkhe->bqhe', a.astype(v.dtype), v)

    o = lax.map(block, qb)
    o = o.transpose(1, 0, 2, 3, 4).reshape(B, L, N_DIFF_HEADS, DIFF_V_DIM)
    o = rms_norm(o, subln_g) * (1.0 - lambda_init)
    return o.reshape(B, L, ATTN_WIDTH)

def hybrid_mixer(x, norm_g, w_in, conv_w, w_f1, b_f1, freq1, w_f2, b_f2, freq2, w_f3, hy_bias,
                 q_norm, k_norm, lam_q1, lam_k1, lam_q2, lam_k2, subln_g, w_hy_o, w_at_o, w_out,
                 lambda_init, cos, sin):
    B, L, _ = x.shape
    h = rms_norm(x, norm_g)
    proj = h @ w_in
    s1 = 3 * HYENA_WIDTH
    s2 = s1 + QK_WIDTH
    s3 = s2 + QK_WIDTH
    s4 = s3 + ATTN_WIDTH
    hy_in = proj[..., :s1]
    q = proj[..., s1:s2].reshape(B, L, N_DIFF_HEADS, 2, DIFF_HEAD_DIM)
    k = proj[..., s2:s3].reshape(B, L, N_DIFF_HEADS, 2, DIFF_HEAD_DIM)
    v = proj[..., s3:s4].reshape(B, L, N_DIFF_HEADS, DIFF_V_DIM)
    gates = jax.nn.sigmoid(proj[..., s4:].astype(F32)).reshape(B, L, N_BRANCHES, D_MODEL)
    filt = hyena_filters(L, w_f1, b_f1, freq1, w_f2, b_f2, freq2, w_f3)
    y_h = hyena_mixer(hy_in, conv_w, filt, hy_bias)
    q = apply_rope(rms_norm(q, q_norm), cos, sin)
    k = apply_rope(rms_norm(k, k_norm), cos, sin)
    lam = (jnp.exp(jnp.sum(lam_q1.astype(F32) * lam_k1.astype(F32)))
           - jnp.exp(jnp.sum(lam_q2.astype(F32) * lam_k2.astype(F32))) + lambda_init)
    y_a = diff_attention(q, k, v, lam, lambda_init, subln_g)
    merged = (gates[..., 0, :] * (y_h @ w_hy_o).astype(F32)
              + gates[..., 1, :] * (y_a @ w_at_o).astype(F32))
    return merged.astype(x.dtype) @ w_out

def swiglu(x, w_gate, w_up, w_down):
    return (jax.nn.silu(x @ w_gate) * (x @ w_up)) @ w_down

def moe_ffn(x, w_router, w_gate, w_up, w_down):
    B, L, D = x.shape
    T = B * L
    xt = x.reshape(T, D)
    logits = (xt @ w_router).astype(F32)
    top_val, top_idx = lax.top_k(logits, TOP_K)
    top_w = jax.nn.softmax(top_val, axis=-1)
    A = T * TOP_K
    e_flat = top_idx.reshape(A).astype(jnp.int32)
    tok = jnp.arange(A, dtype=jnp.int32) // TOP_K
    order = jnp.argsort(e_flat)
    e_s = e_flat[order]
    tok_s = tok[order]
    w_s = top_w.reshape(A)[order]
    counts = jnp.bincount(e_flat, length=N_EXPERTS).astype(jnp.int32)
    starts = jnp.cumsum(counts) - counts
    padded = (counts + MOE_BLOCK - 1) // MOE_BLOCK * MOE_BLOCK
    pad_end = jnp.cumsum(padded)
    pad_start = pad_end - padded
    dest = pad_start[e_s] + (jnp.arange(A, dtype=jnp.int32) - starts[e_s])
    n_blocks = -(-A // MOE_BLOCK) + N_EXPERTS
    P = n_blocks * MOE_BLOCK
    xp = jnp.zeros((P, D), x.dtype).at[dest].set(xt[tok_s])
    block_start = jnp.arange(n_blocks, dtype=jnp.int32) * MOE_BLOCK
    block_e = jnp.minimum(jnp.searchsorted(pad_end, block_start, side='right'), N_EXPERTS - 1)

    def run(args):
        xb, e = args
        return swiglu(xb, w_gate[e], w_up[e], w_down[e])

    yp = lax.map(run, (xp.reshape(n_blocks, MOE_BLOCK, D), block_e)).reshape(P, D)
    contrib = yp[dest] * w_s[:, None].astype(x.dtype)
    out = jnp.zeros((T, D), x.dtype).at[tok_s].add(contrib)
    return out.reshape(B, L, D)

def setup_inputs(seed: int = 0) -> dict:
    key = jax.random.key(seed)
    ks = jax.random.split(key, 32)
    n = lambda k, shape, s: jax.random.normal(k, shape, F32) * s
    gain = lambda k, shape: 1.0 + 0.02 * jax.random.normal(k, shape, F32)
    HW = HYENA_WIDTH
    return {
        'x': jax.random.normal(ks[0], (BATCH, SEQ, D_MODEL), F32),
        'norm_mix': gain(ks[1], (DEPTH, D_MODEL)),
        'w_in': n(ks[2], (DEPTH, D_MODEL, IN_WIDTH), D_MODEL ** -0.5),
        'conv_w': n(ks[3], (DEPTH, SHORT_CONV, 3 * HW), SHORT_CONV ** -0.5),
        'w_f1': n(ks[4], (DEPTH, FILTER_EMB, FILTER_HIDDEN), FILTER_EMB ** -0.5),
        'b_f1': n(ks[5], (DEPTH, FILTER_HIDDEN), 0.1),
        'freq1': gain(ks[6], (DEPTH, FILTER_HIDDEN)),
        'w_f2': n(ks[7], (DEPTH, FILTER_HIDDEN, FILTER_HIDDEN), FILTER_HIDDEN ** -0.5),
        'b_f2': n(ks[8], (DEPTH, FILTER_HIDDEN), 0.1),
        'freq2': gain(ks[9], (DEPTH, FILTER_HIDDEN)),
        'w_f3': n(ks[10], (DEPTH, FILTER_HIDDEN, HYENA_ORDER * 2 * HW), (FILTER_HIDDEN * SEQ / 8.0) ** -0.5),
        'hy_bias': n(ks[11], (DEPTH, HYENA_ORDER, HW), 0.3),
        'q_norm': gain(ks[12], (DEPTH, DIFF_HEAD_DIM)),
        'k_norm': gain(ks[13], (DEPTH, DIFF_HEAD_DIM)),
        'lam_q1': n(ks[14], (DEPTH, DIFF_HEAD_DIM), 0.1),
        'lam_k1': n(ks[15], (DEPTH, DIFF_HEAD_DIM), 0.1),
        'lam_q2': n(ks[16], (DEPTH, DIFF_HEAD_DIM), 0.1),
        'lam_k2': n(ks[17], (DEPTH, DIFF_HEAD_DIM), 0.1),
        'subln_g': gain(ks[18], (DEPTH, DIFF_V_DIM)),
        'w_hy_o': n(ks[19], (DEPTH, HW, D_MODEL), HW ** -0.5),
        'w_at_o': n(ks[20], (DEPTH, ATTN_WIDTH, D_MODEL), ATTN_WIDTH ** -0.5),
        'w_out': n(ks[21], (DEPTH, D_MODEL, D_MODEL), D_MODEL ** -0.5),
        'norm_ffn': gain(ks[22], (DEPTH, D_MODEL)),
        'w_dense_gate': n(ks[23], (N_DENSE, D_MODEL, D_FF), D_MODEL ** -0.5),
        'w_dense_up': n(ks[24], (N_DENSE, D_MODEL, D_FF), D_MODEL ** -0.5),
        'w_dense_down': n(ks[25], (N_DENSE, D_FF, D_MODEL), D_FF ** -0.5),
        'w_router': n(ks[26], (N_MOE, D_MODEL, N_EXPERTS), D_MODEL ** -0.5),
        'w_moe_gate': n(ks[27], (N_MOE, N_EXPERTS, D_MODEL, D_FF), D_MODEL ** -0.5),
        'w_moe_up': n(ks[28], (N_MOE, N_EXPERTS, D_MODEL, D_FF), D_MODEL ** -0.5),
        'w_moe_down': n(ks[29], (N_MOE, N_EXPERTS, D_FF, D_MODEL), D_FF ** -0.5),
    }

def reference(x, norm_mix, w_in, conv_w, w_f1, b_f1, freq1, w_f2, b_f2, freq2, w_f3, hy_bias,
              q_norm, k_norm, lam_q1, lam_k1, lam_q2, lam_k2, subln_g, w_hy_o, w_at_o, w_out,
              norm_ffn, w_dense_gate, w_dense_up, w_dense_down, w_router, w_moe_gate, w_moe_up,
              w_moe_down):
    L = x.shape[1]
    cos, sin = rope_tables(L, DIFF_HEAD_DIM)
    for layer in range(DEPTH):
        lambda_init = 0.8 - 0.6 * math.exp(-0.3 * layer)
        x = x + hybrid_mixer(
            x, norm_mix[layer], w_in[layer], conv_w[layer], w_f1[layer], b_f1[layer], freq1[layer],
            w_f2[layer], b_f2[layer], freq2[layer], w_f3[layer], hy_bias[layer], q_norm[layer],
            k_norm[layer], lam_q1[layer], lam_k1[layer], lam_q2[layer], lam_k2[layer], subln_g[layer],
            w_hy_o[layer], w_at_o[layer], w_out[layer], lambda_init, cos, sin)
        h = rms_norm(x, norm_ffn[layer])
        i = layer // 2
        if layer % 2 == 0:
            x = x + swiglu(h, w_dense_gate[i], w_dense_up[i], w_dense_down[i])
        else:
            x = x + moe_ffn(h, w_router[i], w_moe_gate[i], w_moe_up[i], w_moe_down[i])
    return x


_drawn_inputs = setup_inputs


def setup_inputs(seed=0):
    import zlib

    import numpy as np

    out = dict(_drawn_inputs(seed))
    spreads = {}
    factors = {'freq1': 2.934, 'freq2': 3.588}
    for name, (base, spread) in spreads.items():
        noise = np.random.default_rng([zlib.crc32(name.encode()), seed]).standard_normal(out[name].shape)
        drawn = base * np.exp(spread * noise) if base else spread * noise
        out[name] = __import__('jax').numpy.asarray(drawn.astype(out[name].dtype))
    for name, factor in factors.items():
        out[name] = (out[name] * factor).astype(out[name].dtype)
    return out
```

```python
from contextlib import ExitStack

import numpy as np

import concourse.bass as bass
from concourse import mybir

ALU = mybir.AluOpType
ACT = mybir.ActivationFunctionType
AX_X = mybir.AxisListType.X
F32 = mybir.dt.float32
F32R = mybir.dt.float32r
I32 = mybir.dt.int32

P = 128
D = 1024
T = 256
TB = T // P
DEPTH = 2
HW = D // 2
KD = D // P
NH, DH, DV = 4, 64, 128
FE, FH = 33, 64
FF = 2752
NE, TOPK = 8, 2
EPS = 1e-6

SLAB = 2048
RAW_SLOTS, SPLIT_SLOTS = 6, 3
CHUNK = 256
NCH = FF // CHUNK
TAIL = FF - NCH * CHUNK
MIX_SLABS = 28
FFN_SLABS = 3 * (NCH + 1)
XTRA = (T * TOPK) // (P + 1)
NBLK = NE + XTRA

FIRST = {("mix", 0): 0, ("ffn", 0): MIX_SLABS, ("mix", 1): MIX_SLABS + FFN_SLABS,
         ("ffn", 1): 2 * MIX_SLABS + FFN_SLABS}
STAGES = [("mix", 0), ("ffn", 0), ("mix", 1), ("ffn", 1)]
LENGTH = {"mix": MIX_SLABS, "ffn": FFN_SLABS}


def slot_uses(n):
    return [(n - s + RAW_SLOTS - 1) // RAW_SLOTS for s in range(RAW_SLOTS)]


def uses_before(stage):
    total = [0] * RAW_SLOTS
    for s in STAGES[:STAGES.index(stage)]:
        total = [a + b for a, b in zip(total, slot_uses(LENGTH[s[0]]))]
    return total


def back(p, *before):
    if p >= RAW_SLOTS:
        return RAW_SLOTS
    return min(p + n - max(q for q in range(n) if q % RAW_SLOTS == p) for n in before)


CHUNKS = ["v", "x1", "q", "x2", "k", "av", "g0", "g1", "g2", "g3"]
COLUMN = {"x1": 0, "x2": 512, "v": 1024, "q": 1536, "k": 2048, "av": 2560,
          "g0": 3072, "g1": 3584, "g2": 4096, "g3": 4608}

PLAN = [("f1", [0]), ("f2", [1]), ("hf0", [4, 5, 6, 7]), ("ft0", [0, 1, 2, 3]), ("hf1", [4, 5, 6, 7]),
        ("ft1", [0, 1, 2, 3]), ("ht", [4, 5, 6, 7]),
        ("v", [0, 1, 2, 3]), ("x1", [4, 5, 6, 7]), ("q", [0, 1]), ("vT", [2, 3]), ("x2", [4, 5, 6, 7]),
        ("k", [0, 1]), ("x1T", [2, 3]), ("av", [4, 5]), ("x2T", [6, 7]),
        ("cf0", [0, 1, 2, 3]), ("g0", [4, 5]), ("qT", [6, 7]), ("g1", [4, 5]), ("kT", [6, 7]),
        ("ci0", [0, 1]), ("g2", [2, 3]), ("cf1", [4, 5, 6, 7]), ("g3", [0, 1]),
        ("sc0", [2, 3]), ("ci1", [0, 1]), ("sc1", [4, 5]), ("aT0", [6]), ("sc2", [2, 3]), ("av0", [7]),
        ("aT1", [6]), ("sc3", [4, 5]), ("av1", [7]), ("aT2", [6]), ("yT", [0, 1]), ("av2", [7]),
        ("aT3", [6]), ("av3", [7]),
        ("ph0", [2, 3]), ("ph1", [4, 5]), ("yaT", [0, 1]), ("pa0", [6, 7]), ("pa1", [2, 3]),
        ("mT", [4, 5, 6, 7]), ("wo0", [0, 1]), ("wo1", [2, 3]), ("fht", [4, 5, 6, 7])]
PLAN_MOE = [("rt", [0]), ("pos", [1])]


BANKS = dict(PLAN + PLAN_MOE)

LAST_SLAB = {}
for _i, _c in enumerate(CHUNKS):
    LAST_SLAB[_c] = 2 * _i + 1
LAST_SLAB.update({"ph0": 20, "ph1": 21, "pa0": 22, "pa1": 23, "wo0": 25, "wo1": 27})


def turns(counted):
    count, out = [0] * 8, {}
    for layer in range(DEPTH):
        for step, banks in PLAN + (PLAN_MOE if layer == 1 else []):
            for b in banks:
                count[b] += int(counted(step))
                out[layer, step, b] = count[b]
    return out


FILLS = turns(lambda step: step not in LAST_SLAB)
DRAINS = turns(lambda step: 1)

ROUND = 12582912.0
TWO_PI = (6.28125, 0.0019350051879882812, 3.019916050561733e-07)
PI_BELOW = 3.1415925

Q_FIRST = [0, NCH + 1]
LAMBDA_INIT = [0.8 - 0.6 * float(np.exp(-0.3 * layer)) for layer in range(DEPTH)]

PAR_CONV, PAR_GM, PAR_GF, PAR_QN, PAR_KN, PAR_SUB = 0, 36, 44, 52, 116, 180
PAR_N = PAR_SUB + DV


def trunk(nc, x_in, slabs, par_d, lamv_d, wf1_d, wf2_d, bf_d, wf3_d, hyb_d, nffn_d, wr_d,
          cst_d, dft_d, decay_d, zt_d, moec_d, out):
    ctx = ExitStack()

    def sb(name, shape, dt=F32):
        return ctx.enter_context(nc.sbuf_tensor(name, shape, dt))

    def region(name, floats, variants):
        found = {}
        for variant in variants:
            inner = ExitStack()
            for n, shape, dt in variant:
                found[n] = inner.enter_context(nc.sbuf_tensor(n, shape, dt))
            assert sum(int(np.prod(s[1:])) for _, s, _ in variant) <= floats, name
            inner.close()
        sb(name, [P, floats])
        return found

    semaphores = {}

    def sem(name):
        if name not in semaphores:
            semaphores[name] = ctx.enter_context(nc.semaphore(name))
        return semaphores[name]

    RAW = sb("raw", [P, RAW_SLOTS, SLAB])
    HI = sb("w_hi", [P, SPLIT_SLOTS, SLAB], F32R)
    LO = sb("w_lo", [P, SPLIT_SLOTS, SLAB], F32R)
    X = sb("x", [P, TB, D])
    HTH = sb("hT_hi", [P, KD, T], F32R)
    HTL = sb("hT_lo", [P, KD, T], F32R)
    TMP = sb("tmp", [P, 1024])
    IDENT = sb("ident", [P, P])
    ROPE = sb("rope", [P, 2, TB, 32])
    PAR = sb("par", [P, PAR_N])
    STAT = sb("stat", [P, 80])
    LAM = sb("lam", [P, 8])
    HALF = sb("minus_half", [P, 16])
    SQUARES = sb("squares", [P, DV])
    R = {}
    R.update(region("r_h", 2 * 4 * 258, [[("h_tok", [P, TB, D], F32)], [("upad", [P, 2, 4, 258], F32)],
                                         [("qT", [P, NH, T], F32), ("kT", [P, NH, T], F32)]]))
    R.update(region("r_conv", 2048, [[("conv", [P, 2, 4, T], F32)], [("ys", [P, 2, 2, 512], F32)],
                                     [("act_hi", [P, 2, T], F32R), ("act_lo", [P, 2, T], F32R),
                                      ("silu", [P, TB, CHUNK], F32), ("act", [P, TB, CHUNK], F32)]]))
    late = [("g_row", [P, D], F32), ("moec", [P, 3 * P + 64 + 8 + 4], F32),
            ("wr", [P, KD, NE], F32), ("wr_hi", [P, KD, NE], F32R), ("wr_lo", [P, KD, NE], F32R),
            ("lg", [P, TB, NE], F32), ("cmp", [P, TB, NE, NE], F32), ("cmp2", [P, TB, NE, NE], F32),
            ("rank", [P, TB, NE], F32), ("sel1", [P, TB, NE], F32), ("sel2", [P, TB, NE], F32),
            ("sel", [P, TB, NE], F32), ("wts", [P, TB, NE], F32), ("posm", [P, TB, NE], F32),
            ("cnt", [P, NE], F32), ("over", [P, NE], F32), ("oh", [P, 4, NE], F32),
            ("pcol", [P, TB, NBLK + 1], F32), ("wcol", [P, TB, NBLK + 1], F32), ("tv", [P, 8, TB], F32),
            ("nbf", [P, 16], F32), ("nbi", [P, 16], I32), ("wcur", [P, TB], F32), ("wslot", [P, 1], F32),
            ("prod", [P, 4, NE], F32)]
    R.update(region("r_gate", 4096, [[("decay", [P, 2, 2, 512], F32), ("fpm", [P, 2, 2, 512], F32)],
                                     [("gates", [P, TB, 2, D], F32)],
                                     [("hg_hi", [P, TB, D], F32R), ("hg_lo", [P, TB, D], F32R)]]))
    R.update(region("r_xv", 3072, [[("fb", [P, 2, 512], F32), ("zT", [FE, T], F32), ("wf1", [FE, FH], F32),
                                    ("wf2", [FH, FH], F32), ("bf", [FH, 4], F32), ("lamv", [P, 4, DH], F32),
                                    ("arg", [FH, T], F32), ("rnd", [FH, T], F32), ("hdn", [FH, 2, T], F32)],
                                   [("xv", [P, 3, TB, HW], F32)],
                                   [("y_hi", [P, D], F32R), ("y_lo", [P, D], F32R),
                                    ("psel", [P, TB, P], F32R), ("pselT", [P, TB, P], F32R)]]))
    R.update(region("r_qkv", 3072, [[("wf3", [FH, 2048], F32), ("hyb", [1, 1024], F32)],
                                    [("qkv", [P, 3, TB, 512], F32)],
                                    [("e", [P, 2, 2, T], F32), ("a", [P, 2, T], F32), ("aT", [P, 2, T], F32)],
                                    late]))
    FSP = sb("filters", [P, 2, 2, 2, 512])
    DFT = sb("dft", [P, 4, 2, T])
    H_TOK, UPAD, QT, KT = R["h_tok"], R["upad"], R["qT"], R["kT"]
    CONV, YS = R["conv"], R["ys"]
    XV, QKV, GATES = R["xv"], R["qkv"], R["gates"]
    PS = [ctx.enter_context(nc.psum_tensor(f"bank{b}", [P, 512], F32)) for b in range(8)]

    raw_loaded = [sem(f"raw_loaded{s}") for s in range(RAW_SLOTS)]
    hi_ready, lo_ready, slab_used = sem("hi_ready"), sem("lo_ready"), sem("slab_used")
    filled = [sem(f"bank_filled{b}") for b in range(8)]
    drained = [sem(f"bank_drained{b}") for b in range(8)]
    silu_done, act_done = sem("silu_done"), sem("act_done")
    turned, act_hi_ready, act_lo_ready = sem("act_turned"), sem("act_hi_ready"), sem("act_lo_ready")
    y_hi_ready, y_ready = sem("y_hi_ready"), sem("y_ready")
    gathered, g_hi_ready, g_lo_ready = sem("gathered"), sem("g_hi_ready"), sem("g_lo_ready")
    psel_ready, pselT_done, pselT_ready = sem("psel_ready"), sem("pselT_done"), sem("pselT_ready")
    scattered, scatter_added = sem("scattered"), sem("scatter_added")

    class Steps:

        def __init__(self, eng, name):
            self.eng, self.own, self.count, self.last = eng, sem(name), 0, None

        def do(self, ins, signal=None, value=None):
            if signal is None:
                self.count += 1
                signal, value = self.own, self.count
            ins.then_inc(signal, 1)
            self.last = (signal, value)

        def settle(self):
            if self.last is not None:
                self.eng.wait_ge(*self.last)

    def event(name, layer):
        return sem(f"{name}_{layer}")

    def wait_filled(eng, layer, step, i):
        b = BANKS[step][i]
        if step in LAST_SLAB:
            eng.wait_ge(slab_used, FIRST["mix", layer] + LAST_SLAB[step] + 1)
        else:
            eng.wait_ge(filled[b], FILLS[layer, step, b])

    def bank(step, i):
        return PS[BANKS[step][i]]

    def drain_of(layer, step, i):
        b = BANKS[step][i]
        return drained[b], DRAINS[layer, step, b]

    def wait_drained(eng, layer, step, i):
        eng.wait_ge(*drain_of(layer, step, i))

    S_MAX, S_NEG, S_SUM, S_FAC = (STAT[:, 64 + 4 * i:68 + 4 * i] for i in range(4))

    def raw_value(stage, p):
        return 32 * (uses_before(stage)[p % RAW_SLOTS] + p // RAW_SLOTS + 1)

    def router(dve, v, tt, ts, stt):
        vec = nc.vector
        lg, cmp, cmp2, rank = R["lg"], R["cmp"], R["cmp2"], R["rank"]
        sel1, sel2, sel, wts, posm, tv = (R[k] for k in ("sel1", "sel2", "sel", "wts", "posm", "tv"))
        over, oh, prod, nbf = R["over"], R["oh"], R["prod"], R["nbf"]
        tril = R["moec"][:, 3 * P:3 * P + 64].rearrange("p (a b) -> p a b", a=NE)
        erow = R["moec"][:, 3 * P + 64:3 * P + 72]

        def flat(ap):
            return ap.rearrange("p a b -> p (a b)")

        def reduce(dst, src, signal=None, value=None):
            v.do(vec.tensor_reduce(dst, src, AX_X, ALU.add), signal, value)

        dve.wait_ge(sem("hg_hi_ready"), 1)
        tt(R["hg_lo"][:, :, :], H_TOK[:, :, :], R["hg_hi"][:, :, :].bitcast(F32), ALU.subtract,
           sem("hg_lo_ready"), 1)
        wait_filled(dve, 1, "rt", 0)
        v.do(vec.tensor_copy(flat(lg[:, :, :]), bank("rt", 0)[:, 0:TB * NE]), *drain_of(1, "rt", 0))
        v.settle()
        other = lg[:, :, :].unsqueeze(2).broadcast_to([P, TB, NE, NE])
        own = lg[:, :, :].unsqueeze(3).broadcast_to([P, TB, NE, NE])
        tt(cmp[:, :, :, :], other, own, ALU.is_gt)
        tt(cmp2[:, :, :, :], other, own, ALU.is_equal)
        v.settle()
        for tb in range(TB):
            tt(cmp2[:, tb, :, :], cmp2[:, tb, :, :], tril, ALU.mult)
        v.settle()
        tt(cmp[:, :, :, :], cmp[:, :, :, :], cmp2[:, :, :, :], ALU.add)
        v.settle()
        reduce(flat(rank[:, :, :]), cmp[:, :, :, :].rearrange("p t a b -> p (t a) b"))
        v.settle()
        ts(sel1[:, :, :], rank[:, :, :], 0.0, None, ALU.is_equal)
        ts(sel2[:, :, :], rank[:, :, :], 1.0, None, ALU.is_equal)
        v.settle()
        tt(sel[:, :, :], sel1[:, :, :], sel2[:, :, :], ALU.add, sem("sel_ready"), 1)
        tt(cmp[:, :, 0, :], sel1[:, :, :], lg[:, :, :], ALU.mult)
        tt(cmp[:, :, 1, :], sel2[:, :, :], lg[:, :, :], ALU.mult)
        v.settle()
        reduce(tv[:, 0, :], cmp[:, :, 0, :])
        reduce(tv[:, 1, :], cmp[:, :, 1, :])
        v.settle()
        tt(tv[:, 2, :], tv[:, 1, :], tv[:, 0, :], ALU.subtract, sem("top_diff"), 1)
        dve.wait_ge(sem("top_exp"), 1)
        ts(tv[:, 4, :], tv[:, 3, :], 1.0, None, ALU.add)
        v.settle()
        v.do(vec.reciprocal(tv[:, 5, :], tv[:, 4, :]))
        v.settle()
        tt(tv[:, 6, :], tv[:, 3, :], tv[:, 5, :], ALU.mult)
        v.settle()
        for tb in range(TB):
            ts(wts[:, tb, :], sel1[:, tb, :], tv[:, 5, tb:tb + 1], None, ALU.mult)
        v.settle()
        for tb in range(TB):
            stt(wts[:, tb, :], sel2[:, tb, :], tv[:, 6, tb:tb + 1], wts[:, tb, :], ALU.mult, ALU.add)
        wait_filled(dve, 1, "pos", 0)
        stt(flat(posm[:, :, :]), bank("pos", 0)[:, 0:TB * NE], 1.0, flat(sel[:, :, :]), ALU.add, ALU.mult)
        ts(over[:, :], bank("pos", 0)[:, TB * NE:(TB + 1) * NE], float(P), None, ALU.is_gt, None,
           *drain_of(1, "pos", 0))
        v.settle()
        ts(posm[:, :, :], posm[:, :, :], -1.0, None, ALU.add)
        tt(cmp[:, 0, :, :], over[:, :].unsqueeze(1).broadcast_to([P, NE, NE]), tril, ALU.mult)
        v.settle()
        reduce(R["cnt"][:, :], cmp[:, 0, :, :])
        v.settle()
        for j in range(XTRA):
            stt(oh[:, j, :], R["cnt"][:, :], float(j), over[:, :], ALU.is_equal, ALU.mult)
        v.do(vec.memset(R["pcol"][:, :, NBLK:NBLK + 1], -1.0))
        v.do(vec.memset(R["wcol"][:, :, NBLK:NBLK + 1], 0.0))
        v.do(vec.memset(nbf[:, :], 0.0))
        v.settle()
        for tb in range(TB):
            v.do(vec.tensor_copy(R["pcol"][:, tb, 0:NE], posm[:, tb, :]))
            v.do(vec.tensor_copy(R["wcol"][:, tb, 0:NE], wts[:, tb, :]))
            for src, dst in ((posm, R["pcol"]), (wts, R["wcol"])):
                tt(prod[:, 0:XTRA, :], oh[:, 0:XTRA, :], src[:, tb, :].unsqueeze(1).broadcast_to([P, XTRA, NE]),
                   ALU.mult)
                v.settle()
                reduce(dst[:, tb, NE:NBLK], prod[:, 0:XTRA, :])
                v.settle()
            ts(R["pcol"][:, tb, NE:NBLK], R["pcol"][:, tb, NE:NBLK], -float(P), None, ALU.add)
        v.settle()
        tt(prod[:, 0:XTRA, :], oh[:, 0:XTRA, :], erow.unsqueeze(1).broadcast_to([P, XTRA, NE]), ALU.mult)
        reduce(nbf[:, 0:1], over[:, :])
        v.settle()
        reduce(nbf[:, NE:NBLK], prod[:, 0:XTRA, :])
        ts(nbf[:, 0:1], nbf[:, 0:1], float(NE), None, ALU.add)
        v.settle()
        v.do(vec.tensor_copy(R["nbi"][:, :], nbf[:, :]), sem("blocks_known"), 1)
        v.do(vec.memset(R["wslot"][:, :], 0.0))
        v.do(vec.memset(R["pselT"][:, :, :].bitcast(F32), 0.0))
        v.settle()

    block = ctx.enter_context(nc.Block())

    @block.sync
    def _(sp):
        def mixer_slabs(layer):
            w_in, w_hy, w_at, w_out = (slabs[k][layer] for k in ("w_in", "w_hy_o", "w_at_o", "w_out"))
            found = []
            for c in CHUNKS:
                for k in (0, 4):
                    found.append(w_in[k * P:(k + 4) * P, COLUMN[c]:COLUMN[c] + 512])
            for w in (w_hy, w_at):
                for h in range(2):
                    found.append(w[:, h * 512:(h + 1) * 512])
            for h in range(2):
                for k in (0, 4):
                    found.append(w_out[k * P:(k + 4) * P, h * 512:(h + 1) * 512])
            return found

        def put(p, dst, src, free):
            if free is not None:
                sp.wait_ge(lo_ready, free)
            for d, s in zip(dst, src):
                sp.dma_start(d, s).then_inc(raw_loaded[p % RAW_SLOTS], 16)

        sp.dma_start(X[:, :, :], x_in.rearrange("(t p) d -> p t d", p=P)).then_inc(sem("x_loaded"), 16)
        for layer in range(DEPTH):
            first = FIRST["mix", layer]
            for p, src in enumerate(mixer_slabs(layer)):
                dst = RAW[:, p % RAW_SLOTS, :].rearrange("p (k n) -> p k n", k=4)
                src = src.rearrange("(k p) n -> p k n", p=P)
                free = None if first + p < RAW_SLOTS else first + p - back(p, FFN_SLABS) + 1
                put(p, [dst[:, 0:2, :], dst[:, 2:4, :]], [src[:, 0:2, :], src[:, 2:4, :]], free)

            first = FIRST["ffn", layer]
            kind = "dense" if layer == 0 else "moe"
            w_gate, w_up, w_down = (slabs[f"w_{kind}_{k}"] for k in ("gate", "up", "down"))
            lengths = (MIX_SLABS,) if layer == 0 else (MIX_SLABS, FFN_SLABS)

            def gate_up(e, p, n, part, col, width):
                dst = RAW[:, p % RAW_SLOTS, 0:8 * width].rearrange("p (k n) -> p k n", k=4)
                src = [w[e, 4 * part * P:4 * (part + 1) * P, col].rearrange("o (k p) n -> p (o k) n", p=P)
                       for w in (w_gate, w_up)]
                put(p, [dst[:, :, 0:width], dst[:, :, width:2 * width]], src, n - back(p, *lengths) + 1)

            def down(e, p, n, rows, heights=(P, P)):
                dst = RAW[:, p % RAW_SLOTS, :].rearrange("p (k n) -> p k n", k=2)
                src = [w_down[e, r, :].rearrange("o p n -> p (o n)") for r in rows]
                put(p, [dst[0:heights[j], j, :] for j in range(2)], src, n - back(p, *lengths) + 1)

            def chunk_rows(c):
                return [slice(c * CHUNK, c * CHUNK + P), slice(c * CHUNK + P, (c + 1) * CHUNK)]

            def pair(e, n0, i, p0):
                for j in range(2):
                    p = p0 + 3 * j
                    for part in range(2):
                        gate_up(e, p + part, n0 + p + part, part,
                                slice((2 * i + j + 1) * CHUNK, (2 * i + j + 2) * CHUNK), CHUNK)
                    down(e, p + 2, n0 + p + 2, chunk_rows(2 * i + j))

            def block_slabs(n0, e):
                for part in range(2):
                    gate_up(e, part, n0 + part, part, slice(0, CHUNK), CHUNK)
                pair(e, n0, 0, 2)
                with sp.Fori(1, 4) as i:
                    ni = sp.snap(n0 + 6 * i)
                    for j in range(2):
                        col = bass.ds(sp.snap((2 * i + j + 1) * CHUNK), CHUNK)
                        r0 = sp.snap((2 * i + j) * CHUNK)
                        for part in range(2):
                            p = 2 + 3 * j + part
                            gate_up(e, p + RAW_SLOTS, ni + p, part, col, CHUNK)
                        p = 4 + 3 * j
                        down(e, p + RAW_SLOTS, ni + p, [bass.ds(r0, P), bass.ds(sp.snap(r0 + P), P)])
                c = NCH - 1
                for part in range(2):
                    gate_up(e, 26 + part, n0 + 26 + part, part, slice(c * CHUNK, (c + 1) * CHUNK), CHUNK)
                down(e, 28, n0 + 28, chunk_rows(c - 1))
                for part in range(2):
                    gate_up(e, 29 + part, n0 + 29 + part, part, slice(NCH * CHUNK, FF), TAIL)
                down(e, 31, n0 + 31, chunk_rows(c))
                down(e, 32, n0 + 32, [slice(NCH * CHUNK, NCH * CHUNK + P), slice(NCH * CHUNK + P, FF)],
                     (P, TAIL - P))

            if layer == 0:
                block_slabs(first, slice(0, 1))
            else:
                with sp.Fori(0, NE) as b:
                    block_slabs(sp.snap(FFN_SLABS * b + first), bass.ds(b, 1))
                sp.wait_ge(sem("blocks_known"), 1)
                nb = sp.value_load(R["nbi"][0:1, 0:1], min_val=NE, max_val=NBLK)
                with sp.If(nb > NE):
                    with sp.Fori(NE, nb) as b:
                        e = sp.value_load(R["nbi"][0:1, bass.ds(b, 1)], min_val=0, max_val=NE - 1)
                        block_slabs(sp.snap(FFN_SLABS * b + first), bass.ds(e, 1))
                n0 = sp.snap(FFN_SLABS * nb + first)
                e = slice(0, 1)
                for part in range(2):
                    gate_up(e, part, n0 + part, part, slice(0, CHUNK), CHUNK)
                gate_up(e, 2, n0 + 2, 0, slice(CHUNK, 2 * CHUNK), CHUNK)
        sp.wait_ge(scatter_added, 4 * nb + 4)
        sp.dma_start(out.rearrange("(t p) d -> p t d", p=P), X[:, :, :]).then_inc(sem("stored"), 16)
        sp.wait_ge(sem("stored"), 16)

    @block.gpsimd
    def _(pool):
        g = Steps(pool, "pool_steps")
        pool.dma_start(IDENT[:, :], cst_d[:, 0:P]).then_inc(sem("cst_loaded"), 16)
        pool.dma_start(ROPE[:, :, :, :].rearrange("p a b c -> p (a b c)"), cst_d[:, P:2 * P])\
            .then_inc(sem("cst_loaded"), 16)
        pool.dma_start(DFT[:, :, :, :].rearrange("p a b c -> p (a b c)"), dft_d).then_inc(sem("cst_loaded"), 16)

        def rstd(layer, name, src, dst, n, width):
            pool.wait_ge(event(f"{name}_ss", layer), 1)
            g.do(nc.gpsimd.tensor_scalar(dst, src, 1.0 / width, EPS, ALU.mult, ALU.add))
            g.settle()
            s = event(f"{name}_rstd", layer)
            g.do(nc.gpsimd.tensor_tensor(dst, dst, HALF[:, 0:n], ALU.pow), s, 1)

        g.do(nc.gpsimd.memset(HALF[:, :], -0.5))
        g.settle()
        for layer in range(DEPTH):
            loaded = event("par_loaded", layer)
            if layer:
                wait_drained(pool, layer - 1, "fht", 3)
            for dst, src in ((R["zT"][:, :], zt_d), (R["wf1"][:, :], wf1_d[layer]), (R["wf2"][:, :], wf2_d[layer]),
                             (R["bf"][:, :], bf_d[layer]), (R["wf3"][:, :], wf3_d[layer]),
                             (PAR[:, :], par_d[layer]),
                             (R["decay"][:, :, :, :].rearrange("p a b c -> p (a b c)"), decay_d),
                             (R["lamv"][:, :, :].rearrange("p a b -> p (a b)"), lamv_d[layer:layer + 1, :].to_broadcast([P, 4 * DH])),
                             (R["hyb"][:, :], hyb_d[layer:layer + 1, :])):
                pool.dma_start(dst, src).then_inc(loaded, 16)
            rstd(layer, "norm_mix", STAT[:, 0:TB], STAT[:, 2:2 + TB], TB, D)
            rstd(layer, "q", STAT[:, 8:24], STAT[:, 24:40], 16, DH)
            rstd(layer, "k", STAT[:, 8:24], STAT[:, 40:56], 16, DH)
            for h in range(NH):
                pool.wait_ge(event("o_ss", layer), h + 1)
                g.do(nc.gpsimd.tensor_scalar(STAT[:, 60:62], STAT[:, 56 + 2 * (h % 2):58 + 2 * (h % 2)],
                                             1.0 / DV, EPS, ALU.mult, ALU.add))
                g.settle()
                g.do(nc.gpsimd.tensor_tensor(STAT[:, 4 + 2 * (h % 2):6 + 2 * (h % 2)], STAT[:, 60:62],
                                             HALF[:, 0:TB], ALU.pow), event("o_rstd", layer), h + 1)
            if layer == 1:
                wait_drained(pool, layer, "wo1", 1)
                pool.dma_start(R["g_row"][:, :], nffn_d.to_broadcast([P, D])).then_inc(sem("moe_loaded"), 16)
                pool.dma_start(R["wr"][:, :, :], wr_d.rearrange("(k p) e -> p k e", p=P)).then_inc(sem("moe_loaded"), 16)
                pool.dma_start(R["moec"][:, :], moec_d).then_inc(sem("moe_loaded"), 16)
            rstd(layer, "norm_ffn", STAT[:, 0:TB], STAT[:, 2:2 + TB], TB, D)

    @block.scalar
    def _(act):
        a = Steps(act, "act_steps")
        done = [0]

        def copy(dst, src, signal=None, value=None, **kw):
            a.do(nc.scalar.activation(dst, src, ACT.Copy, **kw), signal, value)

        def split(n, slot_value, raw_slot, split_slot, width=SLAB):
            act.wait_ge(raw_loaded[raw_slot], slot_value)
            if not isinstance(n, int) or n >= SPLIT_SLOTS:
                act.wait_ge(slab_used, n - (SPLIT_SLOTS - 1))
            nc.scalar.activation(HI[:, split_slot, 0:width], RAW[:, raw_slot, 0:width], ACT.Copy)\
              .then_inc(hi_ready, 1)

        def split_to(last, stage):
            first = FIRST[stage]
            while done[0] <= min(last, first + LENGTH[stage[0]] - 1):
                n = done[0]
                p = n - first
                split(n, raw_value(stage, p), p % RAW_SLOTS, n % SPLIT_SLOTS)
                done[0] += 1

        for layer in range(DEPTH):
            stage = ("mix", layer)
            first = FIRST[stage]

            def ahead(step):
                split_to(first + LAST_SLAB[step] + 2, stage)

            def evac(step, i, dst, src=None, **kw):
                wait_filled(act, layer, step, i)
                copy(dst, bank(step, i)[:, :] if src is None else src, *drain_of(layer, step, i), **kw)

            act.wait_ge(sem("x_loaded") if layer == 0 else event("ffn_added", 0), 16 if layer == 0 else 1)
            for tb in range(TB):
                a.do(nc.scalar.activation(H_TOK[:, tb, :], X[:, tb, :], ACT.Square,
                                          accum_out=STAT[:, tb:tb + 1]),
                     *((event("norm_mix_ss", layer), 1) if tb == TB - 1 else (None, None)))
            act.wait_ge(event("lam_sums", layer), 1)
            a.do(nc.scalar.activation(LAM[:, 2:4], LAM[:, 0:2], ACT.Exp), event("lam_exp", layer), 1)
            for j in range(2):
                act.wait_ge(event("sin_arg", layer), j + 1)
                a.do(nc.scalar.activation(R["hdn"][:, j, :], R["rnd"][:, :], ACT.Sin), event("sin_done", layer), j + 1)
            for o in range(2):
                for i in range(4):
                    evac(f"ft{o}", i, FSP[:, i // 2, o, i % 2, :], scale=1.0 / T)
            split_to(first + 2, stage)
            for i in range(4):
                wait_filled(act, layer, "ht", i)
                for j in range(2):
                    kd = 2 * i + j
                    copy(HTH[:, kd, :], bank("ht", i)[:, j * T:(j + 1) * T], event("ht_hi", layer), kd + 1,
                         scale=PAR[:, PAR_GM + kd:PAR_GM + kd + 1])
            act.wait_ge(event("pads", layer), 1)
            for step, _ in PLAN[PLAN.index(("v", [0, 1, 2, 3])):]:
                if step in LAST_SLAB:
                    ahead(step)
                if step in ("v", "x1", "x2"):
                    c = ("v", "x1", "x2").index(step)
                    if c == 2:
                        act.wait_ge(event("conv_done", layer), 4)
                    for i in range(4):
                        evac(step, i, UPAD[:, c % 2, i, 1:T + 1], bank(step, i)[:, 0:T])
                elif step in ("q", "k", "av"):
                    if step == "q":
                        act.wait_ge(event("fpm", layer), 4)
                    c = ("q", "k", "av").index(step)
                    for tb in range(TB):
                        evac(step, tb, QKV[:, c, tb, :])
                elif step in ("vT", "x1T", "x2T"):
                    c = ("x1T", "x2T", "vT").index(step)
                    for tb in range(TB):
                        evac(step, tb, XV[:, c, tb, :])
                elif step in ("g0", "g1", "g2", "g3"):
                    c = int(step[1])
                    for tb in range(TB):
                        wait_filled(act, layer, step, tb)
                        a.do(nc.scalar.activation(GATES[:, tb, c // 2, (c % 2) * 512:(c % 2 + 1) * 512],
                                                  bank(step, tb)[:, :], ACT.Sigmoid), *drain_of(layer, step, tb))
                elif step in ("qT", "kT"):
                    act.wait_ge(event("conv_done", layer), 12)
                    dst = QT if step == "qT" else KT
                    for i in range(2):
                        evac(step, i, dst[:, 2 * i:2 * i + 2, :].rearrange("p a b -> p (a b)"))
                elif step[:2] == "sc":
                    h = int(step[2])
                    act.wait_ge(event("neg_max", layer), h + 1)
                    if h:
                        act.wait_ge(event("a_ready", layer), 2 * h)
                    for c in range(2):
                        for tb in range(TB):
                            k = 2 * c + tb
                            a.do(nc.scalar.activation(R["e"][:, tb, c, :], bank(step, c)[:, tb * T:(tb + 1) * T],
                                                      ACT.Exp, scale=DH ** -0.5, bias=S_NEG[:, k:k + 1],
                                                      accum_out=S_SUM[:, k:k + 1]),
                                 *(drain_of(layer, step, c) if tb else (None, None)))
                elif step[:2] == "aT":
                    evac(step, 0, R["aT"][:, :, :].rearrange("p a b -> p (a b)"))
                elif step in ("av0", "av1", "av2", "av3"):
                    h = int(step[2])
                    wait_filled(act, layer, step, 0)
                    if h >= 2:
                        act.wait_ge(event("o_rstd", layer), h - 1)
                    for tb in range(TB):
                        a.settle()
                        a.do(nc.scalar.activation(SQUARES[:, :], bank(step, 0)[:, tb * DV:(tb + 1) * DV], ACT.Square,
                                                  accum_out=STAT[:, 56 + 2 * (h % 2) + tb:57 + 2 * (h % 2) + tb]),
                             *((event("o_ss", layer), h + 1) if tb == 1 else (None, None)))
                elif step in ("yT", "yaT", "mT", "fht"):
                    if step == "fht":
                        break
                    at = 4 if step == "yaT" else 0
                    for i in range(len(BANKS[step])):
                        wait_filled(act, layer, step, i)
                        copy(HTH[:, at + 2 * i:at + 2 * i + 2, :].rearrange("p a b -> p (a b)"), bank(step, i)[:, :],
                             event(f"{step}_hi", layer), i + 1)
            wait_drained(act, layer, "wo1", 1)
            for tb in range(TB):
                a.do(nc.scalar.activation(H_TOK[:, tb, :], X[:, tb, :], ACT.Square,
                                          accum_out=STAT[:, tb:tb + 1]),
                     *((event("norm_ffn_ss", layer), 1) if tb == TB - 1 else (None, None)))
            stage = ("ffn", layer)
            first = FIRST[stage]
            if layer == 0:
                split_to(first + 2, stage)
            for i in range(4):
                wait_filled(act, layer, "fht", i)
                for j in range(2):
                    kd = 2 * i + j
                    kw = {"scale": PAR[:, PAR_GF + kd:PAR_GF + kd + 1]} if layer == 0 else {}
                    copy(HTH[:, kd, :], bank("fht", i)[:, j * T:(j + 1) * T], event("fht_hi", layer), kd + 1, **kw)
            if layer == 1:
                act.wait_ge(sem("moe_loaded"), 48)
                copy(R["wr_hi"][:, :, :], R["wr"][:, :, :], sem("wr_hi_ready"), 1)
                act.wait_ge(sem("h_scaled"), TB)
                copy(R["hg_hi"][:, :, :], H_TOK[:, :, :], sem("hg_hi_ready"), 1)
                act.wait_ge(sem("top_diff"), 1)
                a.do(nc.scalar.activation(R["tv"][:, 3, :], R["tv"][:, 2, :], ACT.Exp), sem("top_exp"), 1)

            uses = uses_before(stage)

            def raw_n(p, b6, b5):
                s = p % RAW_SLOTS
                return 32 * (uses[s] + p // RAW_SLOTS + 1) + (b6 if s < 3 else b5)

            def ffn_split(p, n0, b6, b5, width=SLAB):
                split(n0 + p, raw_n(p, b6, b5), p % RAW_SLOTS, (first + p) % SPLIT_SLOTS, width)

            tbs = TB if layer == 0 else 1

            def silu(q, n, parity, width=CHUNK):
                act.wait_ge(slab_used, n + 1)
                if not isinstance(q, int) or q:
                    act.wait_ge(act_done, q)
                for tb in range(tbs):
                    src = PS[tb if layer == 0 else parity][:, 0:width]
                    ins = nc.scalar.activation(R["silu"][:, tb, 0:width], src, ACT.Silu)
                ins.then_inc(silu_done, 1)

            def turned_hi(q):
                act.wait_ge(turned, q + 1)
                nc.scalar.activation(R["act_hi"][:, :, 0:tbs * P], PS[2][:, 0:2 * tbs * P].rearrange("p (k t) -> p k t", k=2),
                                     ACT.Copy).then_inc(act_hi_ready, 1)

            def gather_hi(b):
                for i in range(2):
                    act.wait_ge(gathered, 4 * b + i + 1)
                    ins = nc.scalar.activation(HTH[:, 4 * i:4 * i + 4, 0:P],
                                               PS[6 + i][:, :].rearrange("p (k t) -> p k t", k=4), ACT.Copy)
                ins.then_inc(g_hi_ready, 1)

            def ffn_block(b, is_moe):
                n0 = act.snap(FFN_SLABS * b + first) if is_moe else first
                b6 = act.snap(32 * 6 * b) if is_moe else 0
                b5 = act.snap(32 * 5 * b) if is_moe else 0
                qb = act.snap((NCH + 1) * b + Q_FIRST[layer]) if is_moe else Q_FIRST[layer]
                if is_moe:
                    act.wait_ge(slab_used, n0)
                    for h in range(2):
                        ins = nc.scalar.activation(R["y_hi"][:, h * 512:(h + 1) * 512], PS[4 + h][:, :], ACT.Copy,
                                                   scale=R["wslot"][:, 0:1])
                    ins.then_inc(y_hi_ready, 1)
                    ffn_split(2, n0, b6, b5)
                ffn_split(3, n0, b6, b5)
                silu(qb, n0 + 1, 0)
                ffn_split(4, n0, b6, b5)

                def chunk(p, q, parity, n0, b6, b5):
                    turned_hi(q - 1)
                    ffn_split(p + 3, n0, b6, b5)
                    silu(q, n0 + p + 1, parity)
                    ffn_split(p + 4, n0, b6, b5)
                    ffn_split(p + 5, n0, b6, b5)

                with act.Fori(0, 4) as i:
                    n0i, b6i, b5i = act.snap(n0 + 6 * i), act.snap(b6 + 32 * i), act.snap(b5 + 32 * i)
                    qi = act.snap(qb + 2 * i)
                    chunk(2, qi + 1, 1, n0i, b6i, b5i)
                    chunk(5, qi + 2, 0, n0i, b6i, b5i)
                if is_moe:
                    act.wait_ge(pselT_done, b + 1)
                    nc.scalar.activation(R["pselT"][:, :, :].rearrange("p a b -> p (a b)"), PS[3][:, 0:TB * P], ACT.Copy)
                    nc.scalar.activation(R["wslot"][:, 0:1], PS[3][:, 2 * P:2 * P + 1], ACT.Copy).then_inc(pselT_ready, 1)
                turned_hi(qb + NCH - 2)
                ffn_split(29, n0, b6, b5, 8 * TAIL)
                silu(qb + NCH - 1, n0 + 27, 1)
                ffn_split(30, n0, b6, b5, 8 * TAIL)
                ffn_split(31, n0, b6, b5)
                turned_hi(qb + NCH - 1)
                ffn_split(32, n0, b6, b5)
                silu(qb + NCH, n0 + 30, 0, TAIL)

                def next_block(p):
                    split(n0 + FFN_SLABS + p,
                          32 * (uses[p] + 1) + (b6 + 32 * 6), p, (first + p) % SPLIT_SLOTS)
                if is_moe:
                    next_block(0)
                turned_hi(qb + NCH)
                if is_moe:
                    gather_hi(b + 1)
                    next_block(1)

            if layer == 0:
                ffn_block(0, False)
                done[0] = FIRST["mix", 1]
            else:
                split(first, 32 * (uses[0] + 1), 0, first % SPLIT_SLOTS)
                split(first + 1, 32 * (uses[1] + 1), 1, (first + 1) % SPLIT_SLOTS)
                gather_hi(0)
                act.wait_ge(sem("blocks_known"), 1)
                nb = act.value_load(R["nbi"][0:1, 0:1], min_val=NE, max_val=NBLK)
                with act.Fori(0, nb) as b:
                    ffn_block(b, True)
                act.wait_ge(slab_used, FFN_SLABS * nb + first)
                for h in range(2):
                    ins = nc.scalar.activation(R["y_hi"][:, h * 512:(h + 1) * 512], PS[4 + h][:, :], ACT.Copy,
                                               scale=R["wslot"][:, 0:1])
                ins.then_inc(y_hi_ready, 1)

    @block.vector
    def _(dve):
        v = Steps(dve, "dve_steps")
        vec = nc.vector
        done = [0]

        def tt(dst, in0, in1, op, signal=None, value=None):
            v.do(vec.tensor_tensor(dst, in0, in1, op), signal, value)

        def ts(dst, in0, s1, s2, op0, op1=None, signal=None, value=None):
            v.do(vec.tensor_scalar(dst, in0, s1, s2, op0, *([op1] if op1 else [])), signal, value)

        def stt(dst, in0, s, in1, op0, op1, signal=None, value=None):
            v.do(vec.scalar_tensor_tensor(out=dst, in0=in0, scalar=s, in1=in1, op0=op0, op1=op1), signal, value)

        def split(n, raw_slot, split_slot, width=SLAB):
            dve.wait_ge(hi_ready, n + 1)
            vec.tensor_tensor(LO[:, split_slot, 0:width], RAW[:, raw_slot, 0:width],
                              HI[:, split_slot, 0:width].bitcast(F32), ALU.subtract).then_inc(lo_ready, 1)

        def split_to(last, stage):
            first = FIRST[stage]
            while done[0] <= min(last, first + LENGTH[stage[0]] - 1):
                n = done[0]
                split(n, (n - first) % RAW_SLOTS, n % SPLIT_SLOTS)
                done[0] += 1

        def flat(ap):
            return ap.rearrange("p a b -> p (a b)")

        for layer in range(DEPTH):
            stage = ("mix", layer)
            first = FIRST[stage]
            dve.wait_ge(event("par_loaded", layer), 9 * 16)
            if layer == 0:
                dve.wait_ge(sem("cst_loaded"), 3 * 16)
            lv = R["lamv"]
            tt(TMP[:, 0:DH], lv[:, 0, :], lv[:, 1, :], ALU.mult)
            tt(TMP[:, DH:2 * DH], lv[:, 2, :], lv[:, 3, :], ALU.mult)
            ts(PAR[:, PAR_SUB:PAR_SUB + DV], PAR[:, PAR_SUB:PAR_SUB + DV], 1.0 - LAMBDA_INIT[layer], None, ALU.mult)
            v.settle()
            v.do(vec.tensor_reduce(LAM[:, 0:2], TMP[:, 0:2 * DH].rearrange("p (a b) -> p a b", a=2), AX_X, ALU.add),
                 event("lam_sums", layer), 1)
            for j in range(2):
                wait_filled(dve, layer, f"f{j + 1}", 0)
                arg, rnd = R["arg"][:, :], R["rnd"][:, :]
                ts(arg, bank(f"f{j + 1}", 0)[0:FH, 0:T], R["bf"][:, 2 * j:2 * j + 1], R["bf"][:, 2 * j + 1:2 * j + 2],
                   ALU.add, ALU.mult, *drain_of(layer, f"f{j + 1}", 0))
                v.settle()
                ts(rnd, arg, float(np.float32(0.5 / np.pi)), ROUND, ALU.mult, ALU.add)
                v.settle()
                ts(rnd, rnd, ROUND, None, ALU.subtract)
                for part in TWO_PI:
                    v.settle()
                    stt(arg, rnd, -part, arg, ALU.mult, ALU.add)
                v.settle()
                ts(rnd, arg, PI_BELOW, -PI_BELOW, ALU.min, ALU.max, event("sin_arg", layer), j + 1)
                if j == 0:
                    dve.wait_ge(event("lam_exp", layer), 1)
                    tt(LAM[:, 4:5], LAM[:, 3:4], LAM[:, 2:3], ALU.subtract)
                    v.settle()
                    ts(LAM[:, 4:5], LAM[:, 4:5], -LAMBDA_INIT[layer], None, ALU.add)
            dve.wait_ge(event("norm_mix_rstd", layer), 1)
            for tb in range(TB):
                ts(H_TOK[:, tb, :], X[:, tb, :], STAT[:, 2 + tb:3 + tb], None, ALU.mult, None,
                   event("h_ready", layer), tb + 1)
            fb, fpm = R["fb"], R["fpm"]
            for o in range(2):
                if o:
                    wait_filled(dve, layer, "ft0", 3)
                for jt in range(2):
                    for i in range(2):
                        wait_filled(dve, layer, f"hf{o}", 2 * jt + i)
                        tt(fb[:, i, :], bank(f"hf{o}", 2 * jt + i)[:, :], R["decay"][:, jt, i, :], ALU.mult,
                           *drain_of(layer, f"hf{o}", 2 * jt + i))
                    v.settle()
                    if jt == 0:
                        tt(fb[0:1, 0, :], fb[0:1, 0, :], R["hyb"][0:1, o * HW:(o + 1) * HW], ALU.add)
                        v.settle()
                    tt(fpm[:, jt, 0, :], fb[:, 0, :], fb[:, 1, :], ALU.add)
                    tt(fpm[:, jt, 1, :], fb[:, 0, :], fb[:, 1, :], ALU.subtract, event("fpm", layer), 2 * o + jt + 1)
                    v.settle()
            split_to(first + 2, stage)
            for i in range(4):
                dve.wait_ge(event("ht_hi", layer), 2 * i + 2)
                for j in range(2):
                    kd = 2 * i + j
                    stt(HTL[:, kd, :], bank("ht", i)[:, j * T:(j + 1) * T], PAR[:, PAR_GM + kd:PAR_GM + kd + 1],
                        HTH[:, kd, :].bitcast(F32), ALU.mult, ALU.subtract,
                        *(drain_of(layer, "ht", i) if j else (None, None)))
            wait_filled(dve, layer, "ht", 3)
            v.do(vec.memset(UPAD[:, :, :, 0:1], 0.0))
            v.do(vec.memset(UPAD[:, :, :, T + 1:T + 2], 0.0), event("pads", layer), 1)

            def norm_rope(step, c, rstd_at):
                x = QKV[:, c, :, :].rearrange("p t (s d) -> p (t s) d", d=DH)
                tmp = TMP[:, :].rearrange("p (s d) -> p s d", d=DH)
                for tb in range(TB):
                    wait_drained(dve, layer, step, tb)
                v.settle()
                tt(tmp, x, x, ALU.mult)
                v.settle()
                v.do(vec.tensor_reduce(STAT[:, 8:24], tmp, AX_X, ALU.add), event(f"{step}_ss", layer), 1)
                dve.wait_ge(event(f"{step}_rstd", layer), 1)
                tt(x, x, STAT[:, rstd_at:rstd_at + 16].unsqueeze(2).broadcast_to([P, 16, DH]), ALU.mult)
                v.settle()
                gain = PAR[:, (PAR_QN if step == "q" else PAR_KN):][:, 0:DH]
                tt(x, x, gain.unsqueeze(1).broadcast_to([P, 16, DH]), ALU.mult)
                v.settle()
                for tb in range(TB):
                    y = QKV[:, c, tb, :].rearrange("p (s d) -> p s d", d=DH)
                    x1, x2 = y[:, :, 0:32], y[:, :, 32:64]
                    cos, sin = (ROPE[:, k, tb, :].unsqueeze(1).broadcast_to([P, 8, 32]) for k in range(2))
                    t = TMP[:, tb * 512:(tb + 1) * 512].rearrange("p (k s d) -> p k s d", k=2, d=32)
                    tt(t[:, 0], x2, sin, ALU.mult)
                    tt(t[:, 1], x1, sin, ALU.mult)
                    v.settle()
                    tt(x1, x1, cos, ALU.mult)
                    tt(x2, x2, cos, ALU.mult)
                    v.settle()
                    tt(x1, x1, t[:, 0], ALU.subtract)
                    tt(x2, x2, t[:, 1], ALU.add, event(f"{step}_roped", layer), tb + 1)

            for step, _ in PLAN[PLAN.index(("v", [0, 1, 2, 3])):]:
                if step in LAST_SLAB:
                    split_to(first + LAST_SLAB[step] + 2, stage)
                if step in ("v", "x1", "x2"):
                    c = ("v", "x1", "x2").index(step)
                    if c == 2:
                        wait_filled(dve, layer, "vT", 1)
                    for tap in range(3):
                        if tap:
                            v.settle()
                        for i in range(4):
                            w = PAR[:, PAR_CONV + 3 * (COLUMN[step] // P + i) + tap:][:, 0:1]
                            src, dst = UPAD[:, c % 2, i, tap:tap + T], CONV[:, c % 2, i, :]
                            if tap == 0:
                                wait_drained(dve, layer, step, i)
                                ts(dst, src, w, None, ALU.mult)
                            else:
                                stt(dst, src, w, dst, ALU.mult, ALU.add,
                                    *((event("conv_done", layer), 4 * c + i + 1) if tap == 2 else (None, None)))
                elif step in ("q", "k"):
                    norm_rope(step, ("q", "k").index(step), 24 if step == "q" else 40)
                elif step in ("cf0", "cf1"):
                    o = int(step[2])
                    for kt in range(2):
                        re, im = bank(step, 2 * kt)[:, :], bank(step, 2 * kt + 1)[:, :]
                        wait_filled(dve, layer, step, 2 * kt + 1)
                        if o == 0 and kt == 0:
                            wait_drained(dve, layer, "ft1", 3)
                            wait_filled(dve, layer, "x2T", 1)
                        v.settle()
                        tt(YS[:, kt, 0, :], FSP[:, kt, o, 0, :], re, ALU.mult)
                        tt(TMP[:, 0:512], FSP[:, kt, o, 1, :], im, ALU.mult)
                        tt(YS[:, kt, 1, :], FSP[:, kt, o, 0, :], im, ALU.mult, *drain_of(layer, step, 2 * kt + 1))
                        tt(TMP[:, 512:1024], FSP[:, kt, o, 1, :], re, ALU.mult, *drain_of(layer, step, 2 * kt))
                        v.settle()
                        tt(YS[:, kt, 0, :], YS[:, kt, 0, :], TMP[:, 0:512], ALU.subtract)
                        tt(YS[:, kt, 1, :], YS[:, kt, 1, :], TMP[:, 512:1024], ALU.add,
                           event("ys_ready", layer), 2 * o + kt + 1)
                elif step in ("ci0", "ci1"):
                    o = int(step[2])
                    for tb in range(TB):
                        wait_filled(dve, layer, step, tb)
                        wait_drained(dve, layer, ("x1T", "x2T")[o], tb)
                        tt(XV[:, o, tb, :], XV[:, o, tb, :], bank(step, tb)[:, :], ALU.mult,
                           *drain_of(layer, step, tb))
                elif step[:2] == "sc":
                    h = int(step[2])
                    for c in range(2):
                        wait_filled(dve, layer, step, c)
                        v.do(vec.tensor_reduce(S_MAX[:, 2 * c:2 * c + 2],
                                               bank(step, c)[:, :].rearrange("p (t k) -> p t k", t=TB), AX_X, ALU.max))
                    v.settle()
                    ts(S_NEG, S_MAX, -DH ** -0.5, None, ALU.mult, None, event("neg_max", layer), h + 1)
                    for c in range(2):
                        wait_drained(dve, layer, step, c)
                    v.do(vec.reciprocal(S_FAC, S_SUM))
                    v.settle()
                    ts(S_FAC[:, 2:4], S_FAC[:, 2:4], LAM[:, 4:5], None, ALU.mult)
                    if h:
                        wait_filled(dve, layer, f"aT{h - 1}", 0)
                    v.settle()
                    for tb in range(TB):
                        ts(R["a"][:, tb, :], R["e"][:, tb, 1, :], S_FAC[:, 2 + tb:3 + tb], None, ALU.mult)
                    v.settle()
                    for tb in range(TB):
                        stt(R["a"][:, tb, :], R["e"][:, tb, 0, :], S_FAC[:, tb:tb + 1], R["a"][:, tb, :],
                            ALU.mult, ALU.add, event("a_ready", layer), 2 * h + tb + 1)
                elif step[:2] == "av" and step != "av":
                    h = int(step[2])
                    wait_filled(dve, layer, step, 0)
                    dve.wait_ge(event("o_rstd", layer), h + 1)
                    for tb in range(TB):
                        stt(QKV[:, 2, tb, h * DV:(h + 1) * DV], bank(step, 0)[:, tb * DV:(tb + 1) * DV],
                            STAT[:, 4 + 2 * (h % 2) + tb:5 + 2 * (h % 2) + tb], PAR[:, PAR_SUB:PAR_SUB + DV],
                            ALU.mult, ALU.mult, *(drain_of(layer, step, 0) if tb else (None, None)))
                elif step in ("yT", "yaT", "mT"):
                    at = 4 if step == "yaT" else 0
                    for i in range(len(BANKS[step])):
                        dve.wait_ge(event(f"{step}_hi", layer), i + 1)
                        tt(flat(HTL[:, at + 2 * i:at + 2 * i + 2, :]), bank(step, i)[:, :],
                           flat(HTH[:, at + 2 * i:at + 2 * i + 2, :]).bitcast(F32), ALU.subtract,
                           *drain_of(layer, step, i))
                elif step[:2] == "ph":
                    half = slice(int(step[2]) * 512, int(step[2]) * 512 + 512)
                    for tb in range(TB):
                        wait_filled(dve, layer, step, tb)
                        wait_drained(dve, layer, f"g{step[2]}", tb)
                        tt(GATES[:, tb, 0, half], GATES[:, tb, 0, half], bank(step, tb)[:, :], ALU.mult,
                           *drain_of(layer, step, tb))
                elif step[:2] == "pa":
                    half = slice(int(step[2]) * 512, int(step[2]) * 512 + 512)
                    for tb in range(TB):
                        wait_filled(dve, layer, step, tb)
                        wait_drained(dve, layer, f"g{2 + int(step[2])}", tb)
                        v.settle()
                        tt(TMP[:, 0:512], GATES[:, tb, 1, half], bank(step, tb)[:, :], ALU.mult,
                           *drain_of(layer, step, tb))
                        v.settle()
                        tt(GATES[:, tb, 0, half], GATES[:, tb, 0, half], TMP[:, 0:512], ALU.add,
                           event("merged", layer), 2 * int(step[2]) + tb + 1)
                elif step[:2] == "wo":
                    half = slice(int(step[2]) * 512, int(step[2]) * 512 + 512)
                    for tb in range(TB):
                        wait_filled(dve, layer, step, tb)
                        tt(X[:, tb, half], X[:, tb, half], bank(step, tb)[:, :], ALU.add,
                           *drain_of(layer, step, tb))

            stage = ("ffn", layer)
            first = FIRST[stage]
            dve.wait_ge(event("norm_ffn_rstd", layer), 1)
            for tb in range(TB):
                ts(H_TOK[:, tb, :], X[:, tb, :], STAT[:, 2 + tb:3 + tb], None, ALU.mult, None,
                   *((event("hf_ready", 0), tb + 1) if layer == 0 else (None, None)))
            if layer == 1:
                dve.wait_ge(sem("moe_loaded"), 48)
                v.settle()
                for tb in range(TB):
                    tt(H_TOK[:, tb, :], H_TOK[:, tb, :], R["g_row"][:, :], ALU.mult, sem("h_scaled"), tb + 1)
                dve.wait_ge(sem("wr_hi_ready"), 1)
                tt(R["wr_lo"][:, :, :], R["wr"][:, :, :], R["wr_hi"][:, :, :].bitcast(F32), ALU.subtract)
            else:
                split_to(first + 2, stage)
            for i in range(4):
                dve.wait_ge(event("fht_hi", layer), 2 * i + 2)
                for j in range(2):
                    kd = 2 * i + j
                    src, hi = bank("fht", i)[:, j * T:(j + 1) * T], HTH[:, kd, :].bitcast(F32)
                    sig = drain_of(layer, "fht", i) if j else (None, None)
                    if layer == 0:
                        stt(HTL[:, kd, :], src, PAR[:, PAR_GF + kd:PAR_GF + kd + 1], hi, ALU.mult, ALU.subtract, *sig)
                    else:
                        tt(HTL[:, kd, :], src, hi, ALU.subtract, *sig)
            if layer == 1:
                router(dve, v, tt, ts, stt)

            tbs = TB if layer == 0 else 1

            def mult(q, parity, width=CHUNK):
                dve.wait_ge(silu_done, q + 1)
                for tb in range(tbs):
                    ins = vec.tensor_tensor(R["act"][:, tb, 0:width], R["silu"][:, tb, 0:width],
                                            PS[tb if layer == 0 else parity][:, width:2 * width], ALU.mult)
                ins.then_inc(act_done, 1)

            def turned_lo(q):
                dve.wait_ge(act_hi_ready, q + 1)
                vec.tensor_tensor(R["act_lo"][:, :, 0:tbs * P],
                                  PS[2][:, 0:2 * tbs * P].rearrange("p (k t) -> p k t", k=2),
                                  R["act_hi"][:, :, 0:tbs * P].bitcast(F32), ALU.subtract).then_inc(act_lo_ready, 1)

            def gather_lo(b):
                for i in range(2):
                    dve.wait_ge(gathered, 4 * b + i + 3)
                    ins = vec.tensor_copy(HTL[:, 4 * i:4 * i + 4, 0:P],
                                          PS[(3, 1)[i]][:, :].rearrange("p (k t) -> p k t", k=4))
                ins.then_inc(g_lo_ready, 1)

            def select(b):
                for tb in range(TB):
                    vec.tensor_scalar(R["psel"][:, tb, :], R["moec"][:, 0:P],
                                      R["pcol"][:, tb, bass.ds(b, 1)] if not isinstance(b, int)
                                      else R["pcol"][:, tb, b:b + 1], None, ALU.is_equal)
                src = R["wcol"][:, :, bass.ds(b, 1)] if not isinstance(b, int) else R["wcol"][:, :, b:b + 1]
                vec.tensor_copy(R["wcur"][:, :], src.rearrange("p a b -> p (a b)")).then_inc(psel_ready, 1)

            def y_lo():
                for h in range(2):
                    ins = vec.scalar_tensor_tensor(out=R["y_lo"][:, h * 512:(h + 1) * 512], in0=PS[4 + h][:, :],
                                                   scalar=R["wslot"][:, 0:1],
                                                   in1=R["y_hi"][:, h * 512:(h + 1) * 512].bitcast(F32),
                                                   op0=ALU.mult, op1=ALU.subtract)
                ins.then_inc(y_ready, 1)

            def add_scattered(b):
                for i in range(4):
                    dve.wait_ge(scattered, 4 * b + i + 1)
                    tb, half = i // 2, slice((i % 2) * 512, (i % 2) * 512 + 512)
                    vec.tensor_tensor(X[:, tb, half], X[:, tb, half], PS[(6, 7, 3, 2)[i]][:, :], ALU.add)\
                       .then_inc(scatter_added, 1)

            def ffn_split(p, n0, width=SLAB):
                split(n0 + p, p % FFN_SLABS % RAW_SLOTS, (first + p) % SPLIT_SLOTS, width)

            def ffn_block(b, is_moe):
                n0 = dve.snap(FFN_SLABS * b + first) if is_moe else first
                qb = dve.snap((NCH + 1) * b + Q_FIRST[layer]) if is_moe else Q_FIRST[layer]
                if is_moe:
                    dve.wait_ge(y_hi_ready, b + 1)
                    y_lo()
                    ffn_split(2, n0)
                ffn_split(3, n0)
                mult(qb, 0)
                ffn_split(4, n0)
                if is_moe:
                    add_scattered(b)

                def chunk(p, q, parity, n0):
                    turned_lo(q - 1)
                    ffn_split(p + 3, n0)
                    mult(q, parity)
                    ffn_split(p + 4, n0)
                    ffn_split(p + 5, n0)

                with dve.Fori(0, 4) as i:
                    n0i, qi = dve.snap(n0 + 6 * i), dve.snap(qb + 2 * i)
                    chunk(2, qi + 1, 1, n0i)
                    chunk(5, qi + 2, 0, n0i)
                if is_moe:
                    dve.wait_ge(pselT_done, b + 1)
                    select(b + 1)
                turned_lo(qb + NCH - 2)
                ffn_split(29, n0, 8 * TAIL)
                mult(qb + NCH - 1, 1)
                ffn_split(30, n0, 8 * TAIL)
                ffn_split(31, n0)
                turned_lo(qb + NCH - 1)
                ffn_split(32, n0)
                mult(qb + NCH, 0, TAIL)
                if is_moe:
                    ffn_split(FFN_SLABS, n0)
                turned_lo(qb + NCH)
                if is_moe:
                    gather_lo(b + 1)
                    ffn_split(FFN_SLABS + 1, n0)

            if layer == 0:
                ffn_block(0, False)
                dve.wait_ge(slab_used, first + FFN_SLABS)
                for i in range(4):
                    tb, half = i // 2, slice((i % 2) * 512, (i % 2) * 512 + 512)
                    tt(X[:, tb, half], X[:, tb, half], PS[4 + i][:, :], ALU.add,
                       *((event("ffn_added", 0), 1) if i == 3 else (None, None)))
                done[0] = FIRST["mix", 1]
            else:
                select(0)
                ffn_split(0, first)
                ffn_split(1, first)
                gather_lo(0)
                nb = dve.value_load(R["nbi"][0:1, 0:1], min_val=NE, max_val=NBLK)
                with dve.Fori(0, nb) as b:
                    ffn_block(b, True)
                dve.wait_ge(y_hi_ready, nb + 1)
                y_lo()
                add_scattered(nb)

    @block.tensor
    def _(pe):
        mm = nc.tensor.matmul

        def three(out_, l_hi, l_lo, r_hi, r_lo, start, stop):
            mm(out_, l_hi, r_hi, start=start, stop=False)
            mm(out_, l_hi, r_lo, start=False, stop=False)
            return mm(out_, l_lo, r_hi, start=False, stop=stop)

        def bank_free(layer, step, i):
            b = BANKS[step][i]
            if DRAINS[layer, step, b] > 1:
                pe.wait_ge(drained[b], DRAINS[layer, step, b] - 1)

        def fill(layer, step, i, ins):
            ins.then_inc(filled[BANKS[step][i]], 1)

        def turn(dst, src):
            return nc.tensor.transpose(dst, src, IDENT[:, :])

        def w_parts(n_mod, lo, hi):
            return HI[:, n_mod, lo:hi], LO[:, n_mod, lo:hi]

        def project(layer, step, n, k0, nk, start, stop, turned_w):
            pe.wait_ge(lo_ready, n + 1)
            s = n % SPLIT_SLOTS
            for k in range(nk):
                kd = k0 + k
                st, sp_ = start and k == 0, stop and k == nk - 1
                if turned_w:
                    for m in range(4):
                        w_hi, w_lo = w_parts(s, k * 512 + m * P, k * 512 + (m + 1) * P)
                        ins = three(bank(step, m)[:, 0:T], w_hi, w_lo, HTH[:, kd, :], HTL[:, kd, :], st, sp_)
                else:
                    w_hi, w_lo = w_parts(s, k * 512, (k + 1) * 512)
                    for tb in range(TB):
                        tok = slice(tb * P, (tb + 1) * P)
                        ins = three(bank(step, tb)[:, :], HTH[:, kd, tok], HTL[:, kd, tok], w_hi, w_lo, st, sp_)
            ins.then_inc(slab_used, 1)

        for layer in range(DEPTH):
            first = FIRST["mix", layer]
            if layer == 0:
                pe.wait_ge(sem("cst_loaded"), 3 * 16)
            else:
                pe.wait_ge(event("ffn_added", 0), 1)
            pe.wait_ge(event("par_loaded", layer), 9 * 16)
            for step, banks in PLAN:
                if step in LAST_SLAB:
                    last = first + LAST_SLAB[step]
                    for i in range(len(banks)):
                        bank_free(layer, step, i)
                    if step in ("ph0", "pa0"):
                        for i in range(2):
                            wait_drained(pe, layer, "yT" if step == "ph0" else "yaT", i)
                    if step in ("v", "wo0"):
                        for i in range(4):
                            wait_drained(pe, layer, "ht" if step == "v" else "mT", i)
                    if step[:2] in ("ph", "pa"):
                        project(layer, step, last, 4 * (step[:2] == "pa"), 4, True, True, False)
                    else:
                        for part in range(2):
                            project(layer, step, last - 1 + part, 4 * part, 4, part == 0, part == 1,
                                    step in ("v", "x1", "x2"))
                    continue
                if step == "f2":
                    pe.wait_ge(event("sin_done", layer), 1)
                elif step[:2] == "hf":
                    pe.wait_ge(event("sin_done", layer), 2)
                elif step[:2] == "ft":
                    pe.wait_ge(event("fpm", layer), 2 * int(step[2]) + 2)
                elif step == "ht":
                    pe.wait_ge(event("h_ready", layer), TB)
                elif step in ("vT", "x1T", "x2T"):
                    pe.wait_ge(event("conv_done", layer), {"vT": 4, "x1T": 8, "x2T": 12}[step])
                elif step == "cf0":
                    for tb in range(TB):
                        wait_drained(pe, layer, "vT", tb)
                elif step == "cf1":
                    for tb in range(TB):
                        wait_drained(pe, layer, "ci0", tb)
                elif step[:2] == "ci":
                    pe.wait_ge(event("ys_ready", layer), 2 * int(step[2]) + 2)
                elif step in ("qT", "kT"):
                    pe.wait_ge(event(f"{step[0]}_roped", layer), TB)
                elif step == "sc0":
                    for i in range(2):
                        wait_drained(pe, layer, "qT", i)
                        wait_drained(pe, layer, "kT", i)
                elif step[:2] == "aT":
                    pe.wait_ge(event("a_ready", layer), 2 * int(step[2]) + 2)
                elif step[:2] == "av":
                    wait_drained(pe, layer, f"aT{step[2]}", 0)
                    for tb in range(TB):
                        wait_drained(pe, layer, "av", tb)
                elif step == "yT":
                    for tb in range(TB):
                        wait_drained(pe, layer, "ci1", tb)
                elif step == "yaT":
                    wait_drained(pe, layer, "av3", 0)
                elif step == "mT":
                    pe.wait_ge(event("merged", layer), 4)
                elif step == "fht":
                    pe.wait_ge(sem("h_scaled") if layer else event("hf_ready", 0), TB)
                for i in range(len(banks)):
                    bank_free(layer, step, i)
                    dst = bank(step, i)
                    if step == "f1":
                        ins = mm(dst[0:FH, 0:T], R["wf1"][:, :], R["zT"][:, :], start=True, stop=True)
                    elif step == "f2":
                        ins = mm(dst[0:FH, 0:T], R["wf2"][:, :], R["hdn"][:, 0, :], start=True, stop=True)
                    elif step[:2] == "hf":
                        jt, part = i // 2, 2 * int(step[2]) + i % 2
                        ins = mm(dst[:, :], R["hdn"][:, 1, jt * P:(jt + 1) * P],
                                 R["wf3"][:, part * HW:(part + 1) * HW], start=True, stop=True)
                    elif step[:2] in ("ft", "cf"):
                        kt, ri = i // 2, i % 2
                        for jt in range(2):
                            src = R["fpm"][:, jt, ri, :] if step[:2] == "ft" else XV[:, 0 if step == "cf1" else 2, jt, :]
                            ins = mm(dst[:, :], DFT[:, ri, jt, kt * P:(kt + 1) * P], src, start=jt == 0, stop=jt == 1)
                    elif step[:2] == "ci":
                        for k in range(4):
                            kt, ri = k // 2, k % 2
                            ins = mm(dst[:, :], DFT[:, 2 + ri, kt, i * P:(i + 1) * P], YS[:, kt, ri, :],
                                     start=k == 0, stop=k == 3)
                    elif step in ("ht", "fht", "mT"):
                        for j in range(4):
                            kd, tb = 2 * i + j // 2, j % 2
                            col = slice(kd * P, (kd + 1) * P)
                            src = GATES[:, tb, 0, col] if step == "mT" else H_TOK[:, tb, col]
                            ins = turn(dst[:, j * P:(j + 1) * P], src)
                    elif step in ("vT", "x1T", "x2T"):
                        c = ("vT", "x1T", "x2T").index(step)
                        for j in range(4):
                            ins = turn(dst[:, j * P:(j + 1) * P], CONV[:, c % 2, j, i * P:(i + 1) * P])
                    elif step in ("qT", "kT", "yT", "yaT"):
                        for j in range(4):
                            t, tb = 2 * i + j // 2, j % 2
                            col = slice(t * P, (t + 1) * P)
                            src = XV[:, 1, tb, col] if step == "yT" else \
                                QKV[:, {"qT": 0, "kT": 1, "yaT": 2}[step], tb, col]
                            ins = turn(dst[:, j * P:(j + 1) * P], src)
                    elif step[:2] == "sc":
                        h = int(step[2])
                        d = slice(i * DH, (i + 1) * DH)
                        for tb in range(TB):
                            ins = mm(dst[:, tb * T:(tb + 1) * T], QT[d, h, tb * P:(tb + 1) * P], KT[d, h, :],
                                     start=True, stop=True)
                    elif step[:2] == "aT":
                        for j in range(4):
                            kt, tb = j // 2, j % 2
                            ins = turn(dst[:, j * P:(j + 1) * P], R["a"][:, tb, kt * P:(kt + 1) * P])
                    elif step[:2] == "av":
                        h = int(step[2])
                        for j in range(4):
                            tb, kt = j // 2, j % 2
                            ins = mm(dst[:, tb * DV:(tb + 1) * DV], R["aT"][:, kt, tb * P:(tb + 1) * P],
                                     QKV[:, 2, kt, h * DV:(h + 1) * DV], start=kt == 0, stop=kt == 1)
                    fill(layer, step, i, ins)

            first = FIRST["ffn", layer]
            for i in range(4):
                wait_drained(pe, layer, "fht", i)
            if layer == 1:
                bank_free(1, "rt", 0)
                for tb in range(TB):
                    tok = slice(tb * P, (tb + 1) * P)
                    for kd in range(KD):
                        ins = three(bank("rt", 0)[:, tb * NE:(tb + 1) * NE], HTH[:, kd, tok], HTL[:, kd, tok],
                                    R["wr_hi"][:, kd, :], R["wr_lo"][:, kd, :], kd == 0, kd == KD - 1)
                fill(1, "rt", 0, ins)
                pe.wait_ge(sem("sel_ready"), 1)
                bank_free(1, "pos", 0)
                tri, ones = R["moec"][:, P:2 * P], R["moec"][:, 2 * P:3 * P]
                for i, terms in enumerate((((tri, 0),), ((ones, 0), (tri, 1)), ((ones, 0), (ones, 1)))):
                    for k, (m, tb) in enumerate(terms):
                        ins = mm(bank("pos", 0)[:, i * NE:(i + 1) * NE], m, R["sel"][:, tb, :],
                                 start=k == 0, stop=k == len(terms) - 1)
                fill(1, "pos", 0, ins)

            tbs = TB if layer == 0 else 1

            def gate_up(n, s, part, width, q, parity):
                pe.wait_ge(lo_ready, n + 1)
                if part == 0 and not (isinstance(q, int) and q == 0):
                    pe.wait_ge(act_done, q)
                for k in range(4):
                    kd = 4 * part + k
                    w_hi, w_lo = w_parts(s, k * 2 * width, (k + 1) * 2 * width)
                    for tb in range(tbs):
                        tok = slice(tb * P, (tb + 1) * P)
                        ins = three(PS[tb if layer == 0 else parity][:, 0:2 * width], HTH[:, kd, tok],
                                    HTL[:, kd, tok], w_hi, w_lo, kd == 0, kd == KD - 1)
                ins.then_inc(slab_used, 1)

            def turn_act(q, width=CHUNK):
                pe.wait_ge(act_done, q + 1)
                for k in range(2):
                    h = min(P, width - k * P)
                    for tb in range(tbs):
                        at = (k * tbs + tb) * P
                        ins = turn(PS[2][0:h, at:at + P], R["act"][:, tb, k * P:k * P + h])
                ins.then_inc(turned, 1)

            def down(n, s, q, start, stop=False, width=CHUNK):
                pe.wait_ge(lo_ready, n + 1)
                pe.wait_ge(act_lo_ready, q + 1)
                for k in range(2):
                    h = min(P, width - k * P)
                    for tb in range(tbs):
                        tok = slice(tb * P, (tb + 1) * P)
                        for half in range(2):
                            at = k * D + half * 512
                            ins = three(PS[4 + 2 * tb + half][:, :], R["act_hi"][0:h, k, tok], R["act_lo"][0:h, k, tok],
                                        HI[0:h, s, at:at + 512], LO[0:h, s, at:at + 512],
                                        start and k == 0, stop and k == 1)
                ins.then_inc(slab_used, 1)

            def gather(b):
                pe.wait_ge(psel_ready, b + 1)
                for i, (src, bk) in enumerate(((R["hg_hi"], 6), (R["hg_hi"], 7), (R["hg_lo"], 3), (R["hg_lo"], 1))):
                    for k in range(4):
                        kd = 4 * (i % 2) + k
                        for tb in range(TB):
                            ins = mm(PS[bk][:, k * P:(k + 1) * P], src[:, tb, kd * P:(kd + 1) * P],
                                     R["psel"][:, tb, :], start=tb == 0, stop=tb == 1)
                    ins.then_inc(gathered, 1)

            def scatter(b):
                pe.wait_ge(y_ready, b + 1)
                for i, bk in enumerate((6, 7, 3, 2)):
                    tb, cols = i // 2, slice((i % 2) * 512, (i % 2) * 512 + 512)
                    mm(PS[bk][:, :], R["pselT"][:, tb, :], R["y_hi"][:, cols], start=True, stop=False)
                    mm(PS[bk][:, :], R["pselT"][:, tb, :], R["y_lo"][:, cols], start=False, stop=True)\
                        .then_inc(scattered, 1)

            def ffn_block(b, is_moe):
                n0 = pe.snap(FFN_SLABS * b + first) if is_moe else first
                qb = pe.snap((NCH + 1) * b + Q_FIRST[layer]) if is_moe else Q_FIRST[layer]

                def slot(p):
                    return (first + p) % SPLIT_SLOTS
                if is_moe:
                    pe.wait_ge(g_hi_ready, b + 1)
                    pe.wait_ge(g_lo_ready, b + 1)
                for part in range(2):
                    gate_up(n0 + part, slot(part), part, CHUNK, qb, 0)
                if is_moe:
                    scatter(b)
                    pe.wait_ge(scatter_added, 4 * b + 4)

                def pair(n0, qb, start):
                    for j in range(2):
                        p, q = 2 + 3 * j, qb + 1 + j
                        gate_up(n0 + p, slot(p), 0, CHUNK, q, 1 - j)
                        turn_act(q - 1)
                        gate_up(n0 + p + 1, slot(p + 1), 1, CHUNK, q, 1 - j)
                        down(n0 + p + 2, slot(p + 2), q - 1, start and j == 0)

                pair(n0, qb, True)
                with pe.Fori(1, 4) as i:
                    pair(pe.snap(n0 + 6 * i), pe.snap(qb + 2 * i), False)
                if is_moe:
                    for tb in range(TB):
                        turn(PS[3][:, tb * P:(tb + 1) * P], R["psel"][:, tb, :].bitcast(F32))
                    for tb in range(TB):
                        ins = mm(PS[3][:, 2 * P:2 * P + 1], R["psel"][:, tb, :].bitcast(F32), R["wcur"][:, tb:tb + 1],
                                 start=tb == 0, stop=tb == 1)
                    ins.then_inc(pselT_done, 1)
                q = qb + NCH - 1
                gate_up(n0 + 26, slot(26), 0, CHUNK, q, 1)
                turn_act(q - 1)
                gate_up(n0 + 27, slot(27), 1, CHUNK, q, 1)
                down(n0 + 28, slot(28), q - 1, False)
                gate_up(n0 + 29, slot(29), 0, TAIL, q + 1, 0)
                turn_act(q)
                gate_up(n0 + 30, slot(30), 1, TAIL, q + 1, 0)
                down(n0 + 31, slot(31), q, False)
                turn_act(q + 1, TAIL)
                if is_moe:
                    pe.wait_ge(pselT_ready, b + 1)
                    gather(b + 1)
                down(n0 + 32, slot(32), q + 1, False, True, TAIL)

            if layer == 0:
                ffn_block(0, False)
            else:
                pe.wait_ge(sem("hg_lo_ready"), 1)
                pe.wait_ge(psel_ready, 1)
                for half in range(2):
                    mm(PS[4 + half][:, :], R["pselT"][:, 0, :], HTH[:, 2 * half:2 * half + 2, :].rearrange("p a b -> p (a b)"),
                       start=True, stop=True)
                gather(0)
                pe.wait_ge(sem("blocks_known"), 1)
                nb = pe.value_load(R["nbi"][0:1, 0:1], min_val=NE, max_val=NBLK)
                with pe.Fori(0, nb) as b:
                    ffn_block(b, True)
                scatter(nb)

    ctx.close()


def constants():
    f = np.float32
    k = np.arange(T)
    angle = 2 * np.pi * np.outer(np.arange(T), k + 0.5) / (2 * T)
    tables = np.stack([np.cos(angle), np.sin(angle), np.cos(angle).T, np.sin(angle).T])
    dft = tables.reshape(4, 2, P, T).transpose(2, 0, 1, 3).reshape(P, 4 * 2 * T).astype(f)
    inv = (f(1.0) / (f(10000.0) ** (np.arange(0, DH, 2, dtype=f) / f(DH)))).astype(f)
    ang = np.arange(T, dtype=f)[:, None] * inv[None, :]
    rope = np.stack([np.cos(ang), np.sin(ang)]).astype(f).reshape(2, TB, P, DH // 2)
    cst = np.concatenate([np.eye(P, dtype=f), rope.transpose(2, 0, 1, 3).reshape(P, P)], axis=1)
    t = np.linspace(0.0, 1.0, T, dtype=f)[:, None]
    w = (f(2.0 * np.pi) * np.arange(T, dtype=f)[:, None] / f(T)).astype(f)
    bands = (FE - 1) // 2
    fr = np.linspace(1e-4, bands - 1, bands, dtype=f)[None, :]
    z = np.concatenate([t, np.cos(fr * w), -np.sin(fr * w)], axis=-1).astype(f)
    deltas = np.linspace(np.log(1e-2) / 1.5, np.log(1e-2) / 0.3, HW).astype(f)
    decay = np.exp(-t * np.abs(deltas)[None, :]).astype(f)
    both = np.stack([decay, decay])
    both[1, 0] = 0
    both = both.reshape(2, 2, P, HW).transpose(2, 1, 0, 3).reshape(P, 4 * HW)
    moec = np.zeros((P, 3 * P + 64 + 8 + 4), f)
    moec[:, 0:P] = np.arange(P)
    moec[:, P:2 * P] = np.triu(np.ones((P, P)), 1)
    moec[:, 2 * P:3 * P] = 1
    moec[:, 3 * P:3 * P + 64] = np.tril(np.ones((NE, NE)), -1).reshape(1, 64)
    moec[:, 3 * P + 64:3 * P + 72] = np.arange(NE)
    return {"cst": cst, "dft": dft, "decay": both, "zt": z.T, "moec": moec}


STREAMED = ["w_in", "w_hy_o", "w_at_o", "w_out", "w_dense_gate", "w_dense_up", "w_dense_down",
            "w_moe_gate", "w_moe_up", "w_moe_down"]


def kernel(**inputs):
    import concourse.bacc as bacc
    from concourse.bass_utils import run_bass_kernel_spmd

    a = {k: np.asarray(v) for k, v in inputs.items()}
    par = np.zeros((DEPTH, P, PAR_N), np.float32)
    for layer in range(DEPTH):
        par[layer, :, PAR_CONV:PAR_GM] = a["conv_w"][layer].reshape(3, 12, P).transpose(2, 1, 0).reshape(P, 36)
        par[layer, :, PAR_GM:PAR_GF] = a["norm_mix"][layer].reshape(KD, P).T
        par[layer, :, PAR_GF:PAR_QN] = a["norm_ffn"][layer].reshape(KD, P).T
        par[layer, :, PAR_QN:PAR_KN] = a["q_norm"][layer]
        par[layer, :, PAR_KN:PAR_SUB] = a["k_norm"][layer]
        par[layer, :, PAR_SUB:PAR_N] = a["subln_g"][layer]
    ins = dict(
        x=a["x"][0], par=par,
        lamv=np.concatenate([a["lam_q1"], a["lam_k1"], a["lam_q2"], a["lam_k2"]], axis=1),
        wf1=a["w_f1"], wf2=a["w_f2"],
        bf=np.stack([a["b_f1"], a["freq1"], a["b_f2"], a["freq2"]], axis=2),
        wf3=a["w_f3"], hyb=a["hy_bias"].reshape(DEPTH, 2 * HW), nffn=a["norm_ffn"][1:2], wr=a["w_router"][0],
        **constants())
    ins.update({k: a[k] for k in STREAMED if "moe" not in k})
    ins.update({k: a[k][0] for k in STREAMED if "moe" in k})

    nc = bacc.Bacc("TRN2", target_bir_lowering=False, num_devices=1)
    arrays, aps = {}, {}
    for name, value in ins.items():
        value = np.ascontiguousarray(value)
        arrays[f"in_{name}"] = value
        aps[name] = nc.dram_tensor(f"in_{name}", value.shape, mybir.dt.from_np(value.dtype), kind="ExternalInput").ap()
    out = nc.dram_tensor("out_x", (T, D), F32, kind="ExternalOutput").ap()
    trunk(nc, aps["x"], {k: aps[k] for k in STREAMED}, aps["par"], aps["lamv"], aps["wf1"], aps["wf2"], aps["bf"],
          aps["wf3"], aps["hyb"], aps["nffn"], aps["wr"], aps["cst"], aps["dft"], aps["decay"], aps["zt"],
          aps["moec"], out)
    result = run_bass_kernel_spmd(nc, [arrays], core_ids=[0])
    return result.results[0]["out_x"].reshape(1, T, D)
```

```python
from contextlib import ExitStack

import numpy as np

import concourse.bass as bass
from concourse import mybir

ALU = mybir.AluOpType
ACT = mybir.ActivationFunctionType
AX_X = mybir.AxisListType.X
F32 = mybir.dt.float32
F32R = mybir.dt.float32r
I32 = mybir.dt.int32

P = 128
D = 1024
T = 256
TB = T // P
DEPTH = 2
HW = D // 2
KD = D // P
NH, DH, DV = 4, 64, 128
FE, FH = 33, 64
FF = 2752
NE, TOPK = 8, 2
EPS = 1e-6

SLAB = 2048
RAW_SLOTS, SPLIT_SLOTS = 6, 3
CHUNK = 256
NCH = FF // CHUNK
TAIL = FF - NCH * CHUNK
MIX_SLABS = 28
FFN_SLABS = 36
XTRA = (T * TOPK) // (P + 1)
NBLK = NE + XTRA

FIRST = {("mix", 0): 0, ("ffn", 0): MIX_SLABS, ("mix", 1): MIX_SLABS + FFN_SLABS,
         ("ffn", 1): 2 * MIX_SLABS + FFN_SLABS}
STAGES = [("mix", 0), ("ffn", 0), ("mix", 1), ("ffn", 1)]
LENGTH = {"mix": MIX_SLABS, "ffn": FFN_SLABS}


def raw_place(stage, p):
    return p + (RAW_SLOTS - MIX_SLABS % RAW_SLOTS if stage[0] == "mix" else 0)


def raw_slot(stage, p):
    return raw_place(stage, p) % RAW_SLOTS


def uses_before(stage):
    total = [0] * RAW_SLOTS
    for s in STAGES[:STAGES.index(stage)]:
        for p in range(LENGTH[s[0]]):
            total[raw_slot(s, p)] += 1
    return total


def raw_value(stage, p):
    before = sum(raw_slot(stage, q) == raw_slot(stage, p) for q in range(p))
    return 32 * (uses_before(stage)[raw_slot(stage, p)] + before + 1)


def back(stage, p):
    every = [(s, q) for s in STAGES[:3] + [("ffn", 1)] for q in range(LENGTH[s[0]])]
    n = every.index((stage, p))
    return next((b for b in range(1, n + 1) if raw_slot(*every[n - b]) == raw_slot(stage, p)), None)


CHUNKS = ["v", "x1", "q", "x2", "k", "av", "g0", "g1", "g2", "g3"]
COLUMN = {"x1": 0, "x2": 512, "v": 1024, "q": 1536, "k": 2048, "av": 2560,
          "g0": 3072, "g1": 3584, "g2": 4096, "g3": 4608}

PLAN = [("f1", [0]), ("f2", [1]), ("hf0", [4, 5, 6, 7]), ("ht", [0, 1, 2, 3]), ("ft0", [4, 5, 6, 7]),
        ("v", [0, 1, 2, 3]), ("hf1", [4, 5, 6, 7]), ("x1", [0, 1, 2, 3]), ("ft1", [4, 5, 6, 7]),
        ("q", [0, 1]), ("vT", [2, 3]), ("x2", [4, 5, 6, 7]),
        ("k", [0, 1]), ("x1T", [2, 3]), ("av", [4, 5]), ("x2T", [6, 7]),
        ("cf0", [0, 1, 2, 3]), ("g0", [4, 5]), ("qT", [6, 7]), ("g1", [4, 5]), ("kT", [6, 7]),
        ("ci0", [0, 1]), ("sc0", [2, 3]), ("g2", [4, 5]), ("aT0", [6]), ("sc1", [2, 3]), ("av0", [7]),
        ("cf1", [4, 5, 0, 1]), ("aT1", [6]), ("sc2", [2, 3]), ("av1", [7]), ("g3", [4, 5]),
        ("aT2", [6]), ("sc3", [2, 3]), ("av2", [7]), ("ci1", [0, 1]), ("aT3", [6]), ("yT", [4, 5]),
        ("av3", [7]), ("ph0", [0, 1]), ("yaT", [2, 3]), ("ph1", [4, 5]), ("pa0", [6, 7]), ("pa1", [0, 1]),
        ("mT", [2, 3, 4, 5]), ("wo0", [6, 7]), ("wo1", [0, 1]), ("fht", [2, 3, 4, 5])]
PLAN_MOE = [("rt", [0]), ("pos", [1])]


BANKS = dict(PLAN + PLAN_MOE)

LAST_SLAB = {}
for _i, _c in enumerate(CHUNKS):
    LAST_SLAB[_c] = 2 * _i + 1
LAST_SLAB.update({"ph0": 20, "ph1": 21, "pa0": 22, "pa1": 23, "wo0": 25, "wo1": 27})


def turns(counted):
    count, out = [0] * 8, {}
    for layer in range(DEPTH):
        for step, banks in PLAN + (PLAN_MOE if layer == 1 else []):
            for b in banks:
                count[b] += int(counted(step))
                out[layer, step, b] = count[b]
    return out


FILLS = turns(lambda step: step not in LAST_SLAB)
DRAINS = turns(lambda step: 1)

ROUND = 12582912.0
TWO_PI = (6.28125, 0.0019350051879882812, 3.019916050561733e-07)
PI_BELOW = 3.1415925

Q_FIRST = [0, NCH + 1]
LAMBDA_INIT = [0.8 - 0.6 * float(np.exp(-0.3 * layer)) for layer in range(DEPTH)]

PAR_CONV, PAR_GM, PAR_GF, PAR_QN, PAR_KN, PAR_SUB = 0, 36, 44, 52, 116, 180
PAR_N = PAR_SUB + DV


def trunk(nc, x_in, slabs, par_d, lamv_d, wf1_d, wf2_d, bf_d, wf3_d, hyb_d, nffn_d, wr_d,
          cst_d, dft_d, decay_d, zt_d, moec_d, out):
    ctx = ExitStack()

    def sb(name, shape, dt=F32):
        return ctx.enter_context(nc.sbuf_tensor(name, shape, dt))

    def region(name, floats, variants):
        found = {}
        for variant in variants:
            inner = ExitStack()
            for n, shape, dt in variant:
                found[n] = inner.enter_context(nc.sbuf_tensor(n, shape, dt))
            assert sum(int(np.prod(s[1:])) for _, s, _ in variant) <= floats, name
            inner.close()
        sb(name, [P, floats])
        return found

    semaphores = {}

    def sem(name):
        if name not in semaphores:
            semaphores[name] = ctx.enter_context(nc.semaphore(name))
        return semaphores[name]

    RAW = sb("raw", [P, RAW_SLOTS, SLAB])
    HI = sb("w_hi", [P, SPLIT_SLOTS, SLAB], F32R)
    LO = sb("w_lo", [P, SPLIT_SLOTS, SLAB], F32R)
    X = sb("x", [P, TB, D])
    HTH = sb("hT_hi", [P, KD, T], F32R)
    HTL = sb("hT_lo", [P, KD, T], F32R)
    TMP = sb("tmp", [P, 1024])
    IDENT = sb("ident", [P, P])
    ROPE = sb("rope", [P, 2, TB, 32])
    PAR = sb("par", [P, PAR_N])
    STAT = sb("stat", [P, 96])
    LAM = sb("lam", [P, 8])
    HALF = sb("minus_half", [P, 16])
    SQUARES = sb("squares", [P, DV])
    R = {}
    R.update(region("r_h", 2 * 4 * 258, [[("h_tok", [P, TB, D], F32)], [("upad", [P, 2, 4, 258], F32)],
                                         [("qT", [P, NH, T], F32), ("kT", [P, NH, T], F32)]]))
    R.update(region("r_conv", 2048, [[("conv", [P, 2, 4, T], F32)], [("ys", [P, 2, 2, 512], F32)],
                                     [("act_hi", [P, 2, T], F32R), ("act_lo", [P, 2, T], F32R),
                                      ("silu", [P, TB, CHUNK], F32), ("act", [P, TB, CHUNK], F32)]]))
    late = [("g_row", [P, D], F32), ("moec", [P, 3 * P + 64 + 8 + 4], F32),
            ("wr", [P, KD, NE], F32), ("wr_hi", [P, KD, NE], F32R), ("wr_lo", [P, KD, NE], F32R),
            ("lg", [P, TB, NE], F32), ("cmp", [P, TB, NE, NE], F32), ("cmp2", [P, TB, NE, NE], F32),
            ("rank", [P, TB, NE], F32), ("sel1", [P, TB, NE], F32), ("sel2", [P, TB, NE], F32),
            ("sel", [P, TB, NE], F32), ("wts", [P, TB, NE], F32), ("posm", [P, TB, NE], F32),
            ("cnt", [P, NE], F32), ("over", [P, NE], F32), ("oh", [P, 4, NE], F32),
            ("pcol", [P, TB, NBLK + 1], F32), ("wcol", [P, TB, NBLK + 1], F32), ("tv", [P, 8, TB], F32),
            ("nbf", [P, 16], F32), ("nbi", [P, 16], I32), ("nbe", [P, 16], I32), ("wcur", [P, TB], F32), ("wslot", [P, 1], F32),
            ("prod", [P, 4, NE], F32)]
    R.update(region("r_gate", 4096, [[("decay", [P, 2, 2, 512], F32), ("fpm", [P, 2, 2, 512], F32)],
                                     [("gates", [P, TB, 2, D], F32)],
                                     [("hg_hi", [P, TB, D], F32R), ("hg_lo", [P, TB, D], F32R)]]))
    R.update(region("r_xv", 3072, [[("fb", [P, 2, 512], F32), ("zT", [FE, T], F32), ("wf1", [FE, FH], F32),
                                    ("wf2", [FH, FH], F32), ("bf", [FH, 4], F32), ("lamv", [P, 4, DH], F32),
                                    ("arg", [FH, T], F32), ("rnd", [FH, T], F32), ("hdn", [FH, 2, T], F32)],
                                   [("xv", [P, 3, TB, HW], F32)],
                                   [("y_hi", [P, D], F32R), ("y_lo", [P, D], F32R),
                                    ("psel", [P, TB, P], F32R), ("pselT", [P, TB, P], F32R)]]))
    R.update(region("r_qkv", 3072, [[("wf3", [FH, 2048], F32), ("hyb", [1, 1024], F32)],
                                    [("qkv", [P, 3, TB, 512], F32)],
                                    [("e", [P, 2, 2, T], F32), ("a", [P, 2, T], F32), ("aT", [P, 2, T], F32)],
                                    late]))
    FSP = sb("filters", [P, 2, 2, 2, 512])
    HG = FSP[:, 0].rearrange("p a b c -> p a (b c)")
    DFT = sb("dft", [P, 4, 2, T])
    H_TOK, UPAD, QT, KT = R["h_tok"], R["upad"], R["qT"], R["kT"]
    CONV, YS = R["conv"], R["ys"]
    XV, QKV, GATES = R["xv"], R["qkv"], R["gates"]
    PS = [ctx.enter_context(nc.psum_tensor(f"bank{b}", [P, 512], F32)) for b in range(8)]

    raw_loaded = [sem(f"raw_loaded{s}") for s in range(RAW_SLOTS)]
    hi_ready, lo_ready, slab_used = sem("hi_ready"), sem("lo_ready"), sem("slab_used")
    filled = [sem(f"bank_filled{b}") for b in range(8)]
    drained = [sem(f"bank_drained{b}") for b in range(8)]
    silu_done, act_done = sem("silu_done"), sem("act_done")
    turned, act_hi_ready, act_lo_ready = sem("act_turned"), sem("act_hi_ready"), sem("act_lo_ready")
    y_hi_ready, y_ready = sem("y_hi_ready"), sem("y_ready")
    gathered, g_hi_ready, g_lo_ready = sem("gathered"), sem("g_hi_ready"), sem("g_lo_ready")
    wcur_ready = sem("wcur_ready")
    psel_ready, pselT_done, pselT_ready = sem("psel_ready"), sem("pselT_done"), sem("pselT_ready")
    scattered, scatter_added = sem("scattered"), sem("scatter_added")

    class Steps:

        def __init__(self, eng, name):
            self.eng, self.own, self.count, self.last = eng, sem(name), 0, None

        def do(self, ins, signal=None, value=None):
            if signal is None:
                self.count += 1
                signal, value = self.own, self.count
            ins.then_inc(signal, 1)
            self.last = (signal, value)

        def settle(self):
            if self.last is not None:
                self.eng.wait_ge(*self.last)

    def event(name, layer):
        return sem(f"{name}_{layer}")

    def wait_filled(eng, layer, step, i):
        b = BANKS[step][i]
        if step in LAST_SLAB:
            eng.wait_ge(slab_used, FIRST["mix", layer] + LAST_SLAB[step] + 1)
        else:
            eng.wait_ge(filled[b], FILLS[layer, step, b])

    def bank(step, i):
        return PS[BANKS[step][i]]

    def drain_of(layer, step, i):
        b = BANKS[step][i]
        return drained[b], DRAINS[layer, step, b]

    def wait_drained(eng, layer, step, i):
        eng.wait_ge(*drain_of(layer, step, i))

    S_MAX, S_NEG, S_SUM, S_FAC = (STAT[:, 64 + 4 * i:68 + 4 * i] for i in range(4))

    def router(dve, v, tt, ts, stt, gather_lo):
        vec = nc.vector
        lg, cmp, cmp2, rank = R["lg"], R["cmp"], R["cmp2"], R["rank"]
        sel1, sel2, sel, wts, posm, tv = (R[k] for k in ("sel1", "sel2", "sel", "wts", "posm", "tv"))
        over, oh, prod, nbf = R["over"], R["oh"], R["prod"], R["nbf"]
        tril = R["moec"][:, 3 * P:3 * P + 64].rearrange("p (a b) -> p a b", a=NE)
        erow = R["moec"][:, 3 * P + 64:3 * P + 72]

        def flat(ap):
            return ap.rearrange("p a b -> p (a b)")

        def reduce(dst, src, signal=None, value=None):
            v.do(vec.tensor_reduce(dst, src, AX_X, ALU.add), signal, value)

        v.do(vec.memset(R["wslot"][:, :], 0.0))
        v.do(vec.memset(R["pselT"][:, :, :].bitcast(F32), 0.0))
        v.do(vec.memset(R["pcol"][:, :, NBLK:NBLK + 1], -1.0))
        v.do(vec.memset(R["wcol"][:, :, NBLK:NBLK + 1], 0.0))
        v.do(vec.memset(nbf[:, :], 0.0))
        wait_filled(dve, 1, "rt", 0)
        v.do(vec.tensor_copy(flat(lg[:, :, :]), bank("rt", 0)[:, 0:TB * NE]), *drain_of(1, "rt", 0))
        v.settle()
        other = lg[:, :, :].unsqueeze(2).broadcast_to([P, TB, NE, NE])
        own = lg[:, :, :].unsqueeze(3).broadcast_to([P, TB, NE, NE])
        tt(cmp[:, :, :, :], other, own, ALU.is_gt)
        tt(cmp2[:, :, :, :], other, own, ALU.is_equal)
        v.settle()
        for tb in range(TB):
            tt(cmp2[:, tb, :, :], cmp2[:, tb, :, :], tril, ALU.mult)
        v.settle()
        tt(cmp[:, :, :, :], cmp[:, :, :, :], cmp2[:, :, :, :], ALU.add)
        v.settle()
        reduce(flat(rank[:, :, :]), cmp[:, :, :, :].rearrange("p t a b -> p (t a) b"))
        v.settle()
        ts(sel1[:, :, :], rank[:, :, :], 0.0, None, ALU.is_equal)
        ts(sel2[:, :, :], rank[:, :, :], 1.0, None, ALU.is_equal)
        v.settle()
        tt(sel[:, :, :], sel1[:, :, :], sel2[:, :, :], ALU.add, sem("sel_ready"), 1)
        tt(cmp[:, :, 0, :], sel1[:, :, :], lg[:, :, :], ALU.mult)
        tt(cmp[:, :, 1, :], sel2[:, :, :], lg[:, :, :], ALU.mult)
        v.settle()
        reduce(tv[:, 0, :], cmp[:, :, 0, :])
        reduce(tv[:, 1, :], cmp[:, :, 1, :])
        v.settle()
        tt(tv[:, 2, :], tv[:, 1, :], tv[:, 0, :], ALU.subtract, sem("top_diff"), 1)
        wait_filled(dve, 1, "pos", 0)
        stt(flat(posm[:, :, :]), bank("pos", 0)[:, 0:TB * NE], 1.0, flat(sel[:, :, :]), ALU.add, ALU.mult)
        ts(over[:, :], bank("pos", 0)[:, TB * NE:(TB + 1) * NE], float(P), None, ALU.is_gt, None,
           *drain_of(1, "pos", 0))
        v.settle()
        ts(posm[:, :, :], posm[:, :, :], -1.0, None, ALU.add)
        reduce(nbf[:, 0:1], over[:, :])
        v.settle()
        for tb in range(TB):
            ts(R["psel"][:, tb, :], R["moec"][:, 0:P], posm[:, tb, 0:1], None, ALU.is_equal, None,
               *((psel_ready, 1) if tb == 1 else (None, None)))
        ts(nbf[:, 0:1], nbf[:, 0:1], float(NE), None, ALU.add)
        v.settle()
        v.do(vec.tensor_copy(R["nbi"][:, :], nbf[:, :]), sem("blocks_known"), 1)
        dve.wait_ge(sem("hg_hi_ready"), 1)
        tt(R["hg_lo"][:, :, :], HG, R["hg_hi"][:, :, :].bitcast(F32), ALU.subtract, sem("hg_lo_ready"), 1)
        dve.wait_ge(sem("top_exp"), 1)
        ts(tv[:, 4, :], tv[:, 3, :], 1.0, None, ALU.add)
        v.settle()
        v.do(vec.reciprocal(tv[:, 5, :], tv[:, 4, :]))
        v.settle()
        tt(tv[:, 6, :], tv[:, 3, :], tv[:, 5, :], ALU.mult)
        v.settle()
        for tb in range(TB):
            ts(wts[:, tb, :], sel1[:, tb, :], tv[:, 5, tb:tb + 1], None, ALU.mult)
        v.settle()
        for tb in range(TB):
            stt(wts[:, tb, :], sel2[:, tb, :], tv[:, 6, tb:tb + 1], wts[:, tb, :], ALU.mult, ALU.add)
        v.settle()
        v.do(vec.tensor_copy(R["wcur"][:, :].unsqueeze(2), wts[:, :, 0:1]), wcur_ready, 1)
        gather_lo()
        tt(cmp[:, 0, :, :], over[:, :].unsqueeze(1).broadcast_to([P, NE, NE]), tril, ALU.mult)
        v.settle()
        reduce(R["cnt"][:, :], cmp[:, 0, :, :])
        v.settle()
        for j in range(XTRA):
            stt(oh[:, j, :], R["cnt"][:, :], float(j), over[:, :], ALU.is_equal, ALU.mult)
        v.settle()
        for tb in range(TB):
            v.do(vec.tensor_copy(R["pcol"][:, tb, 0:NE], posm[:, tb, :]))
            v.do(vec.tensor_copy(R["wcol"][:, tb, 0:NE], wts[:, tb, :]))
            for src, dst in ((posm, R["pcol"]), (wts, R["wcol"])):
                tt(prod[:, 0:XTRA, :], oh[:, 0:XTRA, :], src[:, tb, :].unsqueeze(1).broadcast_to([P, XTRA, NE]),
                   ALU.mult)
                v.settle()
                reduce(dst[:, tb, NE:NBLK], prod[:, 0:XTRA, :])
                v.settle()
            ts(R["pcol"][:, tb, NE:NBLK], R["pcol"][:, tb, NE:NBLK], -float(P), None, ALU.add)
        v.settle()
        tt(prod[:, 0:XTRA, :], oh[:, 0:XTRA, :], erow.unsqueeze(1).broadcast_to([P, XTRA, NE]), ALU.mult)
        v.settle()
        reduce(nbf[:, NE:NBLK], prod[:, 0:XTRA, :])
        v.settle()
        v.do(vec.tensor_copy(R["nbe"][:, :], nbf[:, :]), sem("experts_known"), 1)

    def load_parameters(eng, layer):
        for dst, src in ((R["zT"][:, :], zt_d), (R["wf1"][:, :], wf1_d[layer]), (R["bf"][:, :], bf_d[layer]),
                         (R["wf2"][:, :], wf2_d[layer])):
            eng.dma_start(dst, src).then_inc(event("hidden_loaded", layer), 16)
        for dst, src in ((R["lamv"][:, :, :].rearrange("p a b -> p (a b)"),
                          lamv_d[layer:layer + 1, :].to_broadcast([P, 4 * DH])),
                         (R["wf3"][:, :], wf3_d[layer]),
                         (R["decay"][:, :, :, :].rearrange("p a b c -> p (a b c)"), decay_d),
                         (R["hyb"][:, :], hyb_d[layer:layer + 1, :]),
                         (PAR[:, :], par_d[layer])):
            eng.dma_start(dst, src).then_inc(event("par_loaded", layer), 16)

    block = ctx.enter_context(nc.Block())

    @block.sync
    def _(sp):
        def mixer_slabs(layer):
            w_in, w_hy, w_at, w_out = (slabs[k][layer] for k in ("w_in", "w_hy_o", "w_at_o", "w_out"))
            found = []
            for c in CHUNKS:
                for k in (0, 4):
                    found.append(w_in[k * P:(k + 4) * P, COLUMN[c]:COLUMN[c] + 512])
            for w in (w_hy, w_at):
                for h in range(2):
                    found.append(w[:, h * 512:(h + 1) * 512])
            for h in range(2):
                for k in (0, 4):
                    found.append(w_out[k * P:(k + 4) * P, h * 512:(h + 1) * 512])
            return found

        def put(slot, dst, src, free):
            if free is not None:
                sp.wait_ge(lo_ready, free)
            for d, s in zip(dst, src):
                sp.dma_start(d, s).then_inc(raw_loaded[slot], 16)

        sp.dma_start(IDENT[:, :], cst_d[:, 0:P]).then_inc(sem("cst_loaded"), 16)
        load_parameters(sp, 0)
        sp.dma_start(X[:, :, :], x_in.rearrange("(t p) d -> p t d", p=P)).then_inc(sem("x_loaded"), 16)
        sp.dma_start(DFT[:, :, :, :].rearrange("p a b c -> p (a b c)"), dft_d).then_inc(sem("cst_loaded"), 16)
        sp.dma_start(ROPE[:, :, :, :].rearrange("p a b c -> p (a b c)"), cst_d[:, P:2 * P])\
            .then_inc(sem("cst_loaded"), 16)
        for layer in range(DEPTH):
            stage, first = ("mix", layer), FIRST["mix", layer]
            for p, src in enumerate(mixer_slabs(layer)):
                slot = raw_slot(stage, p)
                dst = RAW[:, slot, :].rearrange("p (k n) -> p k n", k=4)
                src = src.rearrange("(k p) n -> p k n", p=P)
                far = back(stage, p)
                put(slot, [dst[:, 0:2, :], dst[:, 2:4, :]], [src[:, 0:2, :], src[:, 2:4, :]],
                    None if far is None else first + p - far + 1)

            first = FIRST["ffn", layer]
            kind = "dense" if layer == 0 else "moe"
            w_gate, w_up, w_down = (slabs[f"w_{kind}_{k}"] for k in ("gate", "up", "down"))
            assert all(back(("ffn", layer), p) == RAW_SLOTS for p in range(FFN_SLABS))

            def gate_up(e, p, n, k0, nk, col, width):
                dst = RAW[:, p % RAW_SLOTS, 0:2 * nk * width].rearrange("p (k n) -> p k n", k=nk)
                src = [w[e, k0 * P:(k0 + nk) * P, col].rearrange("o (k p) n -> p (o k) n", p=P)
                       for w in (w_gate, w_up)]
                put(p % RAW_SLOTS, [dst[:, :, 0:width], dst[:, :, width:2 * width]], src, n - RAW_SLOTS + 1)

            def down(e, p, n, rows):
                dst = RAW[:, p % RAW_SLOTS, :].rearrange("p (k n) -> p k n", k=2)
                put(p % RAW_SLOTS, [dst[:, j, :] for j in range(2)],
                    [w_down[e, r, :].rearrange("o p n -> p (o n)") for r in rows], n - RAW_SLOTS + 1)

            def down_tail(e, p, n, k):
                lo, hi = NCH * CHUNK + k * P, min(NCH * CHUNK + (k + 1) * P, FF)
                halves = [slice(0, 512), slice(512, D)]
                put(p % RAW_SLOTS, [RAW[0:hi - lo, p % RAW_SLOTS, h] for h in halves],
                    [w_down[e, lo:hi, h].rearrange("o p n -> p (o n)") for h in halves], n - RAW_SLOTS + 1)

            def chunk_rows(c):
                return [slice(c * CHUNK, c * CHUNK + P), slice(c * CHUNK + P, (c + 1) * CHUNK)]

            def pair(e, n0, p0, cols, rows):
                for j in range(2):
                    p = p0 + 3 * j
                    for part in range(2):
                        gate_up(e, p + part, n0 + p + part, 4 * part, 4, cols[j], CHUNK)
                    down(e, p + 2, n0 + p + 2, rows[j])

            def block_slabs(n0, e):
                for part in range(2):
                    gate_up(e, part, n0 + part, 4 * part, 4, slice(0, CHUNK), CHUNK)
                with sp.Fori(0, 4) as i:
                    c0 = [sp.snap((2 * i + j) * CHUNK) for j in range(3)]
                    r1 = [sp.snap((2 * i + j) * CHUNK + P) for j in range(2)]
                    pair(e, sp.snap(n0 + 6 * i), 2, [bass.ds(c0[j + 1], CHUNK) for j in range(2)],
                         [[bass.ds(c0[j], P), bass.ds(r1[j], P)] for j in range(2)])
                c = NCH - 1
                for part in range(2):
                    gate_up(e, 26 + part, n0 + 26 + part, 4 * part, 4, slice(c * CHUNK, (c + 1) * CHUNK), CHUNK)
                down(e, 28, n0 + 28, chunk_rows(c - 1))
                for part in range(4):
                    gate_up(e, 29 + part, n0 + 29 + part, 2 * part, 2, slice(NCH * CHUNK, FF), TAIL)
                down(e, 33, n0 + 33, chunk_rows(c))
                for k in range(2):
                    down_tail(e, 34 + k, n0 + 34 + k, k)

            if layer == 0:
                block_slabs(first, slice(0, 1))
            else:
                with sp.Fori(0, NE) as b:
                    block_slabs(sp.snap(FFN_SLABS * b + first), bass.ds(b, 1))
                sp.wait_ge(sem("experts_known"), 1)
                nb = sp.value_load(R["nbi"][0:1, 0:1], min_val=NE, max_val=NBLK)
                with sp.If(nb > NE):
                    with sp.Fori(NE, nb) as b:
                        e = sp.value_load(R["nbe"][0:1, bass.ds(b, 1)], min_val=0, max_val=NE - 1)
                        block_slabs(sp.snap(FFN_SLABS * b + first), bass.ds(e, 1))
                n0 = sp.snap(FFN_SLABS * nb + first)
                e = slice(0, 1)
                for part in range(2):
                    gate_up(e, part, n0 + part, 4 * part, 4, slice(0, CHUNK), CHUNK)
                gate_up(e, 2, n0 + 2, 0, 4, slice(CHUNK, 2 * CHUNK), CHUNK)
        sp.wait_ge(scatter_added, 4 * nb + 4)
        sp.dma_start(out.rearrange("(t p) d -> p t d", p=P), X[:, :, :]).then_inc(sem("stored"), 16)
        sp.wait_ge(sem("stored"), 16)

    @block.gpsimd
    def _(pool):
        g = Steps(pool, "pool_steps")
        def rstd(layer, name, src, dst, n, width):
            pool.wait_ge(event(f"{name}_ss", layer), 1)
            if width == D:
                g.do(nc.gpsimd.tensor_tensor(dst, src, STAT[:, TB:2 * TB], ALU.add))
                g.settle()
                src = dst
            g.do(nc.gpsimd.tensor_scalar(dst, src, 1.0 / width, EPS, ALU.mult, ALU.add))
            g.settle()
            s = event(f"{name}_rstd", layer)
            g.do(nc.gpsimd.tensor_tensor(dst, dst, HALF[:, 0:n], ALU.pow), s, 1)

        g.do(nc.gpsimd.memset(HALF[:, :], -0.5))
        g.settle()
        for layer in range(DEPTH):
            if layer:
                wait_drained(pool, layer - 1, "fht", 3)
                load_parameters(pool, layer)
            rstd(layer, "norm_mix", STAT[:, 0:TB], STAT[:, 4:4 + TB], TB, D)
            rstd(layer, "q", STAT[:, 8:24], STAT[:, 24:40], 16, DH)
            rstd(layer, "k", STAT[:, 8:24], STAT[:, 40:56], 16, DH)
            for h in range(NH):
                pool.wait_ge(event("o_ss", layer), h + 1)
                g.do(nc.gpsimd.tensor_scalar(STAT[:, 84:86], STAT[:, 56 + 2 * (h % 2):58 + 2 * (h % 2)],
                                             1.0 / DV, EPS, ALU.mult, ALU.add))
                g.settle()
                g.do(nc.gpsimd.tensor_tensor(STAT[:, 80 + 2 * (h % 2):82 + 2 * (h % 2)], STAT[:, 84:86],
                                             HALF[:, 0:TB], ALU.pow), event("o_rstd", layer), h + 1)
            if layer == 1:
                wait_filled(pool, layer, "yaT", 1)
                pool.dma_start(R["g_row"][:, :], nffn_d.to_broadcast([P, D])).then_inc(sem("moe_loaded"), 16)
                pool.dma_start(R["wr"][:, :, :], wr_d.rearrange("(k p) e -> p k e", p=P)).then_inc(sem("moe_loaded"), 16)
                pool.dma_start(R["moec"][:, :], moec_d).then_inc(sem("moe_loaded"), 16)
            rstd(layer, "norm_ffn", STAT[:, 0:TB], STAT[:, 4:4 + TB], TB, D)

    @block.scalar
    def _(act):
        a = Steps(act, "act_steps")
        done = [0]

        def copy(dst, src, signal=None, value=None, **kw):
            a.do(nc.scalar.activation(dst, src, ACT.Copy, **kw), signal, value)

        def split(n, slot_value, raw_slot, split_slot, width=SLAB):
            act.wait_ge(raw_loaded[raw_slot], slot_value)
            if not isinstance(n, int) or n >= SPLIT_SLOTS:
                act.wait_ge(slab_used, n - (SPLIT_SLOTS - 1))
            nc.scalar.activation(HI[:, split_slot, 0:width], RAW[:, raw_slot, 0:width], ACT.Copy)\
              .then_inc(hi_ready, 1)

        def split_to(last, stage):
            first = FIRST[stage]
            while done[0] <= min(last, first + LENGTH[stage[0]] - 1):
                n = done[0]
                p = n - first
                split(n, raw_value(stage, p), raw_slot(stage, p), n % SPLIT_SLOTS)
                done[0] += 1

        for layer in range(DEPTH):
            stage = ("mix", layer)
            first = FIRST[stage]

            def ahead(step):
                split_to(first + LAST_SLAB[step] + 2, stage)

            def evac(step, i, dst, src=None, **kw):
                wait_filled(act, layer, step, i)
                copy(dst, bank(step, i)[:, :] if src is None else src, *drain_of(layer, step, i), **kw)

            def squares(i, name):
                tb, half = i // 2, i % 2
                cols = slice(half * 512, (half + 1) * 512)
                a.do(nc.scalar.activation(H_TOK[:, tb, cols], X[:, tb, cols], ACT.Square,
                                          accum_out=STAT[:, TB * half + tb:TB * half + tb + 1]),
                     *((event(f"{name}_ss", layer), 1) if i == 3 else (None, None)))

            if layer == 0:
                act.wait_ge(sem("x_loaded"), 16)
            for i in range(4):
                if layer:
                    act.wait_ge(event("ffn_added", 0), i + 1)
                squares(i, "norm_mix")
            for j in range(2):
                act.wait_ge(event("sin_arg", layer), j + 1)
                a.do(nc.scalar.activation(R["hdn"][:, j, :], R["rnd"][:, :], ACT.Sin), event("sin_done", layer), j + 1)
            act.wait_ge(event("lam_sums", layer), 1)
            a.do(nc.scalar.activation(LAM[:, 2:4], LAM[:, 0:2], ACT.Exp), event("lam_exp", layer), 1)
            for step, _ in PLAN[2:]:
                if step in LAST_SLAB:
                    ahead(step)
                if step == "ht":
                    for i in range(4):
                        wait_filled(act, layer, "ht", i)
                        for j in range(2):
                            kd = 2 * i + j
                            copy(HTH[:, kd, :], bank("ht", i)[:, j * T:(j + 1) * T], event("ht_hi", layer), kd + 1,
                                 scale=PAR[:, PAR_GM + kd:PAR_GM + kd + 1])
                    split_to(first + 2, stage)
                elif step[:2] == "ft":
                    for i in range(4):
                        evac(step, i, FSP[:, i // 2, int(step[2]), i % 2, :], scale=1.0 / T)
                if step in ("v", "x1", "x2"):
                    c = ("v", "x1", "x2").index(step)
                    if c == 0:
                        act.wait_ge(event("pads", layer), 1)
                    if c == 2:
                        act.wait_ge(event("conv_done", layer), 4)
                    for i in range(4):
                        evac(step, i, UPAD[:, c % 2, i, 1:T + 1], bank(step, i)[:, 0:T])
                elif step in ("q", "k", "av"):
                    if step == "q":
                        act.wait_ge(event("fpm", layer), 4)
                    c = ("q", "k", "av").index(step)
                    for tb in range(TB):
                        evac(step, tb, QKV[:, c, tb, :])
                elif step in ("vT", "x1T", "x2T"):
                    c = ("x1T", "x2T", "vT").index(step)
                    for tb in range(TB):
                        evac(step, tb, XV[:, c, tb, :])
                elif step in ("g0", "g1", "g2", "g3"):
                    c = int(step[1])
                    for tb in range(TB):
                        wait_filled(act, layer, step, tb)
                        a.do(nc.scalar.activation(GATES[:, tb, c // 2, (c % 2) * 512:(c % 2 + 1) * 512],
                                                  bank(step, tb)[:, :], ACT.Sigmoid), *drain_of(layer, step, tb))
                elif step in ("qT", "kT"):
                    act.wait_ge(event("conv_done", layer), 12)
                    dst = QT if step == "qT" else KT
                    for i in range(2):
                        evac(step, i, dst[:, 2 * i:2 * i + 2, :].rearrange("p a b -> p (a b)"))
                elif step[:2] == "sc":
                    h = int(step[2])
                    act.wait_ge(event("neg_max", layer), h + 1)
                    if h:
                        act.wait_ge(event("a_ready", layer), 2 * h)
                    for c in range(2):
                        for tb in range(TB):
                            k = 2 * c + tb
                            a.do(nc.scalar.activation(R["e"][:, tb, c, :], bank(step, c)[:, tb * T:(tb + 1) * T],
                                                      ACT.Exp, scale=DH ** -0.5, bias=S_NEG[:, k:k + 1],
                                                      accum_out=S_SUM[:, k:k + 1]),
                                 *(drain_of(layer, step, c) if tb else (None, None)))
                elif step[:2] == "aT":
                    evac(step, 0, R["aT"][:, :, :].rearrange("p a b -> p (a b)"))
                elif step in ("av0", "av1", "av2", "av3"):
                    h = int(step[2])
                    wait_filled(act, layer, step, 0)
                    if h >= 2:
                        act.wait_ge(event("o_rstd", layer), h - 1)
                    for tb in range(TB):
                        a.settle()
                        a.do(nc.scalar.activation(SQUARES[:, :], bank(step, 0)[:, tb * DV:(tb + 1) * DV], ACT.Square,
                                                  accum_out=STAT[:, 56 + 2 * (h % 2) + tb:57 + 2 * (h % 2) + tb]),
                             *((event("o_ss", layer), h + 1) if tb == 1 else (None, None)))
                elif step in ("yT", "yaT", "mT", "fht"):
                    if step == "fht":
                        break
                    at = 4 if step == "yaT" else 0
                    for i in range(len(BANKS[step])):
                        wait_filled(act, layer, step, i)
                        copy(HTH[:, at + 2 * i:at + 2 * i + 2, :].rearrange("p a b -> p (a b)"), bank(step, i)[:, :],
                             event(f"{step}_hi", layer), i + 1)
            if layer == 1:
                act.wait_ge(sem("moe_loaded"), 48)
                copy(R["wr_hi"][:, :, :], R["wr"][:, :, :], sem("wr_hi_ready"), 1)
            stage = ("ffn", layer)
            first = FIRST[stage]
            for half in range(2):
                for tb in range(TB):
                    wait_drained(act, layer, f"wo{half}", tb)
                    squares(2 * tb + half, "norm_ffn")
                split_to(first + half * (2 - layer), stage)
            for i in range(4):
                wait_filled(act, layer, "fht", i)
                for j in range(2):
                    kd = 2 * i + j
                    copy(HTH[:, kd, :], bank("fht", i)[:, j * T:(j + 1) * T], event("fht_hi", layer), kd + 1,
                         scale=PAR[:, PAR_GF + kd:PAR_GF + kd + 1])
            if layer == 1:
                act.wait_ge(sem("h_scaled"), TB)
                copy(R["hg_hi"][:, :, :], HG, sem("hg_hi_ready"), 1)
                act.wait_ge(sem("top_diff"), 1)
                a.do(nc.scalar.activation(R["tv"][:, 3, :], R["tv"][:, 2, :], ACT.Exp), sem("top_exp"), 1)

            uses = uses_before(stage)

            def ffn_split(p, n0, r0, width=SLAB):
                split(n0 + p, 32 * (uses[p % RAW_SLOTS] + p // RAW_SLOTS + 1) + r0, p % RAW_SLOTS,
                      (first + p) % SPLIT_SLOTS, width)

            tbs = TB if layer == 0 else 1

            def silu(q, n, parity, width=CHUNK):
                act.wait_ge(slab_used, n + 1)
                if not isinstance(q, int) or q:
                    act.wait_ge(act_done, q)
                for tb in range(tbs):
                    src = PS[tb if layer == 0 else parity][:, 0:width]
                    ins = nc.scalar.activation(R["silu"][:, tb, 0:width], src, ACT.Silu)
                ins.then_inc(silu_done, 1)

            def turned_hi(q):
                act.wait_ge(turned, q + 1)
                nc.scalar.activation(R["act_hi"][:, :, 0:tbs * P], PS[2][:, 0:2 * tbs * P].rearrange("p (k t) -> p k t", k=2),
                                     ACT.Copy).then_inc(act_hi_ready, 1)

            def gather_hi(b):
                for i in range(2):
                    act.wait_ge(gathered, 4 * b + i + 1)
                    ins = nc.scalar.activation(HTH[:, 4 * i:4 * i + 4, 0:P],
                                               PS[6 + i][:, :].rearrange("p (k t) -> p k t", k=4), ACT.Copy)
                ins.then_inc(g_hi_ready, 1)

            def scaled_y_hi(n):
                act.wait_ge(slab_used, n)
                for h in range(2):
                    ins = nc.scalar.activation(R["y_hi"][:, h * 512:(h + 1) * 512], PS[4 + h][:, :], ACT.Copy,
                                               scale=R["wslot"][:, 0:1])
                ins.then_inc(y_hi_ready, 1)

            def ffn_block(b, is_moe):
                n0 = act.snap(FFN_SLABS * b + first) if is_moe else first
                r0 = act.snap(32 * (FFN_SLABS // RAW_SLOTS) * b) if is_moe else 0
                qb = act.snap((NCH + 1) * b + Q_FIRST[layer]) if is_moe else Q_FIRST[layer]
                if is_moe:
                    scaled_y_hi(n0)
                    ffn_split(2, n0, r0)
                ffn_split(3, n0, r0)
                silu(qb, n0 + 1, 0)
                ffn_split(4, n0, r0)

                def chunk(p, q, parity, n0, r0, width=SLAB):
                    turned_hi(q - 1)
                    ffn_split(p + 3, n0, r0, width)
                    silu(q, n0 + p + 1, parity)
                    ffn_split(p + 4, n0, r0, width)
                    ffn_split(p + 5, n0, r0, width)

                with act.Fori(0, 4) as i:
                    n0i, r0i = act.snap(n0 + 6 * i), act.snap(r0 + 32 * i)
                    qi = act.snap(qb + 2 * i)
                    chunk(2, qi + 1, 1, n0i, r0i)
                    chunk(5, qi + 2, 0, n0i, r0i)
                if is_moe:
                    act.wait_ge(pselT_done, b + 1)
                    nc.scalar.activation(R["pselT"][:, :, :].rearrange("p a b -> p (a b)"), PS[3][:, 0:TB * P], ACT.Copy)
                    nc.scalar.activation(R["wslot"][:, 0:1], PS[3][:, 2 * P:2 * P + 1], ACT.Copy).then_inc(pselT_ready, 1)
                chunk(26, qb + NCH - 1, 1, n0, r0, 4 * TAIL)
                ffn_split(32, n0, r0, 4 * TAIL)
                turned_hi(qb + NCH - 1)
                ffn_split(33, n0, r0)
                ffn_split(34, n0, r0, D)
                silu(qb + NCH, n0 + 32, 0, TAIL)
                ffn_split(35, n0, r0, D)
                if is_moe:
                    ffn_split(FFN_SLABS, n0, r0)
                turned_hi(qb + NCH)
                if is_moe:
                    gather_hi(b + 1)
                    ffn_split(FFN_SLABS + 1, n0, r0)

            if layer == 0:
                ffn_block(0, False)
                done[0] = FIRST["mix", 1]
            else:
                gather_hi(0)
                act.wait_ge(sem("blocks_known"), 1)
                nb = act.value_load(R["nbi"][0:1, 0:1], min_val=NE, max_val=NBLK)
                with act.Fori(0, nb) as b:
                    ffn_block(b, True)
                scaled_y_hi(FFN_SLABS * nb + first)

    @block.vector
    def _(dve):
        v = Steps(dve, "dve_steps")
        vec = nc.vector
        done = [0]

        def tt(dst, in0, in1, op, signal=None, value=None):
            v.do(vec.tensor_tensor(dst, in0, in1, op), signal, value)

        def ts(dst, in0, s1, s2, op0, op1=None, signal=None, value=None):
            v.do(vec.tensor_scalar(dst, in0, s1, s2, op0, *([op1] if op1 else [])), signal, value)

        def stt(dst, in0, s, in1, op0, op1, signal=None, value=None):
            v.do(vec.scalar_tensor_tensor(out=dst, in0=in0, scalar=s, in1=in1, op0=op0, op1=op1), signal, value)

        def split(n, raw_slot, split_slot, width=SLAB):
            dve.wait_ge(hi_ready, n + 1)
            vec.tensor_tensor(LO[:, split_slot, 0:width], RAW[:, raw_slot, 0:width],
                              HI[:, split_slot, 0:width].bitcast(F32), ALU.subtract).then_inc(lo_ready, 1)

        def split_to(last, stage):
            first = FIRST[stage]
            while done[0] <= min(last, first + LENGTH[stage[0]] - 1):
                n = done[0]
                split(n, raw_slot(stage, n - first), n % SPLIT_SLOTS)
                done[0] += 1

        def flat(ap):
            return ap.rearrange("p a b -> p (a b)")

        for layer in range(DEPTH):
            stage = ("mix", layer)
            first = FIRST[stage]
            dve.wait_ge(event("hidden_loaded", layer), 4 * 16)
            for j in range(2):
                wait_filled(dve, layer, f"f{j + 1}", 0)
                arg, rnd = R["arg"][:, :], R["rnd"][:, :]
                ts(arg, bank(f"f{j + 1}", 0)[0:FH, 0:T], R["bf"][:, 2 * j:2 * j + 1], R["bf"][:, 2 * j + 1:2 * j + 2],
                   ALU.add, ALU.mult, *drain_of(layer, f"f{j + 1}", 0))
                v.settle()
                ts(rnd, arg, float(np.float32(0.5 / np.pi)), ROUND, ALU.mult, ALU.add)
                v.settle()
                ts(rnd, rnd, ROUND, None, ALU.subtract)
                for part in TWO_PI:
                    v.settle()
                    stt(arg, rnd, -part, arg, ALU.mult, ALU.add)
                v.settle()
                ts(rnd, arg, PI_BELOW, -PI_BELOW, ALU.min, ALU.max, event("sin_arg", layer), j + 1)
            dve.wait_ge(event("par_loaded", layer), 5 * 16)
            lv = R["lamv"]
            tt(TMP[:, 0:DH], lv[:, 0, :], lv[:, 1, :], ALU.mult)
            tt(TMP[:, DH:2 * DH], lv[:, 2, :], lv[:, 3, :], ALU.mult)
            ts(PAR[:, PAR_SUB:PAR_SUB + DV], PAR[:, PAR_SUB:PAR_SUB + DV], 1.0 - LAMBDA_INIT[layer], None, ALU.mult)
            v.settle()
            v.do(vec.tensor_reduce(LAM[:, 0:2], TMP[:, 0:2 * DH].rearrange("p (a b) -> p a b", a=2), AX_X, ALU.add),
                 event("lam_sums", layer), 1)
            dve.wait_ge(event("norm_mix_rstd", layer), 1)
            for tb in range(TB):
                ts(H_TOK[:, tb, :], X[:, tb, :], STAT[:, 4 + tb:5 + tb], None, ALU.mult, None,
                   event("h_ready", layer), tb + 1)
            fb, fpm = R["fb"], R["fpm"]

            def norm_rope(step, c, rstd_at):
                x = QKV[:, c, :, :].rearrange("p t (s d) -> p (t s) d", d=DH)
                tmp = TMP[:, :].rearrange("p (s d) -> p s d", d=DH)
                for tb in range(TB):
                    wait_drained(dve, layer, step, tb)
                v.settle()
                tt(tmp, x, x, ALU.mult)
                v.settle()
                v.do(vec.tensor_reduce(STAT[:, 8:24], tmp, AX_X, ALU.add), event(f"{step}_ss", layer), 1)
                dve.wait_ge(event(f"{step}_rstd", layer), 1)
                tt(x, x, STAT[:, rstd_at:rstd_at + 16].unsqueeze(2).broadcast_to([P, 16, DH]), ALU.mult)
                v.settle()
                gain = PAR[:, (PAR_QN if step == "q" else PAR_KN):][:, 0:DH]
                tt(x, x, gain.unsqueeze(1).broadcast_to([P, 16, DH]), ALU.mult)
                v.settle()
                for tb in range(TB):
                    y = QKV[:, c, tb, :].rearrange("p (s d) -> p s d", d=DH)
                    x1, x2 = y[:, :, 0:32], y[:, :, 32:64]
                    cos, sin = (ROPE[:, k, tb, :].unsqueeze(1).broadcast_to([P, 8, 32]) for k in range(2))
                    t = TMP[:, tb * 512:(tb + 1) * 512].rearrange("p (k s d) -> p k s d", k=2, d=32)
                    tt(t[:, 0], x2, sin, ALU.mult)
                    tt(t[:, 1], x1, sin, ALU.mult)
                    v.settle()
                    tt(x1, x1, cos, ALU.mult)
                    tt(x2, x2, cos, ALU.mult)
                    v.settle()
                    tt(x1, x1, t[:, 0], ALU.subtract)
                    tt(x2, x2, t[:, 1], ALU.add, event(f"{step}_roped", layer), tb + 1)

            for step, _ in PLAN[2:]:
                if step in LAST_SLAB:
                    split_to(first + LAST_SLAB[step] + 2, stage)
                if step[:2] == "hf":
                    o = int(step[2])
                    if o:
                        wait_filled(dve, layer, "ft0", 3)
                    for jt in range(2):
                        for i in range(2):
                            wait_filled(dve, layer, step, 2 * jt + i)
                            tt(fb[:, i, :], bank(step, 2 * jt + i)[:, :], R["decay"][:, jt, i, :], ALU.mult,
                               *drain_of(layer, step, 2 * jt + i))
                        v.settle()
                        if jt == 0:
                            tt(fb[0:1, 0, :], fb[0:1, 0, :], R["hyb"][0:1, o * HW:(o + 1) * HW], ALU.add)
                            v.settle()
                        tt(fpm[:, jt, 0, :], fb[:, 0, :], fb[:, 1, :], ALU.add)
                        tt(fpm[:, jt, 1, :], fb[:, 0, :], fb[:, 1, :], ALU.subtract,
                           event("fpm", layer), 2 * o + jt + 1)
                        v.settle()
                elif step == "ht":
                    for i in range(4):
                        dve.wait_ge(event("ht_hi", layer), 2 * i + 2)
                        for j in range(2):
                            kd = 2 * i + j
                            stt(HTL[:, kd, :], bank("ht", i)[:, j * T:(j + 1) * T], PAR[:, PAR_GM + kd:PAR_GM + kd + 1],
                                HTH[:, kd, :].bitcast(F32), ALU.mult, ALU.subtract,
                                *(drain_of(layer, "ht", i) if j else (None, None)))
                    wait_filled(dve, layer, "ht", 3)
                    v.do(vec.memset(UPAD[:, :, :, 0:1], 0.0))
                    v.do(vec.memset(UPAD[:, :, :, T + 1:T + 2], 0.0), event("pads", layer), 1)
                    split_to(first + 2, stage)
                elif step in ("v", "x1", "x2"):
                    c = ("v", "x1", "x2").index(step)
                    if c == 2:
                        wait_filled(dve, layer, "vT", 1)
                    for tap in range(3):
                        if tap:
                            v.settle()
                        for i in range(4):
                            w = PAR[:, PAR_CONV + 3 * (COLUMN[step] // P + i) + tap:][:, 0:1]
                            src, dst = UPAD[:, c % 2, i, tap:tap + T], CONV[:, c % 2, i, :]
                            if tap == 0:
                                wait_drained(dve, layer, step, i)
                                ts(dst, src, w, None, ALU.mult)
                            else:
                                stt(dst, src, w, dst, ALU.mult, ALU.add,
                                    *((event("conv_done", layer), 4 * c + i + 1) if tap == 2 else (None, None)))
                elif step in ("q", "k"):
                    if step == "q":
                        dve.wait_ge(event("lam_exp", layer), 1)
                        tt(LAM[:, 4:5], LAM[:, 3:4], LAM[:, 2:3], ALU.subtract)
                        v.settle()
                        ts(LAM[:, 4:5], LAM[:, 4:5], -LAMBDA_INIT[layer], None, ALU.add)
                        if layer == 0:
                            dve.wait_ge(sem("cst_loaded"), 3 * 16)
                    norm_rope(step, ("q", "k").index(step), 24 if step == "q" else 40)
                elif step in ("cf0", "cf1"):
                    o = int(step[2])
                    for kt in range(2):
                        re, im = bank(step, 2 * kt)[:, :], bank(step, 2 * kt + 1)[:, :]
                        wait_filled(dve, layer, step, 2 * kt + 1)
                        if o == 0 and kt == 0:
                            wait_drained(dve, layer, "ft1", 3)
                            wait_filled(dve, layer, "x2T", 1)
                        v.settle()
                        tt(YS[:, kt, 0, :], FSP[:, kt, o, 0, :], re, ALU.mult)
                        tt(TMP[:, 0:512], FSP[:, kt, o, 1, :], im, ALU.mult)
                        tt(YS[:, kt, 1, :], FSP[:, kt, o, 0, :], im, ALU.mult, *drain_of(layer, step, 2 * kt + 1))
                        tt(TMP[:, 512:1024], FSP[:, kt, o, 1, :], re, ALU.mult, *drain_of(layer, step, 2 * kt))
                        v.settle()
                        tt(YS[:, kt, 0, :], YS[:, kt, 0, :], TMP[:, 0:512], ALU.subtract)
                        tt(YS[:, kt, 1, :], YS[:, kt, 1, :], TMP[:, 512:1024], ALU.add,
                           event("ys_ready", layer), 2 * o + kt + 1)
                elif step in ("ci0", "ci1"):
                    o = int(step[2])
                    for tb in range(TB):
                        wait_filled(dve, layer, step, tb)
                        wait_drained(dve, layer, ("x1T", "x2T")[o], tb)
                        tt(XV[:, o, tb, :], XV[:, o, tb, :], bank(step, tb)[:, :], ALU.mult,
                           *drain_of(layer, step, tb))
                elif step[:2] == "sc":
                    h = int(step[2])
                    for c in range(2):
                        wait_filled(dve, layer, step, c)
                        v.do(vec.tensor_reduce(S_MAX[:, 2 * c:2 * c + 2],
                                               bank(step, c)[:, :].rearrange("p (t k) -> p t k", t=TB), AX_X, ALU.max))
                    v.settle()
                    ts(S_NEG, S_MAX, -DH ** -0.5, None, ALU.mult, None, event("neg_max", layer), h + 1)
                    for c in range(2):
                        wait_drained(dve, layer, step, c)
                    v.do(vec.reciprocal(S_FAC, S_SUM))
                    v.settle()
                    ts(S_FAC[:, 2:4], S_FAC[:, 2:4], LAM[:, 4:5], None, ALU.mult)
                    if h:
                        wait_filled(dve, layer, f"aT{h - 1}", 0)
                    v.settle()
                    for tb in range(TB):
                        ts(R["a"][:, tb, :], R["e"][:, tb, 1, :], S_FAC[:, 2 + tb:3 + tb], None, ALU.mult)
                    v.settle()
                    for tb in range(TB):
                        stt(R["a"][:, tb, :], R["e"][:, tb, 0, :], S_FAC[:, tb:tb + 1], R["a"][:, tb, :],
                            ALU.mult, ALU.add, event("a_ready", layer), 2 * h + tb + 1)
                elif step[:2] == "av" and step != "av":
                    h = int(step[2])
                    wait_filled(dve, layer, step, 0)
                    dve.wait_ge(event("o_rstd", layer), h + 1)
                    for tb in range(TB):
                        stt(QKV[:, 2, tb, h * DV:(h + 1) * DV], bank(step, 0)[:, tb * DV:(tb + 1) * DV],
                            STAT[:, 80 + 2 * (h % 2) + tb:81 + 2 * (h % 2) + tb], PAR[:, PAR_SUB:PAR_SUB + DV],
                            ALU.mult, ALU.mult, *(drain_of(layer, step, 0) if tb else (None, None)))
                elif step in ("yT", "yaT", "mT"):
                    at = 4 if step == "yaT" else 0
                    for i in range(len(BANKS[step])):
                        dve.wait_ge(event(f"{step}_hi", layer), i + 1)
                        tt(flat(HTL[:, at + 2 * i:at + 2 * i + 2, :]), bank(step, i)[:, :],
                           flat(HTH[:, at + 2 * i:at + 2 * i + 2, :]).bitcast(F32), ALU.subtract,
                           *drain_of(layer, step, i))
                elif step[:2] == "ph":
                    half = slice(int(step[2]) * 512, int(step[2]) * 512 + 512)
                    for tb in range(TB):
                        wait_filled(dve, layer, step, tb)
                        wait_drained(dve, layer, f"g{step[2]}", tb)
                        tt(GATES[:, tb, 0, half], GATES[:, tb, 0, half], bank(step, tb)[:, :], ALU.mult,
                           *drain_of(layer, step, tb))
                elif step[:2] == "pa":
                    half = slice(int(step[2]) * 512, int(step[2]) * 512 + 512)
                    for tb in range(TB):
                        wait_filled(dve, layer, step, tb)
                        wait_drained(dve, layer, f"g{2 + int(step[2])}", tb)
                        v.settle()
                        tt(TMP[:, 0:512], GATES[:, tb, 1, half], bank(step, tb)[:, :], ALU.mult,
                           *drain_of(layer, step, tb))
                        v.settle()
                        tt(GATES[:, tb, 0, half], GATES[:, tb, 0, half], TMP[:, 0:512], ALU.add,
                           event("merged", layer), 2 * int(step[2]) + tb + 1)
                elif step[:2] == "wo":
                    half = slice(int(step[2]) * 512, int(step[2]) * 512 + 512)
                    for tb in range(TB):
                        wait_filled(dve, layer, step, tb)
                        tt(X[:, tb, half], X[:, tb, half], bank(step, tb)[:, :], ALU.add,
                           *drain_of(layer, step, tb))

            stage = ("ffn", layer)
            first = FIRST[stage]
            split_to(first, stage)
            if layer == 1:
                dve.wait_ge(sem("wr_hi_ready"), 1)
                tt(R["wr_lo"][:, :, :], R["wr"][:, :, :], R["wr_hi"][:, :, :].bitcast(F32), ALU.subtract)
            dve.wait_ge(event("norm_ffn_rstd", layer), 1)
            for tb in range(TB):
                ts(H_TOK[:, tb, :], X[:, tb, :], STAT[:, 4 + tb:5 + tb], None, ALU.mult, None,
                   event("hf_ready", layer), tb + 1)
            split_to(first + 1, stage)
            for i in range(4):
                dve.wait_ge(event("fht_hi", layer), 2 * i + 2)
                for j in range(2):
                    kd = 2 * i + j
                    stt(HTL[:, kd, :], bank("fht", i)[:, j * T:(j + 1) * T], PAR[:, PAR_GF + kd:PAR_GF + kd + 1],
                        HTH[:, kd, :].bitcast(F32), ALU.mult, ALU.subtract,
                        *(drain_of(layer, "fht", i) if j else (None, None)))
            if layer == 0:
                split_to(first + 2, stage)
            else:
                dve.wait_ge(sem("moe_loaded"), 48)
                for tb in range(TB):
                    tt(HG[:, tb, :], H_TOK[:, tb, :], R["g_row"][:, :], ALU.mult, sem("h_scaled"), tb + 1)

            tbs = TB if layer == 0 else 1

            def mult(q, parity, width=CHUNK):
                dve.wait_ge(silu_done, q + 1)
                for tb in range(tbs):
                    ins = vec.tensor_tensor(R["act"][:, tb, 0:width], R["silu"][:, tb, 0:width],
                                            PS[tb if layer == 0 else parity][:, width:2 * width], ALU.mult)
                ins.then_inc(act_done, 1)

            def turned_lo(q):
                dve.wait_ge(act_hi_ready, q + 1)
                vec.tensor_tensor(R["act_lo"][:, :, 0:tbs * P],
                                  PS[2][:, 0:2 * tbs * P].rearrange("p (k t) -> p k t", k=2),
                                  R["act_hi"][:, :, 0:tbs * P].bitcast(F32), ALU.subtract).then_inc(act_lo_ready, 1)

            def gather_lo(b):
                for i in range(2):
                    dve.wait_ge(gathered, 4 * b + i + 3)
                    ins = vec.tensor_copy(HTL[:, 4 * i:4 * i + 4, 0:P],
                                          PS[(3, 1)[i]][:, :].rearrange("p (k t) -> p k t", k=4))
                ins.then_inc(g_lo_ready, 1)

            def select(b):
                for tb in range(TB):
                    ins = vec.tensor_scalar(R["psel"][:, tb, :], R["moec"][:, 0:P],
                                            R["pcol"][:, tb, bass.ds(b, 1)], None, ALU.is_equal)
                ins.then_inc(psel_ready, 1)
                vec.tensor_copy(R["wcur"][:, :], R["wcol"][:, :, bass.ds(b, 1)].rearrange("p a b -> p (a b)"))\
                   .then_inc(wcur_ready, 1)

            def y_lo():
                for h in range(2):
                    ins = vec.scalar_tensor_tensor(out=R["y_lo"][:, h * 512:(h + 1) * 512], in0=PS[4 + h][:, :],
                                                   scalar=R["wslot"][:, 0:1],
                                                   in1=R["y_hi"][:, h * 512:(h + 1) * 512].bitcast(F32),
                                                   op0=ALU.mult, op1=ALU.subtract)
                ins.then_inc(y_ready, 1)

            def add_scattered(b):
                for i in range(4):
                    dve.wait_ge(scattered, 4 * b + i + 1)
                    tb, half = i // 2, slice((i % 2) * 512, (i % 2) * 512 + 512)
                    vec.tensor_tensor(X[:, tb, half], X[:, tb, half], PS[(6, 7, 3, 2)[i]][:, :], ALU.add)\
                       .then_inc(scatter_added, 1)

            def ffn_split(p, n0, width=SLAB):
                split(n0 + p, p % FFN_SLABS % RAW_SLOTS, (first + p) % SPLIT_SLOTS, width)

            def ffn_block(b, is_moe):
                n0 = dve.snap(FFN_SLABS * b + first) if is_moe else first
                qb = dve.snap((NCH + 1) * b + Q_FIRST[layer]) if is_moe else Q_FIRST[layer]
                if is_moe:
                    dve.wait_ge(y_hi_ready, b + 1)
                    y_lo()
                    ffn_split(2, n0)
                ffn_split(3, n0)
                mult(qb, 0)
                ffn_split(4, n0)
                if is_moe:
                    add_scattered(b)

                def chunk(p, q, parity, n0, width=SLAB):
                    turned_lo(q - 1)
                    ffn_split(p + 3, n0, width)
                    mult(q, parity)
                    ffn_split(p + 4, n0, width)
                    ffn_split(p + 5, n0, width)

                with dve.Fori(0, 4) as i:
                    n0i, qi = dve.snap(n0 + 6 * i), dve.snap(qb + 2 * i)
                    chunk(2, qi + 1, 1, n0i)
                    chunk(5, qi + 2, 0, n0i)
                if is_moe:
                    dve.wait_ge(pselT_done, b + 1)
                    select(b + 1)
                chunk(26, qb + NCH - 1, 1, n0, 4 * TAIL)
                ffn_split(32, n0, 4 * TAIL)
                turned_lo(qb + NCH - 1)
                ffn_split(33, n0)
                ffn_split(34, n0, D)
                mult(qb + NCH, 0, TAIL)
                ffn_split(35, n0, D)
                if is_moe:
                    ffn_split(FFN_SLABS, n0)
                turned_lo(qb + NCH)
                if is_moe:
                    gather_lo(b + 1)
                    ffn_split(FFN_SLABS + 1, n0)

            if layer == 0:
                ffn_block(0, False)
                dve.wait_ge(slab_used, first + FFN_SLABS)
                for i in range(4):
                    tb, half = i // 2, slice((i % 2) * 512, (i % 2) * 512 + 512)
                    tt(X[:, tb, half], X[:, tb, half], PS[4 + i][:, :], ALU.add,
                       event("ffn_added", 0), i + 1)
                done[0] = FIRST["mix", 1]
            else:
                router(dve, v, tt, ts, stt, lambda: gather_lo(0))
                nb = dve.value_load(R["nbi"][0:1, 0:1], min_val=NE, max_val=NBLK)
                with dve.Fori(0, nb) as b:
                    ffn_block(b, True)
                dve.wait_ge(y_hi_ready, nb + 1)
                y_lo()
                add_scattered(nb)

    @block.tensor
    def _(pe):
        mm = nc.tensor.matmul

        def three(out_, l_hi, l_lo, r_hi, r_lo, start, stop):
            mm(out_, l_hi, r_hi, start=start, stop=False)
            mm(out_, l_hi, r_lo, start=False, stop=False)
            return mm(out_, l_lo, r_hi, start=False, stop=stop)

        def bank_free(layer, step, i):
            b = BANKS[step][i]
            if DRAINS[layer, step, b] > 1:
                pe.wait_ge(drained[b], DRAINS[layer, step, b] - 1)

        def fill(layer, step, i, ins):
            ins.then_inc(filled[BANKS[step][i]], 1)

        def turn(dst, src):
            return nc.tensor.transpose(dst, src, IDENT[:, :])

        def w_parts(n_mod, lo, hi):
            return HI[:, n_mod, lo:hi], LO[:, n_mod, lo:hi]

        def project(layer, step, n, k0, nk, start, stop, turned_w, turned_by=None):
            pe.wait_ge(lo_ready, n + 1)
            s = n % SPLIT_SLOTS
            for k in range(nk):
                kd = k0 + k
                st, sp_ = start and k == 0, stop and k == nk - 1
                if turned_by and kd % 2 == 0:
                    wait_drained(pe, layer, turned_by, kd // 2)
                if turned_w:
                    for m in range(4):
                        w_hi, w_lo = w_parts(s, k * 512 + m * P, k * 512 + (m + 1) * P)
                        ins = three(bank(step, m)[:, 0:T], w_hi, w_lo, HTH[:, kd, :], HTL[:, kd, :], st, sp_)
                else:
                    w_hi, w_lo = w_parts(s, k * 512, (k + 1) * 512)
                    for tb in range(TB):
                        tok = slice(tb * P, (tb + 1) * P)
                        ins = three(bank(step, tb)[:, :], HTH[:, kd, tok], HTL[:, kd, tok], w_hi, w_lo, st, sp_)
            ins.then_inc(slab_used, 1)

        for layer in range(DEPTH):
            first = FIRST["mix", layer]
            if layer:
                pe.wait_ge(act_done, Q_FIRST[layer])
            pe.wait_ge(event("hidden_loaded", layer), 4 * 16)
            for step, banks in PLAN:
                if step in LAST_SLAB:
                    last = first + LAST_SLAB[step]
                    for i in range(len(banks)):
                        bank_free(layer, step, i)
                    if step in ("ph0", "pa0"):
                        for i in range(2):
                            wait_drained(pe, layer, "yT" if step == "ph0" else "yaT", i)
                    if step[:2] in ("ph", "pa"):
                        project(layer, step, last, 4 * (step[:2] == "pa"), 4, True, True, False)
                    else:
                        for part in range(2):
                            project(layer, step, last - 1 + part, 4 * part, 4, part == 0, part == 1,
                                    step in ("v", "x1", "x2"), {"v": "ht", "wo0": "mT"}.get(step))
                    continue
                if step == "f2":
                    pe.wait_ge(event("sin_done", layer), 1)
                elif step[:2] == "hf":
                    pe.wait_ge(event("sin_done", layer), 2)
                    pe.wait_ge(event("par_loaded", layer), 5 * 16)
                    if layer:
                        pe.wait_ge(event("ffn_added", 0), 4)
                elif step[:2] == "ft":
                    pe.wait_ge(event("fpm", layer), 2 * int(step[2]) + 2)
                elif step == "ht":
                    pe.wait_ge(event("h_ready", layer), TB)
                    if layer == 0:
                        pe.wait_ge(sem("cst_loaded"), 3 * 16)
                elif step in ("vT", "x1T", "x2T"):
                    pe.wait_ge(event("conv_done", layer), {"vT": 4, "x1T": 8, "x2T": 12}[step])
                elif step == "cf0":
                    for tb in range(TB):
                        wait_drained(pe, layer, "vT", tb)
                elif step == "cf1":
                    for tb in range(TB):
                        wait_drained(pe, layer, "ci0", tb)
                elif step[:2] == "ci":
                    pe.wait_ge(event("ys_ready", layer), 2 * int(step[2]) + 2)
                elif step in ("qT", "kT"):
                    pe.wait_ge(event(f"{step[0]}_roped", layer), TB)
                elif step == "sc0":
                    for i in range(2):
                        wait_drained(pe, layer, "qT", i)
                        wait_drained(pe, layer, "kT", i)
                elif step[:2] == "aT":
                    pe.wait_ge(event("a_ready", layer), 2 * int(step[2]) + 2)
                elif step[:2] == "av":
                    wait_drained(pe, layer, f"aT{step[2]}", 0)
                    for tb in range(TB):
                        wait_drained(pe, layer, "av", tb)
                elif step == "yT":
                    for tb in range(TB):
                        wait_drained(pe, layer, "ci1", tb)
                elif step == "yaT":
                    wait_drained(pe, layer, "av3", 0)
                elif step == "fht":
                    pe.wait_ge(event("hf_ready", layer), TB)
                for i in range(len(banks)):
                    bank_free(layer, step, i)
                    if step == "mT":
                        pe.wait_ge(event("merged", layer), 2 + i // 2 * 2)
                    dst = bank(step, i)
                    if step == "f1":
                        ins = mm(dst[0:FH, 0:T], R["wf1"][:, :], R["zT"][:, :], start=True, stop=True)
                    elif step == "f2":
                        ins = mm(dst[0:FH, 0:T], R["wf2"][:, :], R["hdn"][:, 0, :], start=True, stop=True)
                    elif step[:2] == "hf":
                        jt, part = i // 2, 2 * int(step[2]) + i % 2
                        ins = mm(dst[:, :], R["hdn"][:, 1, jt * P:(jt + 1) * P],
                                 R["wf3"][:, part * HW:(part + 1) * HW], start=True, stop=True)
                    elif step[:2] in ("ft", "cf"):
                        kt, ri = i // 2, i % 2
                        for jt in range(2):
                            src = R["fpm"][:, jt, ri, :] if step[:2] == "ft" else XV[:, 0 if step == "cf1" else 2, jt, :]
                            ins = mm(dst[:, :], DFT[:, ri, jt, kt * P:(kt + 1) * P], src, start=jt == 0, stop=jt == 1)
                    elif step[:2] == "ci":
                        for k in range(4):
                            kt, ri = k // 2, k % 2
                            ins = mm(dst[:, :], DFT[:, 2 + ri, kt, i * P:(i + 1) * P], YS[:, kt, ri, :],
                                     start=k == 0, stop=k == 3)
                    elif step in ("ht", "fht", "mT"):
                        for j in range(4):
                            kd, tb = 2 * i + j // 2, j % 2
                            col = slice(kd * P, (kd + 1) * P)
                            src = GATES[:, tb, 0, col] if step == "mT" else H_TOK[:, tb, col]
                            ins = turn(dst[:, j * P:(j + 1) * P], src)
                    elif step in ("vT", "x1T", "x2T"):
                        c = ("vT", "x1T", "x2T").index(step)
                        for j in range(4):
                            ins = turn(dst[:, j * P:(j + 1) * P], CONV[:, c % 2, j, i * P:(i + 1) * P])
                    elif step in ("qT", "kT", "yT", "yaT"):
                        for j in range(4):
                            t, tb = 2 * i + j // 2, j % 2
                            col = slice(t * P, (t + 1) * P)
                            src = XV[:, 1, tb, col] if step == "yT" else \
                                QKV[:, {"qT": 0, "kT": 1, "yaT": 2}[step], tb, col]
                            ins = turn(dst[:, j * P:(j + 1) * P], src)
                    elif step[:2] == "sc":
                        h = int(step[2])
                        d = slice(i * DH, (i + 1) * DH)
                        for tb in range(TB):
                            ins = mm(dst[:, tb * T:(tb + 1) * T], QT[d, h, tb * P:(tb + 1) * P], KT[d, h, :],
                                     start=True, stop=True)
                    elif step[:2] == "aT":
                        for j in range(4):
                            kt, tb = j // 2, j % 2
                            ins = turn(dst[:, j * P:(j + 1) * P], R["a"][:, tb, kt * P:(kt + 1) * P])
                    elif step[:2] == "av":
                        h = int(step[2])
                        for j in range(4):
                            tb, kt = j // 2, j % 2
                            ins = mm(dst[:, tb * DV:(tb + 1) * DV], R["aT"][:, kt, tb * P:(tb + 1) * P],
                                     QKV[:, 2, kt, h * DV:(h + 1) * DV], start=kt == 0, stop=kt == 1)
                    fill(layer, step, i, ins)

            first = FIRST["ffn", layer]
            if layer == 1:
                bank_free(1, "rt", 0)
                pe.wait_ge(sem("wr_hi_ready"), 1)
                for i in range(4):
                    wait_drained(pe, layer, "fht", i)
                for tb in range(TB):
                    tok = slice(tb * P, (tb + 1) * P)
                    for kd in range(KD):
                        ins = three(bank("rt", 0)[:, tb * NE:(tb + 1) * NE], HTH[:, kd, tok], HTL[:, kd, tok],
                                    R["wr_hi"][:, kd, :], R["wr_lo"][:, kd, :], kd == 0, kd == KD - 1)
                fill(1, "rt", 0, ins)
                pe.wait_ge(sem("sel_ready"), 1)
                bank_free(1, "pos", 0)
                tri, ones = R["moec"][:, P:2 * P], R["moec"][:, 2 * P:3 * P]
                for i, terms in enumerate((((tri, 0),), ((ones, 0), (tri, 1)), ((ones, 0), (ones, 1)))):
                    for k, (m, tb) in enumerate(terms):
                        ins = mm(bank("pos", 0)[:, i * NE:(i + 1) * NE], m, R["sel"][:, tb, :],
                                 start=k == 0, stop=k == len(terms) - 1)
                fill(1, "pos", 0, ins)

            tbs = TB if layer == 0 else 1

            def gate_up(n, s, k0, nk, width, q, parity, turned_by=None):
                pe.wait_ge(lo_ready, n + 1)
                if k0 == 0 and not (isinstance(q, int) and q == 0):
                    pe.wait_ge(act_done, q)
                for k in range(nk):
                    kd = k0 + k
                    if turned_by and kd % 2 == 0:
                        wait_drained(pe, layer, turned_by, kd // 2)
                    w_hi, w_lo = w_parts(s, k * 2 * width, (k + 1) * 2 * width)
                    for tb in range(tbs):
                        tok = slice(tb * P, (tb + 1) * P)
                        ins = three(PS[tb if layer == 0 else parity][:, 0:2 * width], HTH[:, kd, tok],
                                    HTL[:, kd, tok], w_hi, w_lo, kd == 0, kd == KD - 1)
                ins.then_inc(slab_used, 1)

            def turn_act(q, width=CHUNK):
                pe.wait_ge(act_done, q + 1)
                for k in range(2):
                    h = min(P, width - k * P)
                    for tb in range(tbs):
                        at = (k * tbs + tb) * P
                        ins = turn(PS[2][0:h, at:at + P], R["act"][:, tb, k * P:k * P + h])
                ins.then_inc(turned, 1)

            def down(n, s, q, start, stop=False, tiles=((0, P), (1, P))):
                pe.wait_ge(lo_ready, n + 1)
                pe.wait_ge(act_lo_ready, q + 1)
                for j, (k, h) in enumerate(tiles):
                    for tb in range(tbs):
                        tok = slice(tb * P, (tb + 1) * P)
                        for half in range(2):
                            at = j * D + half * 512
                            ins = three(PS[4 + 2 * tb + half][:, :], R["act_hi"][0:h, k, tok], R["act_lo"][0:h, k, tok],
                                        HI[0:h, s, at:at + 512], LO[0:h, s, at:at + 512],
                                        start and k == 0, stop and k == 1)
                ins.then_inc(slab_used, 1)

            def gather(b):
                pe.wait_ge(psel_ready, b + 1)
                for i, (src, bk) in enumerate(((R["hg_hi"], 6), (R["hg_hi"], 7), (R["hg_lo"], 3), (R["hg_lo"], 1))):
                    if isinstance(b, int):
                        pe.wait_ge(sem("hg_hi_ready") if i < 2 else sem("hg_lo_ready"), 1)
                    for k in range(4):
                        kd = 4 * (i % 2) + k
                        for tb in range(TB):
                            ins = mm(PS[bk][:, k * P:(k + 1) * P], src[:, tb, kd * P:(kd + 1) * P],
                                     R["psel"][:, tb, :], start=tb == 0, stop=tb == 1)
                    ins.then_inc(gathered, 1)

            def scatter(b):
                pe.wait_ge(y_ready, b + 1)
                for i, bk in enumerate((6, 7, 3, 2)):
                    tb, cols = i // 2, slice((i % 2) * 512, (i % 2) * 512 + 512)
                    mm(PS[bk][:, :], R["pselT"][:, tb, :], R["y_hi"][:, cols], start=True, stop=False)
                    mm(PS[bk][:, :], R["pselT"][:, tb, :], R["y_lo"][:, cols], start=False, stop=True)\
                        .then_inc(scattered, 1)

            def ffn_block(b, is_moe):
                n0 = pe.snap(FFN_SLABS * b + first) if is_moe else first
                qb = pe.snap((NCH + 1) * b + Q_FIRST[layer]) if is_moe else Q_FIRST[layer]

                def slot(p):
                    return (first + p) % SPLIT_SLOTS
                if is_moe:
                    pe.wait_ge(g_hi_ready, b + 1)
                    pe.wait_ge(g_lo_ready, b + 1)
                for part in range(2):
                    gate_up(n0 + part, slot(part), 4 * part, 4, CHUNK, qb, 0, None if is_moe else "fht")
                if is_moe:
                    scatter(b)
                    pe.wait_ge(scatter_added, 4 * b + 4)

                def pair(n0, qb, start):
                    for j in range(2):
                        p, q = 2 + 3 * j, qb + 1 + j
                        gate_up(n0 + p, slot(p), 0, 4, CHUNK, q, 1 - j)
                        turn_act(q - 1)
                        gate_up(n0 + p + 1, slot(p + 1), 4, 4, CHUNK, q, 1 - j)
                        down(n0 + p + 2, slot(p + 2), q - 1, start and j == 0)

                pair(n0, qb, True)
                with pe.Fori(1, 4) as i:
                    pair(pe.snap(n0 + 6 * i), pe.snap(qb + 2 * i), False)
                if is_moe:
                    pe.wait_ge(wcur_ready, b + 1)
                    for tb in range(TB):
                        turn(PS[3][:, tb * P:(tb + 1) * P], R["psel"][:, tb, :].bitcast(F32))
                    for tb in range(TB):
                        ins = mm(PS[3][:, 2 * P:2 * P + 1], R["psel"][:, tb, :].bitcast(F32), R["wcur"][:, tb:tb + 1],
                                 start=tb == 0, stop=tb == 1)
                    ins.then_inc(pselT_done, 1)
                q = qb + NCH - 1
                gate_up(n0 + 26, slot(26), 0, 4, CHUNK, q, 1)
                turn_act(q - 1)
                gate_up(n0 + 27, slot(27), 4, 4, CHUNK, q, 1)
                down(n0 + 28, slot(28), q - 1, False)
                gate_up(n0 + 29, slot(29), 0, 2, TAIL, q + 1, 0)
                turn_act(q)
                for part in range(1, 4):
                    gate_up(n0 + 29 + part, slot(29 + part), 2 * part, 2, TAIL, q + 1, 0)
                down(n0 + 33, slot(33), q, False)
                turn_act(q + 1, TAIL)
                if is_moe:
                    pe.wait_ge(pselT_ready, b + 1)
                    gather(b + 1)
                down(n0 + 34, slot(34), q + 1, False, tiles=((0, P),))
                down(n0 + 35, slot(35), q + 1, False, True, tiles=((1, TAIL - P),))

            if layer == 0:
                ffn_block(0, False)
            else:
                pe.wait_ge(psel_ready, 1)
                for half in range(2):
                    mm(PS[4 + half][:, :], R["pselT"][:, 0, :], HTH[:, 2 * half:2 * half + 2, :].rearrange("p a b -> p (a b)"),
                       start=True, stop=True)
                gather(0)
                pe.wait_ge(sem("blocks_known"), 1)
                nb = pe.value_load(R["nbi"][0:1, 0:1], min_val=NE, max_val=NBLK)
                with pe.Fori(0, nb) as b:
                    ffn_block(b, True)
                scatter(nb)

    ctx.close()


def constants():
    f = np.float32
    k = np.arange(T)
    angle = 2 * np.pi * np.outer(np.arange(T), k + 0.5) / (2 * T)
    tables = np.stack([np.cos(angle), np.sin(angle), np.cos(angle).T, np.sin(angle).T])
    dft = tables.reshape(4, 2, P, T).transpose(2, 0, 1, 3).reshape(P, 4 * 2 * T).astype(f)
    inv = (f(1.0) / (f(10000.0) ** (np.arange(0, DH, 2, dtype=f) / f(DH)))).astype(f)
    ang = np.arange(T, dtype=f)[:, None] * inv[None, :]
    rope = np.stack([np.cos(ang), np.sin(ang)]).astype(f).reshape(2, TB, P, DH // 2)
    cst = np.concatenate([np.eye(P, dtype=f), rope.transpose(2, 0, 1, 3).reshape(P, P)], axis=1)
    t = np.linspace(0.0, 1.0, T, dtype=f)[:, None]
    w = (f(2.0 * np.pi) * np.arange(T, dtype=f)[:, None] / f(T)).astype(f)
    bands = (FE - 1) // 2
    fr = np.linspace(1e-4, bands - 1, bands, dtype=f)[None, :]
    z = np.concatenate([t, np.cos(fr * w), -np.sin(fr * w)], axis=-1).astype(f)
    deltas = np.linspace(np.log(1e-2) / 1.5, np.log(1e-2) / 0.3, HW).astype(f)
    decay = np.exp(-t * np.abs(deltas)[None, :]).astype(f)
    both = np.stack([decay, decay])
    both[1, 0] = 0
    both = both.reshape(2, 2, P, HW).transpose(2, 1, 0, 3).reshape(P, 4 * HW)
    moec = np.zeros((P, 3 * P + 64 + 8 + 4), f)
    moec[:, 0:P] = np.arange(P)
    moec[:, P:2 * P] = np.triu(np.ones((P, P)), 1)
    moec[:, 2 * P:3 * P] = 1
    moec[:, 3 * P:3 * P + 64] = np.tril(np.ones((NE, NE)), -1).reshape(1, 64)
    moec[:, 3 * P + 64:3 * P + 72] = np.arange(NE)
    return {"cst": cst, "dft": dft, "decay": both, "zt": z.T, "moec": moec}


STREAMED = ["w_in", "w_hy_o", "w_at_o", "w_out", "w_dense_gate", "w_dense_up", "w_dense_down",
            "w_moe_gate", "w_moe_up", "w_moe_down"]


def kernel(**inputs):
    import concourse.bacc as bacc
    from concourse.bass_utils import run_bass_kernel_spmd

    a = {k: np.asarray(v) for k, v in inputs.items()}
    par = np.zeros((DEPTH, P, PAR_N), np.float32)
    for layer in range(DEPTH):
        par[layer, :, PAR_CONV:PAR_GM] = a["conv_w"][layer].reshape(3, 12, P).transpose(2, 1, 0).reshape(P, 36)
        par[layer, :, PAR_GM:PAR_GF] = a["norm_mix"][layer].reshape(KD, P).T
        par[layer, :, PAR_GF:PAR_QN] = a["norm_ffn"][layer].reshape(KD, P).T
        par[layer, :, PAR_QN:PAR_KN] = a["q_norm"][layer]
        par[layer, :, PAR_KN:PAR_SUB] = a["k_norm"][layer]
        par[layer, :, PAR_SUB:PAR_N] = a["subln_g"][layer]
    ins = dict(
        x=a["x"][0], par=par,
        lamv=np.concatenate([a["lam_q1"], a["lam_k1"], a["lam_q2"], a["lam_k2"]], axis=1),
        wf1=a["w_f1"], wf2=a["w_f2"],
        bf=np.stack([a["b_f1"], a["freq1"], a["b_f2"], a["freq2"]], axis=2),
        wf3=a["w_f3"], hyb=a["hy_bias"].reshape(DEPTH, 2 * HW), nffn=a["norm_ffn"][1:2], wr=a["w_router"][0],
        **constants())
    ins.update({k: a[k] for k in STREAMED if "moe" not in k})
    ins.update({k: a[k][0] for k in STREAMED if "moe" in k})

    nc = bacc.Bacc("TRN2", target_bir_lowering=False, num_devices=1)
    arrays, aps = {}, {}
    for name, value in ins.items():
        value = np.ascontiguousarray(value)
        arrays[f"in_{name}"] = value
        aps[name] = nc.dram_tensor(f"in_{name}", value.shape, mybir.dt.from_np(value.dtype), kind="ExternalInput").ap()
    out = nc.dram_tensor("out_x", (T, D), F32, kind="ExternalOutput").ap()
    trunk(nc, aps["x"], {k: aps[k] for k in STREAMED}, aps["par"], aps["lamv"], aps["wf1"], aps["wf2"], aps["bf"],
          aps["wf3"], aps["hyb"], aps["nffn"], aps["wr"], aps["cst"], aps["dft"], aps["decay"], aps["zt"],
          aps["moec"], out)
    result = run_bass_kernel_spmd(nc, [arrays], core_ids=[0])
    return result.results[0]["out_x"].reshape(1, T, D)
```

```python
from contextlib import ExitStack

import numpy as np

import concourse.bass as bass
from concourse import mybir

ALU = mybir.AluOpType
ACT = mybir.ActivationFunctionType
AX_X = mybir.AxisListType.X
F32 = mybir.dt.float32
F32R = mybir.dt.float32r
I32 = mybir.dt.int32

P = 128
D = 1024
T = 256
TB = T // P
DEPTH = 2
HW = D // 2
KD = D // P
NH, DH, DV = 4, 64, 128
FE, FH = 33, 64
FF = 2752
NE, TOPK = 8, 2
EPS = 1e-6

SLAB = 2048
RAW_SLOTS, SPLIT_SLOTS = 6, 3
CHUNK = 256
NCH = FF // CHUNK
TAIL = FF - NCH * CHUNK
MIX_SLABS = 28
FFN_SLABS = 36
XTRA = (T * TOPK) // (P + 1)
NBLK = NE + XTRA

FIRST = {("mix", 0): 0, ("ffn", 0): MIX_SLABS, ("mix", 1): MIX_SLABS + FFN_SLABS,
         ("ffn", 1): 2 * MIX_SLABS + FFN_SLABS}
STAGES = [("mix", 0), ("ffn", 0), ("mix", 1), ("ffn", 1)]
LENGTH = {"mix": MIX_SLABS, "ffn": FFN_SLABS}


def raw_place(stage, p):
    return p + (RAW_SLOTS - MIX_SLABS % RAW_SLOTS if stage[0] == "mix" else 0)


def raw_slot(stage, p):
    return raw_place(stage, p) % RAW_SLOTS


def width_of(stage, p):
    return 4 * CHUNK if stage[0] == "ffn" and p < 4 else SLAB


def uses_before(stage):
    total = [0] * RAW_SLOTS
    for s in STAGES[:STAGES.index(stage)]:
        for p in range(LENGTH[s[0]]):
            total[raw_slot(s, p)] += 1
    return total


def raw_value(stage, p):
    before = sum(raw_slot(stage, q) == raw_slot(stage, p) for q in range(p))
    return 32 * (uses_before(stage)[raw_slot(stage, p)] + before + 1)


def back(stage, p):
    every = [(s, q) for s in STAGES[:3] + [("ffn", 1)] for q in range(LENGTH[s[0]])]
    n = every.index((stage, p))
    return next((b for b in range(1, n + 1) if raw_slot(*every[n - b]) == raw_slot(stage, p)), None)


CHUNKS = ["v", "x1", "q", "x2", "k", "av", "g0", "g1", "g2", "g3"]
COLUMN = {"x1": 0, "x2": 512, "v": 1024, "q": 1536, "k": 2048, "av": 2560,
          "g0": 3072, "g1": 3584, "g2": 4096, "g3": 4608}

PLAN = [("hf0", [0, 1, 2, 3]), ("ht", [4, 5, 6, 7]), ("ft0", [0, 1, 2, 3]),
        ("v", [4, 5, 6, 7]), ("hf1", [0, 1, 2, 3]), ("x1", [4, 5, 6, 7]), ("ft1", [0, 1, 2, 3]),
        ("q", [4, 5]), ("vT", [6, 7]), ("x2", [0, 1, 2, 3]),
        ("k", [4, 5]), ("x1T", [6, 7]), ("av", [0, 1]), ("x2T", [2, 3]),
        ("cf0", [4, 5, 6, 7]), ("g0", [0, 1]), ("qT", [2, 3]), ("g1", [0, 1]), ("kT", [2, 3]),
        ("ci0", [4, 5]), ("sc0", [6, 7]), ("g2", [0, 1]), ("aT0", [2]), ("sc1", [6, 7]), ("av0", [3]),
        ("cf1", [0, 1, 4, 5]), ("aT1", [2]), ("sc2", [6, 7]), ("av1", [3]), ("g3", [0, 1]),
        ("aT2", [2]), ("sc3", [6, 7]), ("av2", [3]), ("ci1", [4, 5]), ("aT3", [2]), ("yT", [0, 1]),
        ("av3", [3]), ("ph0", [4, 5]), ("yaT", [6, 7]), ("ph1", [0, 1]), ("pa0", [2, 3]), ("pa1", [4, 5]),
        ("mT", [6, 7, 0, 1]), ("wo0", [2, 3]), ("wo1", [4, 5]), ("fht", [6, 7, 2, 3])]
PLAN_MOE = [("rt", [0]), ("pos", [1])]
NEXT_HIDDEN = {"mT": ("n1", [4]), "wo1": ("n2", [6])}


def plan(layer):
    steps = [("f1", [0]), ("f2", [1])] if layer == 0 else []
    for step in PLAN:
        if layer + 1 < DEPTH and step[0] in NEXT_HIDDEN:
            steps.append(NEXT_HIDDEN[step[0]])
        steps.append(step)
    return steps + (PLAN_MOE if layer == 1 else [])


BANKS = dict(plan(0) + plan(1))

LAST_SLAB = {}
for _i, _c in enumerate(CHUNKS):
    LAST_SLAB[_c] = 2 * _i + 1
LAST_SLAB.update({"ph0": 20, "ph1": 21, "pa0": 22, "pa1": 23, "wo0": 25, "wo1": 27})


def turns(counted):
    count, out = [0] * 8, {}
    for layer in range(DEPTH):
        for step, banks in plan(layer):
            for b in banks:
                count[b] += int(counted(step))
                out[layer, step, b] = count[b]
    return out


FILLS = turns(lambda step: step not in LAST_SLAB)
DRAINS = turns(lambda step: 1)

ROUND = 12582912.0
TWO_PI = (6.28125, 0.0019350051879882812, 3.019916050561733e-07)
PI_BELOW = 3.1415925

Q_FIRST = [0, NCH + 1]
LAMBDA_INIT = [0.8 - 0.6 * float(np.exp(-0.3 * layer)) for layer in range(DEPTH)]

PAR_CONV, PAR_GM, PAR_GF, PAR_QN, PAR_KN, PAR_SUB = 0, 36, 44, 52, 116, 180
PAR_N = PAR_SUB + DV


def trunk(nc, x_in, slabs, par_d, lamv_d, wf1_d, wf2_d, bf_d, wf3_d, hyb_d, nffn_d, wr_d,
          cst_d, dft_d, decay_d, zt_d, moec_d, out):
    ctx = ExitStack()

    def sb(name, shape, dt=F32):
        return ctx.enter_context(nc.sbuf_tensor(name, shape, dt))

    def region(name, floats, variants):
        found = {}
        for variant in variants:
            inner = ExitStack()
            for n, shape, dt in variant:
                found[n] = inner.enter_context(nc.sbuf_tensor(n, shape, dt))
            assert sum(int(np.prod(s[1:])) for _, s, _ in variant) <= floats, name
            inner.close()
        sb(name, [P, floats])
        return found

    semaphores = {}

    def sem(name):
        if name not in semaphores:
            semaphores[name] = ctx.enter_context(nc.semaphore(name))
        return semaphores[name]

    RAW = sb("raw", [P, RAW_SLOTS, SLAB])
    HI = sb("w_hi", [P, SPLIT_SLOTS, SLAB], F32R)
    LO = sb("w_lo", [P, SPLIT_SLOTS, SLAB], F32R)
    X = sb("x", [P, TB, D])
    HTH = sb("hT_hi", [P, KD, T], F32R)
    HTL = sb("hT_lo", [P, KD, T], F32R)
    TMP = sb("tmp", [P, 1024])
    IDENT = sb("ident", [P, P])
    ROPE = sb("rope", [P, 2, TB, 32])
    PAR = sb("par", [P, PAR_N])
    STAT = sb("stat", [P, 96])
    LAM = sb("lam", [P, 8])
    HALF = sb("minus_half", [P, 16])
    DIAG = TMP[:, 256:512].rearrange("p (t q) -> p t q", t=TB)
    SQUARES = sb("squares", [P, DV])
    R = {}
    R.update(region("r_h", 2 * 4 * 258, [[("x_squared", [P, TB, D], F32)], [("upad", [P, 2, 4, 258], F32)],
                                         [("qT", [P, NH, T], F32), ("kT", [P, NH, T], F32)]]))
    R.update(region("r_conv", 2048, [[("conv", [P, 2, 4, T], F32)], [("ys", [P, 2, 2, 512], F32)],
                                     [("act_hi", [P, 2, T], F32R), ("act_lo", [P, 2, T], F32R),
                                      ("silu", [P, TB, CHUNK], F32), ("act", [P, TB, CHUNK], F32)]]))
    late = [("g_row", [P, D], F32), ("moec", [P, 3 * P + 64 + 8 + 4], F32),
            ("wr", [P, KD, NE], F32), ("wr_hi", [P, KD, NE], F32R), ("wr_lo", [P, KD, NE], F32R),
            ("lg", [P, TB, NE], F32), ("cmp", [P, TB, NE, NE], F32), ("cmp2", [P, TB, NE, NE], F32),
            ("rank", [P, TB, NE], F32), ("sel1", [P, TB, NE], F32), ("sel2", [P, TB, NE], F32),
            ("sel", [P, TB, NE], F32), ("wts", [P, TB, NE], F32), ("posm", [P, TB, NE], F32),
            ("cnt", [P, NE], F32), ("over", [P, NE], F32), ("oh", [P, 4, NE], F32),
            ("pcol", [P, TB, NBLK + 1], F32), ("wcol", [P, TB, NBLK + 1], F32), ("tv", [P, 8, TB], F32),
            ("nbf", [P, 16], F32), ("nbi", [P, 16], I32), ("nbe", [P, 16], I32), ("wcur", [P, TB], F32), ("wslot", [P, 1], F32),
            ("prod", [P, 4, NE], F32)]
    R.update(region("r_gate", 4096, [[("decay", [P, 2, 2, 512], F32), ("fpm", [P, 2, 2, 512], F32)],
                                     [("gates", [P, TB, 2, D], F32)],
                                     [("hg_hi", [P, TB, D], F32R), ("hg_lo", [P, TB, D], F32R)]]))
    R.update(region("r_xv", 3072, [[("fb", [P, 2, 512], F32), ("zT", [FE, T], F32), ("wf1", [FE, FH], F32),
                                    ("wf2", [FH, FH], F32), ("bf", [FH, 4], F32), ("lamv", [P, 4, DH], F32),
                                    ("arg", [FH, T], F32), ("rnd", [FH, T], F32), ("hdn", [FH, 2, T], F32)],
                                   [("xv", [P, 3, TB, HW], F32)],
                                   [("y_hi", [P, D], F32R), ("y_lo", [P, D], F32R),
                                    ("psel", [P, TB, P], F32R), ("pselT", [P, TB, P], F32R)]]))
    R.update(region("r_qkv", 3072, [[("wf3", [FH, 2048], F32), ("hyb", [1, 1024], F32)],
                                    [("qkv", [P, 3, TB, 512], F32)],
                                    [("e", [P, 2, 2, T], F32), ("a", [P, 2, T], F32), ("aT", [P, 2, T], F32)],
                                    late]))
    FSP = sb("filters", [P, 2, 2, 2, 512])
    HG = FSP[:, 0].rearrange("p a b c -> p a (b c)")
    DFT = sb("dft", [P, 2, 2, TB, P])
    X_SQUARED, UPAD, QT, KT = R["x_squared"], R["upad"], R["qT"], R["kT"]
    CONV, YS = R["conv"], R["ys"]
    XV, QKV, GATES = R["xv"], R["qkv"], R["gates"]
    PS = [ctx.enter_context(nc.psum_tensor(f"bank{b}", [P, 512], F32)) for b in range(8)]

    SCATTER_BANKS = (2, 6, 7, 3)

    raw_loaded = [sem(f"raw_loaded{s}") for s in range(RAW_SLOTS)]
    hi_ready, lo_ready, slab_used = sem("hi_ready"), sem("lo_ready"), sem("slab_used")
    filled = [sem(f"bank_filled{b}") for b in range(8)]
    drained = [sem(f"bank_drained{b}") for b in range(8)]
    silu_done, act_done = sem("silu_done"), sem("act_done")
    turned, act_hi_ready, act_lo_ready = sem("act_turned"), sem("act_hi_ready"), sem("act_lo_ready")
    y_hi_ready, y_ready = sem("y_hi_ready"), sem("y_ready")
    gathered, g_hi_ready, g_lo_ready = sem("gathered"), sem("g_hi_ready"), sem("g_lo_ready")
    wcur_ready = sem("wcur_ready")
    psel_ready, pselT_done, pselT_ready = sem("psel_ready"), sem("pselT_done"), sem("pselT_ready")
    scattered, scatter_added = sem("scattered"), sem("scatter_added")

    class Steps:

        def __init__(self, eng, name):
            self.eng, self.own, self.count, self.last = eng, sem(name), 0, None

        def do(self, ins, signal=None, value=None):
            if signal is None:
                self.count += 1
                signal, value = self.own, self.count
            ins.then_inc(signal, 1)
            self.last = (signal, value)

        def settle(self):
            if self.last is not None:
                self.eng.wait_ge(*self.last)

    def event(name, layer):
        return sem(f"{name}_{layer}")

    def wait_filled(eng, layer, step, i):
        b = BANKS[step][i]
        if step in LAST_SLAB:
            eng.wait_ge(slab_used, FIRST["mix", layer] + LAST_SLAB[step] + 1)
        else:
            eng.wait_ge(filled[b], FILLS[layer, step, b])

    def bank(step, i):
        return PS[BANKS[step][i]]

    def drain_of(layer, step, i):
        b = BANKS[step][i]
        return drained[b], DRAINS[layer, step, b]

    def wait_drained(eng, layer, step, i):
        eng.wait_ge(*drain_of(layer, step, i))

    S_MAX, S_NEG, S_SUM, S_FAC = (STAT[:, 64 + 4 * i:68 + 4 * i] for i in range(4))

    def router(dve, v, tt, ts, stt, gather_lo):
        vec = nc.vector
        lg, cmp, cmp2, rank = R["lg"], R["cmp"], R["cmp2"], R["rank"]
        sel1, sel2, sel, wts, posm, tv = (R[k] for k in ("sel1", "sel2", "sel", "wts", "posm", "tv"))
        over, oh, prod, nbf = R["over"], R["oh"], R["prod"], R["nbf"]
        tril = R["moec"][:, 3 * P:3 * P + 64].rearrange("p (a b) -> p a b", a=NE)
        erow = R["moec"][:, 3 * P + 64:3 * P + 72]

        def flat(ap):
            return ap.rearrange("p a b -> p (a b)")

        def reduce(dst, src, signal=None, value=None):
            v.do(vec.tensor_reduce(dst, src, AX_X, ALU.add), signal, value)

        v.do(vec.memset(R["wslot"][:, :], 0.0))
        v.do(vec.memset(R["pselT"][:, :, :].bitcast(F32), 0.0))
        v.do(vec.memset(R["pcol"][:, :, NBLK:NBLK + 1], -1.0))
        v.do(vec.memset(R["wcol"][:, :, NBLK:NBLK + 1], 0.0))
        v.do(vec.memset(nbf[:, :], 0.0))
        wait_filled(dve, 1, "rt", 0)
        v.do(vec.tensor_copy(flat(lg[:, :, :]), bank("rt", 0)[:, 0:TB * NE]), *drain_of(1, "rt", 0))
        v.settle()
        other = lg[:, :, :].unsqueeze(2).broadcast_to([P, TB, NE, NE])
        own = lg[:, :, :].unsqueeze(3).broadcast_to([P, TB, NE, NE])
        tt(cmp[:, :, :, :], other, own, ALU.is_gt)
        tt(cmp2[:, :, :, :], other, own, ALU.is_equal)
        v.settle()
        for tb in range(TB):
            tt(cmp2[:, tb, :, :], cmp2[:, tb, :, :], tril, ALU.mult)
        v.settle()
        tt(cmp[:, :, :, :], cmp[:, :, :, :], cmp2[:, :, :, :], ALU.add)
        v.settle()
        reduce(flat(rank[:, :, :]), cmp[:, :, :, :].rearrange("p t a b -> p (t a) b"))
        v.settle()
        ts(sel1[:, :, :], rank[:, :, :], 0.0, None, ALU.is_equal)
        ts(sel2[:, :, :], rank[:, :, :], 1.0, None, ALU.is_equal)
        v.settle()
        tt(sel[:, :, :], sel1[:, :, :], sel2[:, :, :], ALU.add, sem("sel_ready"), 1)
        tt(cmp[:, :, 0, :], sel1[:, :, :], lg[:, :, :], ALU.mult)
        tt(cmp[:, :, 1, :], sel2[:, :, :], lg[:, :, :], ALU.mult)
        v.settle()
        reduce(tv[:, 0, :], cmp[:, :, 0, :])
        reduce(tv[:, 1, :], cmp[:, :, 1, :])
        v.settle()
        tt(tv[:, 2, :], tv[:, 1, :], tv[:, 0, :], ALU.subtract, sem("top_diff"), 1)
        wait_filled(dve, 1, "pos", 0)
        stt(flat(posm[:, :, :]), bank("pos", 0)[:, 0:TB * NE], 1.0, flat(sel[:, :, :]), ALU.add, ALU.mult)
        ts(over[:, :], bank("pos", 0)[:, TB * NE:(TB + 1) * NE], float(P), None, ALU.is_gt, None,
           *drain_of(1, "pos", 0))
        v.settle()
        ts(posm[:, :, :], posm[:, :, :], -1.0, None, ALU.add)
        reduce(nbf[:, 0:1], over[:, :])
        v.settle()
        for tb in range(TB):
            ts(R["psel"][:, tb, :], R["moec"][:, 0:P], posm[:, tb, 0:1], None, ALU.is_equal, None,
               *((psel_ready, 1) if tb == 1 else (None, None)))
        ts(nbf[:, 0:1], nbf[:, 0:1], float(NE), None, ALU.add)
        v.settle()
        v.do(vec.tensor_copy(R["nbi"][:, :], nbf[:, :]), sem("blocks_known"), 1)
        dve.wait_ge(sem("hg_hi_ready"), 1)
        tt(R["hg_lo"][:, :, :], HG, R["hg_hi"][:, :, :].bitcast(F32), ALU.subtract, sem("hg_lo_ready"), 1)
        dve.wait_ge(sem("top_exp"), 1)
        ts(tv[:, 4, :], tv[:, 3, :], 1.0, None, ALU.add)
        v.settle()
        v.do(vec.reciprocal(tv[:, 5, :], tv[:, 4, :]))
        v.settle()
        tt(tv[:, 6, :], tv[:, 3, :], tv[:, 5, :], ALU.mult)
        v.settle()
        for tb in range(TB):
            ts(wts[:, tb, :], sel1[:, tb, :], tv[:, 5, tb:tb + 1], None, ALU.mult)
        v.settle()
        for tb in range(TB):
            stt(wts[:, tb, :], sel2[:, tb, :], tv[:, 6, tb:tb + 1], wts[:, tb, :], ALU.mult, ALU.add)
        v.settle()
        v.do(vec.tensor_copy(R["wcur"][:, :].unsqueeze(2), wts[:, :, 0:1]), wcur_ready, 1)
        gather_lo()
        tt(cmp[:, 0, :, :], over[:, :].unsqueeze(1).broadcast_to([P, NE, NE]), tril, ALU.mult)
        v.settle()
        reduce(R["cnt"][:, :], cmp[:, 0, :, :])
        v.settle()
        for j in range(XTRA):
            stt(oh[:, j, :], R["cnt"][:, :], float(j), over[:, :], ALU.is_equal, ALU.mult)
        v.settle()
        for tb in range(TB):
            v.do(vec.tensor_copy(R["pcol"][:, tb, 0:NE], posm[:, tb, :]))
            v.do(vec.tensor_copy(R["wcol"][:, tb, 0:NE], wts[:, tb, :]))
            for src, dst in ((posm, R["pcol"]), (wts, R["wcol"])):
                tt(prod[:, 0:XTRA, :], oh[:, 0:XTRA, :], src[:, tb, :].unsqueeze(1).broadcast_to([P, XTRA, NE]),
                   ALU.mult)
                v.settle()
                reduce(dst[:, tb, NE:NBLK], prod[:, 0:XTRA, :])
                v.settle()
            ts(R["pcol"][:, tb, NE:NBLK], R["pcol"][:, tb, NE:NBLK], -float(P), None, ALU.add)
        v.settle()
        tt(prod[:, 0:XTRA, :], oh[:, 0:XTRA, :], erow.unsqueeze(1).broadcast_to([P, XTRA, NE]), ALU.mult)
        v.settle()
        reduce(nbf[:, NE:NBLK], prod[:, 0:XTRA, :])
        v.settle()
        v.do(vec.tensor_copy(R["nbe"][:, :], nbf[:, :]), sem("experts_known"), 1)

    def load_hidden(eng, layer):
        for dst, src in ((R["zT"][:, :], zt_d), (R["wf1"][:, :], wf1_d[layer]), (R["bf"][:, :], bf_d[layer]),
                         (R["wf2"][:, :], wf2_d[layer])):
            eng.dma_start(dst, src).then_inc(event("hidden_loaded", layer), 16)

    def load_parameters(eng, layer):
        for dst, src in ((R["lamv"][:, :, :].rearrange("p a b -> p (a b)"),
                          lamv_d[layer:layer + 1, :].to_broadcast([P, 4 * DH])),
                         (R["wf3"][:, :], wf3_d[layer]),
                         (R["decay"][:, :, :, :].rearrange("p a b c -> p (a b c)"), decay_d),
                         (R["hyb"][:, :], hyb_d[layer:layer + 1, :]),
                         (PAR[:, :], par_d[layer])):
            eng.dma_start(dst, src).then_inc(event("par_loaded", layer), 16)

    block = ctx.enter_context(nc.Block())

    @block.sync
    def _(sp):
        def mixer_slabs(layer):
            w_in, w_hy, w_at, w_out = (slabs[k][layer] for k in ("w_in", "w_hy_o", "w_at_o", "w_out"))
            found = []
            for c in CHUNKS:
                for k in (0, 4):
                    found.append(w_in[k * P:(k + 4) * P, COLUMN[c]:COLUMN[c] + 512])
            for w in (w_hy, w_at):
                for h in range(2):
                    found.append(w[:, h * 512:(h + 1) * 512])
            for h in range(2):
                for k in (0, 4):
                    found.append(w_out[k * P:(k + 4) * P, h * 512:(h + 1) * 512])
            return found

        def put(slot, dst, src, free):
            if free is not None:
                sp.wait_ge(lo_ready, free)
            for d, s in zip(dst, src):
                sp.dma_start(d, s).then_inc(raw_loaded[slot], 16)

        sp.dma_start(IDENT[:, :], cst_d[:, 0:P]).then_inc(sem("ident_loaded"), 16)
        load_hidden(sp, 0)
        sp.dma_start(X[:, :, :], x_in.rearrange("(p t) d -> p t d", t=TB)).then_inc(sem("x_loaded"), 16)
        load_parameters(sp, 0)
        sp.dma_start(DFT[:, :, :, :, :].rearrange("p a b c d -> p (a b c d)"), dft_d).then_inc(sem("cst_loaded"), 16)
        sp.dma_start(ROPE[:, :, :, :].rearrange("p a b c -> p (a b c)"), cst_d[:, P:2 * P])\
            .then_inc(sem("cst_loaded"), 16)
        for layer in range(DEPTH):
            stage, first = ("mix", layer), FIRST["mix", layer]
            for p, src in enumerate(mixer_slabs(layer)):
                slot = raw_slot(stage, p)
                dst = RAW[:, slot, :].rearrange("p (k n) -> p k n", k=4)
                src = src.rearrange("(k p) n -> p k n", p=P)
                far = back(stage, p)
                put(slot, [dst[:, 0:2, :], dst[:, 2:4, :]], [src[:, 0:2, :], src[:, 2:4, :]],
                    None if far is None else first + p - far + 1)

            first = FIRST["ffn", layer]
            kind = "dense" if layer == 0 else "moe"
            w_gate, w_up, w_down = (slabs[f"w_{kind}_{k}"] for k in ("gate", "up", "down"))
            assert all(back(("ffn", layer), p) == RAW_SLOTS for p in range(FFN_SLABS))

            def gate_up(e, p, n, k0, nk, col, width):
                dst = RAW[:, p % RAW_SLOTS, 0:2 * nk * width].rearrange("p (k n) -> p k n", k=nk)
                src = [w[e, k0 * P:(k0 + nk) * P, col].rearrange("o (k p) n -> p (o k) n", p=P)
                       for w in (w_gate, w_up)]
                put(p % RAW_SLOTS, [dst[:, :, 0:width], dst[:, :, width:2 * width]], src, n - RAW_SLOTS + 1)

            def down(e, p, n, rows):
                dst = RAW[:, p % RAW_SLOTS, :].rearrange("p (k n) -> p k n", k=2)
                put(p % RAW_SLOTS, [dst[:, j, :] for j in range(2)],
                    [w_down[e, r, :].rearrange("o p n -> p (o n)") for r in rows], n - RAW_SLOTS + 1)

            def down_tail(e, p, n, k):
                lo, hi = NCH * CHUNK + k * P, min(NCH * CHUNK + (k + 1) * P, FF)
                halves = [slice(0, 512), slice(512, D)]
                put(p % RAW_SLOTS, [RAW[0:hi - lo, p % RAW_SLOTS, h] for h in halves],
                    [w_down[e, lo:hi, h].rearrange("o p n -> p (o n)") for h in halves], n - RAW_SLOTS + 1)

            def chunk_rows(c):
                return [slice(c * CHUNK, c * CHUNK + P), slice(c * CHUNK + P, (c + 1) * CHUNK)]

            def pair(e, n0, p0, cols, rows):
                for j in range(2):
                    p = p0 + 3 * j
                    for part in range(2):
                        gate_up(e, p + part, n0 + p + part, 4 * part, 4, cols[j], CHUNK)
                    down(e, p + 2, n0 + p + 2, rows[j])

            def block_slabs(n0, e):
                for part in range(4):
                    gate_up(e, part, n0 + part, 2 * part, 2, slice(0, CHUNK), CHUNK)
                with sp.Fori(0, 4) as i:
                    c0 = [sp.snap((2 * i + j) * CHUNK) for j in range(3)]
                    r1 = [sp.snap((2 * i + j) * CHUNK + P) for j in range(2)]
                    pair(e, sp.snap(n0 + 6 * i), 4, [bass.ds(c0[j + 1], CHUNK) for j in range(2)],
                         [[bass.ds(c0[j], P), bass.ds(r1[j], P)] for j in range(2)])
                c = NCH - 1
                for part in range(2):
                    gate_up(e, 28 + part, n0 + 28 + part, 4 * part, 4, slice(c * CHUNK, (c + 1) * CHUNK), CHUNK)
                down(e, 30, n0 + 30, chunk_rows(c - 1))
                for part in range(2):
                    gate_up(e, 31 + part, n0 + 31 + part, 4 * part, 4, slice(NCH * CHUNK, FF), TAIL)
                down(e, 33, n0 + 33, chunk_rows(c))
                for k in range(2):
                    down_tail(e, 34 + k, n0 + 34 + k, k)

            if layer == 0:
                block_slabs(first, slice(0, 1))
            else:
                with sp.Fori(0, NE) as b:
                    block_slabs(sp.snap(FFN_SLABS * b + first), bass.ds(b, 1))
                sp.wait_ge(sem("experts_known"), 1)
                nb = sp.value_load(R["nbi"][0:1, 0:1], min_val=NE, max_val=NBLK)
                with sp.If(nb > NE):
                    with sp.Fori(NE, nb) as b:
                        e = sp.value_load(R["nbe"][0:1, bass.ds(b, 1)], min_val=0, max_val=NE - 1)
                        block_slabs(sp.snap(FFN_SLABS * b + first), bass.ds(e, 1))
                n0 = sp.snap(FFN_SLABS * nb + first)
                for part in range(2):
                    gate_up(slice(0, 1), part, n0 + part, 2 * part, 2, slice(0, CHUNK), CHUNK)
        sp.wait_ge(scatter_added, 4 * nb + 4)
        sp.dma_start(out.rearrange("(p t) d -> p t d", t=TB), X[:, :, :]).then_inc(sem("stored"), 16)
        sp.wait_ge(sem("stored"), 16)

    @block.gpsimd
    def _(pool):
        g = Steps(pool, "pool_steps")
        def rstd(layer, name, src, dst, n, width):
            pool.wait_ge(event(f"{name}_ss", layer), 1)
            if width == D:
                g.do(nc.gpsimd.tensor_tensor(dst, src, STAT[:, TB:2 * TB], ALU.add))
                g.settle()
                src = dst
            g.do(nc.gpsimd.tensor_scalar(dst, src, 1.0 / width, EPS, ALU.mult, ALU.add))
            g.settle()
            s = event(f"{name}_rstd", layer)
            g.do(nc.gpsimd.tensor_tensor(dst, dst, HALF[:, 0:n], ALU.pow), s, 1)

        g.do(nc.gpsimd.memset(HALF[:, :], -0.5))
        g.settle()
        for layer in range(DEPTH):
            if layer:
                wait_drained(pool, layer - 1, "fht", 3)
                load_parameters(pool, layer)
            rstd(layer, "norm_mix", STAT[:, 0:TB], STAT[:, 4:4 + TB], TB, D)
            rstd(layer, "q", STAT[:, 8:24], STAT[:, 24:40], 16, DH)
            rstd(layer, "k", STAT[:, 8:24], STAT[:, 40:56], 16, DH)
            for h in range(NH):
                pool.wait_ge(event("o_ss", layer), h + 1)
                g.do(nc.gpsimd.tensor_scalar(STAT[:, 84:86], STAT[:, 56 + 2 * (h % 2):58 + 2 * (h % 2)],
                                             1.0 / DV, EPS, ALU.mult, ALU.add))
                g.settle()
                g.do(nc.gpsimd.tensor_tensor(STAT[:, 80 + 2 * (h % 2):82 + 2 * (h % 2)], STAT[:, 84:86],
                                             HALF[:, 0:TB], ALU.pow), event("o_rstd", layer), h + 1)
            if layer + 1 < DEPTH:
                wait_filled(pool, layer, "yT", 1)
                load_hidden(pool, layer + 1)
            if layer == 1:
                wait_filled(pool, layer, "yaT", 1)
                pool.dma_start(R["g_row"][:, :], nffn_d.to_broadcast([P, D])).then_inc(sem("moe_loaded"), 16)
                pool.dma_start(R["wr"][:, :, :], wr_d.rearrange("(k p) e -> p k e", p=P)).then_inc(sem("moe_loaded"), 16)
                pool.dma_start(R["moec"][:, :], moec_d).then_inc(sem("moe_loaded"), 16)
            rstd(layer, "norm_ffn", STAT[:, 0:TB], STAT[:, 4:4 + TB], TB, D)

    @block.scalar
    def _(act):
        a = Steps(act, "act_steps")
        done = [0]

        def copy(dst, src, signal=None, value=None, **kw):
            a.do(nc.scalar.activation(dst, src, ACT.Copy, **kw), signal, value)

        def split(n, slot_value, raw_slot, split_slot, width=SLAB):
            act.wait_ge(raw_loaded[raw_slot], slot_value)
            if not isinstance(n, int) or n >= SPLIT_SLOTS:
                act.wait_ge(slab_used, n - (SPLIT_SLOTS - 1))
            nc.scalar.activation(HI[:, split_slot, 0:width], RAW[:, raw_slot, 0:width], ACT.Copy)\
              .then_inc(hi_ready, 1)

        def split_to(last, stage):
            first = FIRST[stage]
            while done[0] <= min(last, first + LENGTH[stage[0]] - 1):
                n = done[0]
                p = n - first
                split(n, raw_value(stage, p), raw_slot(stage, p), n % SPLIT_SLOTS, width_of(stage, p))
                done[0] += 1

        for layer in range(DEPTH):
            stage = ("mix", layer)
            first = FIRST[stage]

            def ahead(step):
                split_to(first + LAST_SLAB[step] + 2, stage)

            def evac(step, i, dst, src=None, **kw):
                wait_filled(act, layer, step, i)
                copy(dst, bank(step, i)[:, :] if src is None else src, *drain_of(layer, step, i), **kw)

            def squares(i, name):
                tb, half = i // 2, i % 2
                cols = slice(half * 512, (half + 1) * 512)
                a.do(nc.scalar.activation(X_SQUARED[:, tb, cols], X[:, tb, cols], ACT.Square,
                                          accum_out=STAT[:, TB * half + tb:TB * half + tb + 1]),
                     *((event(f"{name}_ss", layer), 1) if i == 3 else (None, None)))

            def sine(which, j):
                act.wait_ge(event("sin_arg", which), j + 1)
                a.do(nc.scalar.activation(R["hdn"][:, j, :], R["rnd"][:, :], ACT.Sin),
                     event("sin_done", which), j + 1)

            if layer == 0:
                sine(0, 0)
                sine(0, 1)
                act.wait_ge(sem("x_loaded"), 16)
            for i in range(4):
                if layer:
                    act.wait_ge(event("ffn_added", 0), i + 1)
                squares(i, "norm_mix")
            act.wait_ge(event("lam_sums", layer), 1)
            a.do(nc.scalar.activation(LAM[:, 2:4], LAM[:, 0:2], ACT.Exp), event("lam_exp", layer), 1)
            for step, _ in PLAN:
                if layer + 1 < DEPTH and step in ("wo0", "wo1"):
                    sine(layer + 1, int(step[2]))
                if step in LAST_SLAB:
                    ahead(step)
                if step == "ht":
                    for i in range(4):
                        wait_filled(act, layer, "ht", i)
                        for j in range(2):
                            kd = 2 * i + j
                            copy(HTH[:, kd, :], bank("ht", i)[:, j * T:(j + 1) * T], event("ht_hi", layer), kd + 1,
                                 scale=PAR[:, PAR_GM + kd:PAR_GM + kd + 1])
                    split_to(first + 2, stage)
                elif step[:2] in ("ft", "cf"):
                    for ri in range(2):
                        evac(step, 2 * ri + 1,
                             FSP[:, 1, int(step[2]), ri, :] if step[:2] == "ft" else YS[:, 1, ri, :])
                if step in ("v", "x1", "x2"):
                    c = ("v", "x1", "x2").index(step)
                    if c == 0:
                        act.wait_ge(event("pads", layer), 1)
                    if c == 2:
                        act.wait_ge(event("conv_done", layer), 4)
                    for i in range(4):
                        evac(step, i, UPAD[:, c % 2, i, 1:T + 1].rearrange("p (i t) -> p t i", t=TB),
                             bank(step, i)[:, 0:T].rearrange("p (t i) -> p t i", t=TB))
                elif step in ("q", "k", "av"):
                    if step == "q":
                        act.wait_ge(event("fpm", layer), 4)
                    c = ("q", "k", "av").index(step)
                    for tb in range(TB):
                        evac(step, tb, QKV[:, c, tb, :])
                elif step in ("vT", "x1T", "x2T"):
                    c = ("x1T", "x2T", "vT").index(step)
                    for tb in range(TB):
                        evac(step, tb, XV[:, c, tb, :])
                elif step in ("g0", "g1", "g2", "g3"):
                    c = int(step[1])
                    for tb in range(TB):
                        wait_filled(act, layer, step, tb)
                        a.do(nc.scalar.activation(GATES[:, tb, c // 2, (c % 2) * 512:(c % 2 + 1) * 512],
                                                  bank(step, tb)[:, :], ACT.Sigmoid), *drain_of(layer, step, tb))
                elif step in ("qT", "kT"):
                    act.wait_ge(event("conv_done", layer), 12)
                    dst = QT if step == "qT" else KT
                    for i in range(2):
                        evac(step, i, dst[:, 2 * i:2 * i + 2, :].rearrange("p a b -> p (a b)"))
                elif step[:2] == "sc":
                    h = int(step[2])
                    act.wait_ge(event("neg_max", layer), h + 1)
                    if h:
                        act.wait_ge(event("a_ready", layer), 2 * h)
                    for c in range(2):
                        for tb in range(TB):
                            k = 2 * c + tb
                            a.do(nc.scalar.activation(R["e"][:, tb, c, :], bank(step, c)[:, tb * T:(tb + 1) * T],
                                                      ACT.Exp, scale=DH ** -0.5, bias=S_NEG[:, k:k + 1],
                                                      accum_out=S_SUM[:, k:k + 1]),
                                 *(drain_of(layer, step, c) if tb else (None, None)))
                elif step[:2] == "aT":
                    evac(step, 0, R["aT"][:, :, :].rearrange("p a b -> p (a b)"))
                elif step in ("av0", "av1", "av2", "av3"):
                    h = int(step[2])
                    wait_filled(act, layer, step, 0)
                    if h >= 2:
                        act.wait_ge(event("o_rstd", layer), h - 1)
                    for tb in range(TB):
                        a.settle()
                        a.do(nc.scalar.activation(SQUARES[:, :], bank(step, 0)[:, tb * DV:(tb + 1) * DV], ACT.Square,
                                                  accum_out=STAT[:, 56 + 2 * (h % 2) + tb:57 + 2 * (h % 2) + tb]),
                             *((event("o_ss", layer), h + 1) if tb == 1 else (None, None)))
                elif step in ("yT", "yaT", "mT", "fht"):
                    if step == "fht":
                        break
                    at = 4 if step == "yaT" else 0
                    for i in range(len(BANKS[step])):
                        wait_filled(act, layer, step, i)
                        copy(HTH[:, at + 2 * i:at + 2 * i + 2, :].rearrange("p a b -> p (a b)"), bank(step, i)[:, :],
                             event(f"{step}_hi", layer), i + 1)
            if layer == 1:
                act.wait_ge(sem("moe_loaded"), 48)
                copy(R["wr_hi"][:, :, :], R["wr"][:, :, :], sem("wr_hi_ready"), 1)
            stage = ("ffn", layer)
            first = FIRST[stage]
            for half in range(2):
                for tb in range(TB):
                    wait_drained(act, layer, f"wo{half}", tb)
                    squares(2 * tb + half, "norm_ffn")
                split_to(first + half * (2 - layer), stage)
            for i in range(4):
                wait_filled(act, layer, "fht", i)
                for j in range(2):
                    kd = 2 * i + j
                    copy(HTH[:, kd, :], bank("fht", i)[:, j * T:(j + 1) * T], event("fht_hi", layer), kd + 1,
                         scale=PAR[:, PAR_GF + kd:PAR_GF + kd + 1])
            if layer == 0:
                a.do(nc.scalar.activation(SQUARES[:, 0:1], HALF[:, 0:1], ACT.Silu))
            if layer == 1:
                act.wait_ge(sem("h_scaled"), TB)
                copy(R["hg_hi"][:, :, :], HG, sem("hg_hi_ready"), 1)
                act.wait_ge(sem("top_diff"), 1)
                a.do(nc.scalar.activation(R["tv"][:, 3, :], R["tv"][:, 2, :], ACT.Exp), sem("top_exp"), 1)
                a.do(nc.scalar.activation(SQUARES[:, 0:1], HALF[:, 0:1], ACT.Silu))

            uses = uses_before(stage)

            def ffn_split(p, n0, r0, width=SLAB):
                split(n0 + p, 32 * (uses[p % RAW_SLOTS] + p // RAW_SLOTS + 1) + r0, p % RAW_SLOTS,
                      (first + p) % SPLIT_SLOTS, width)

            tbs = TB if layer == 0 else 1

            def silu(q, n, parity, width=CHUNK):
                act.wait_ge(slab_used, n + 1)
                if not isinstance(q, int) or q:
                    act.wait_ge(act_done, q)
                for tb in range(tbs):
                    src = PS[tb if layer == 0 else parity][:, 0:width]
                    ins = nc.scalar.activation(R["silu"][:, tb, 0:width], src, ACT.Silu)
                ins.then_inc(silu_done, 1)

            def turned_hi(q):
                act.wait_ge(turned, q + 1)
                nc.scalar.activation(R["act_hi"][:, :, 0:tbs * P], PS[2][:, 0:2 * tbs * P].rearrange("p (k t) -> p k t", k=2),
                                     ACT.Copy).then_inc(act_hi_ready, 1)

            def gather_hi(b):
                for i in range(2):
                    act.wait_ge(gathered, 4 * b + i + 1)
                    ins = nc.scalar.activation(HTH[:, 4 * i:4 * i + 4, 0:P],
                                               PS[6 + i][:, :].rearrange("p (k t) -> p k t", k=4), ACT.Copy)
                ins.then_inc(g_hi_ready, 1)

            def scaled_y_hi(n):
                act.wait_ge(slab_used, n)
                for h in range(2):
                    ins = nc.scalar.activation(R["y_hi"][:, h * 512:(h + 1) * 512], PS[4 + h][:, :], ACT.Copy,
                                               scale=R["wslot"][:, 0:1])
                ins.then_inc(y_hi_ready, 1)

            def ffn_block(b, is_moe):
                n0 = act.snap(FFN_SLABS * b + first) if is_moe else first
                r0 = act.snap(32 * (FFN_SLABS // RAW_SLOTS) * b) if is_moe else 0
                qb = act.snap((NCH + 1) * b + Q_FIRST[layer]) if is_moe else Q_FIRST[layer]
                if is_moe:
                    ffn_split(2, n0, r0, 4 * CHUNK)
                ffn_split(3, n0, r0, 4 * CHUNK)
                if is_moe:
                    scaled_y_hi(n0)
                ffn_split(4, n0, r0)
                ffn_split(5, n0, r0)
                silu(qb, n0 + 3, 0)
                ffn_split(6, n0, r0)

                def chunk(p, q, parity, n0, r0, width=SLAB):
                    turned_hi(q - 1)
                    ffn_split(p + 3, n0, r0, width)
                    silu(q, n0 + p + 1, parity)
                    ffn_split(p + 4, n0, r0, width)
                    ffn_split(p + 5, n0, r0, width)

                with act.Fori(0, 4) as i:
                    n0i, r0i = act.snap(n0 + 6 * i), act.snap(r0 + 32 * i)
                    qi = act.snap(qb + 2 * i)
                    chunk(4, qi + 1, 1, n0i, r0i)
                    chunk(7, qi + 2, 0, n0i, r0i)
                if is_moe:
                    act.wait_ge(pselT_done, b + 1)
                    nc.scalar.activation(R["pselT"][:, :, :].rearrange("p a b -> p (a b)"), PS[3][:, 0:TB * P], ACT.Copy)
                    nc.scalar.activation(R["wslot"][:, 0:1], PS[3][:, 2 * P:2 * P + 1], ACT.Copy).then_inc(pselT_ready, 1)
                turned_hi(qb + NCH - 2)
                ffn_split(31, n0, r0, 8 * TAIL)
                silu(qb + NCH - 1, n0 + 29, 1)
                ffn_split(32, n0, r0, 8 * TAIL)
                ffn_split(33, n0, r0)
                turned_hi(qb + NCH - 1)
                ffn_split(34, n0, r0, D)
                silu(qb + NCH, n0 + 32, 0, TAIL)
                ffn_split(35, n0, r0, D)
                turned_hi(qb + NCH)
                if is_moe:
                    ffn_split(FFN_SLABS, n0, r0, 4 * CHUNK)
                    gather_hi(b + 1)
                    ffn_split(FFN_SLABS + 1, n0, r0, 4 * CHUNK)

            if layer == 0:
                ffn_block(0, False)
                done[0] = FIRST["mix", 1]
            else:
                gather_hi(0)
                act.wait_ge(sem("blocks_known"), 1)
                nb = act.value_load(R["nbi"][0:1, 0:1], min_val=NE, max_val=NBLK)
                with act.Fori(0, nb) as b:
                    ffn_block(b, True)
                scaled_y_hi(FFN_SLABS * nb + first)

    @block.vector
    def _(dve):
        v = Steps(dve, "dve_steps")
        vec = nc.vector
        done = [0]

        def tt(dst, in0, in1, op, signal=None, value=None):
            v.do(vec.tensor_tensor(dst, in0, in1, op), signal, value)

        def ts(dst, in0, s1, s2, op0, op1=None, signal=None, value=None):
            v.do(vec.tensor_scalar(dst, in0, s1, s2, op0, *([op1] if op1 else [])), signal, value)

        def stt(dst, in0, s, in1, op0, op1, signal=None, value=None):
            v.do(vec.scalar_tensor_tensor(out=dst, in0=in0, scalar=s, in1=in1, op0=op0, op1=op1), signal, value)

        def split(n, raw_slot, split_slot, width=SLAB):
            dve.wait_ge(hi_ready, n + 1)
            vec.tensor_tensor(LO[:, split_slot, 0:width], RAW[:, raw_slot, 0:width],
                              HI[:, split_slot, 0:width].bitcast(F32), ALU.subtract).then_inc(lo_ready, 1)

        def split_to(last, stage):
            first = FIRST[stage]
            while done[0] <= min(last, first + LENGTH[stage[0]] - 1):
                n = done[0]
                split(n, raw_slot(stage, n - first), n % SPLIT_SLOTS, width_of(stage, n - first))
                done[0] += 1

        def flat(ap):
            return ap.rearrange("p a b -> p (a b)")

        for layer in range(DEPTH):
            stage = ("mix", layer)
            first = FIRST[stage]
            def sine_arg(which, step, j):
                dve.wait_ge(event("hidden_loaded", which), 4 * 16)
                wait_filled(dve, layer, step, 0)
                arg, rnd = R["arg"][:, :], R["rnd"][:, :]
                ts(arg, bank(step, 0)[0:FH, 0:T], R["bf"][:, 2 * j:2 * j + 1], R["bf"][:, 2 * j + 1:2 * j + 2],
                   ALU.add, ALU.mult, *drain_of(layer, step, 0))
                v.settle()
                ts(rnd, arg, float(np.float32(0.5 / np.pi)), ROUND, ALU.mult, ALU.add)
                v.settle()
                ts(rnd, rnd, ROUND, None, ALU.subtract)
                for part in TWO_PI:
                    v.settle()
                    stt(arg, rnd, -part, arg, ALU.mult, ALU.add)
                v.settle()
                ts(rnd, arg, PI_BELOW, -PI_BELOW, ALU.min, ALU.max, event("sin_arg", which), j + 1)

            if layer == 0:
                for j in range(2):
                    sine_arg(0, f"f{j + 1}", j)
            dve.wait_ge(event("par_loaded", layer), 5 * 16)
            lv = R["lamv"]
            tt(TMP[:, 0:DH], lv[:, 0, :], lv[:, 1, :], ALU.mult)
            tt(TMP[:, DH:2 * DH], lv[:, 2, :], lv[:, 3, :], ALU.mult)
            ts(PAR[:, PAR_SUB:PAR_SUB + DV], PAR[:, PAR_SUB:PAR_SUB + DV], 1.0 - LAMBDA_INIT[layer], None, ALU.mult)
            v.settle()
            v.do(vec.tensor_reduce(LAM[:, 0:2], TMP[:, 0:2 * DH].rearrange("p (a b) -> p a b", a=2), AX_X, ALU.add),
                 event("lam_sums", layer), 1)
            def diagonal(name, ready):
                dve.wait_ge(event(f"{name}_rstd", layer), 1)
                for tb in range(TB):
                    ts(DIAG[:, tb, :], IDENT[:, :], STAT[:, 4 + tb:5 + tb], None, ALU.mult, None,
                       event(ready, layer), tb + 1)

            if layer == 0:
                dve.wait_ge(sem("ident_loaded"), 16)
            diagonal("norm_mix", "h_ready")
            fb, fpm = R["fb"], R["fpm"]

            def norm_rope(step, c, rstd_at):
                x = QKV[:, c, :, :].rearrange("p t (s d) -> p (t s) d", d=DH)
                tmp = TMP[:, :].rearrange("p (s d) -> p s d", d=DH)
                for tb in range(TB):
                    wait_drained(dve, layer, step, tb)
                v.settle()
                tt(tmp, x, x, ALU.mult)
                v.settle()
                v.do(vec.tensor_reduce(STAT[:, 8:24], tmp, AX_X, ALU.add), event(f"{step}_ss", layer), 1)
                split_to(first + LAST_SLAB[step] + 3, stage)
                dve.wait_ge(event(f"{step}_rstd", layer), 1)
                tt(x, x, STAT[:, rstd_at:rstd_at + 16].unsqueeze(2).broadcast_to([P, 16, DH]), ALU.mult)
                v.settle()
                gain = PAR[:, (PAR_QN if step == "q" else PAR_KN):][:, 0:DH]
                tt(x, x, gain.unsqueeze(1).broadcast_to([P, 16, DH]), ALU.mult)
                v.settle()
                for tb in range(TB):
                    y = QKV[:, c, tb, :].rearrange("p (s d) -> p s d", d=DH)
                    x1, x2 = y[:, :, 0:32], y[:, :, 32:64]
                    cos, sin = (ROPE[:, k, tb, :].unsqueeze(1).broadcast_to([P, 8, 32]) for k in range(2))
                    t = TMP[:, tb * 512:(tb + 1) * 512].rearrange("p (k s d) -> p k s d", k=2, d=32)
                    tt(t[:, 0], x2, sin, ALU.mult)
                    tt(t[:, 1], x1, sin, ALU.mult)
                    v.settle()
                    tt(x1, x1, cos, ALU.mult)
                    tt(x2, x2, cos, ALU.mult)
                    v.settle()
                    tt(x1, x1, t[:, 0], ALU.subtract)
                    tt(x2, x2, t[:, 1], ALU.add, event(f"{step}_roped", layer), tb + 1)

            def butterflies(step, low, high):
                for ri in range(2):
                    wait_drained(dve, layer, step, 2 * ri + 1)
                    even = bank(step, 2 * ri)[:, :]
                    tt(low[:, ri, :], even, high[:, ri, :], ALU.add)
                    v.settle()
                    tt(high[:, ri, :], *((high[:, ri, :], even) if ri else (even, high[:, ri, :])), ALU.subtract,
                       *drain_of(layer, step, 2 * ri))

            t0, t1 = TMP[:, 0:512], TMP[:, 512:1024]

            def multiply_spectra(o, kt):
                re, im = YS[:, kt, 0, :], YS[:, kt, 1, :]
                v.settle()
                tt(t0, FSP[:, kt, o, 1, :], im, ALU.mult)
                tt(t1, FSP[:, kt, o, 1, :], re, ALU.mult)
                v.settle()
                tt(re, FSP[:, kt, o, 0, :], re, ALU.mult)
                tt(im, FSP[:, kt, o, 0, :], im, ALU.mult)
                v.settle()
                tt(re, re, t0, ALU.subtract)
                tt(im, im, t1, ALU.add)

            def even_odd_spectra(o):
                v.settle()
                tt(t0, YS[:, 0, 0, :], YS[:, 1, 0, :], ALU.subtract)
                tt(t1, YS[:, 0, 1, :], YS[:, 1, 1, :], ALU.subtract)
                v.settle()
                tt(YS[:, 0, 0, :], YS[:, 0, 0, :], YS[:, 1, 0, :], ALU.add)
                tt(YS[:, 0, 1, :], YS[:, 0, 1, :], YS[:, 1, 1, :], ALU.add, event("ys_ready", layer), o + 1)

            for step, _ in PLAN:
                if layer + 1 < DEPTH and step in ("wo0", "wo1"):
                    sine_arg(layer + 1, f"n{int(step[2]) + 1}", int(step[2]))
                if step in LAST_SLAB and step != "g3":
                    split_to(first + LAST_SLAB[step] + 2, stage)
                if step[:2] == "hf":
                    o = int(step[2])
                    if o:
                        wait_filled(dve, layer, "ft0", 3)
                    for jt in range(2):
                        for i in range(2):
                            wait_filled(dve, layer, step, 2 * jt + i)
                            tt(fb[:, i, :], bank(step, 2 * jt + i)[:, :], R["decay"][:, jt, i, :], ALU.mult,
                               *drain_of(layer, step, 2 * jt + i))
                        v.settle()
                        if jt == 0:
                            stt(fb[0:1, 0, :], R["hyb"][0:1, o * HW:(o + 1) * HW], 1.0 / T, fb[0:1, 0, :], ALU.mult, ALU.add)
                            v.settle()
                        tt(fpm[:, jt, 0, :], fb[:, 0, :], fb[:, 1, :], ALU.add)
                        tt(fpm[:, jt, 1, :], fb[:, 0, :], fb[:, 1, :], ALU.subtract,
                           event("fpm", layer), 2 * o + jt + 1)
                        v.settle()
                elif step == "ht":
                    for i in range(4):
                        dve.wait_ge(event("ht_hi", layer), 2 * i + 2)
                        for j in range(2):
                            kd = 2 * i + j
                            stt(HTL[:, kd, :], bank("ht", i)[:, j * T:(j + 1) * T], PAR[:, PAR_GM + kd:PAR_GM + kd + 1],
                                HTH[:, kd, :].bitcast(F32), ALU.mult, ALU.subtract,
                                *(drain_of(layer, "ht", i) if j else (None, None)))
                    v.do(vec.memset(UPAD[:, :, :, 0:1], 0.0))
                    v.do(vec.memset(UPAD[:, :, :, T + 1:T + 2], 0.0), event("pads", layer), 1)
                    split_to(first + 2, stage)
                elif step[:2] == "ft":
                    o = int(step[2])
                    butterflies(step, FSP[:, 0, o, :, :], FSP[:, 1, o, :, :])
                elif step in ("v", "x1", "x2"):
                    c = ("v", "x1", "x2").index(step)
                    if c == 2:
                        wait_filled(dve, layer, "vT", 1)
                    for tap in range(3):
                        if tap:
                            v.settle()
                        for i in range(4):
                            w = PAR[:, PAR_CONV + 3 * (COLUMN[step] // P + i) + tap:][:, 0:1]
                            src = UPAD[:, c % 2, i, tap:tap + T].rearrange("p (i t) -> p i t", t=TB)
                            dst = CONV[:, c % 2, i, :].rearrange("p (t i) -> p i t", t=TB)
                            if tap == 0:
                                wait_drained(dve, layer, step, i)
                                ts(dst, src, w, None, ALU.mult)
                            else:
                                stt(dst, src, w, dst, ALU.mult, ALU.add,
                                    *((event("conv_done", layer), 4 * c + i + 1) if tap == 2 else (None, None)))
                elif step in ("q", "k"):
                    if step == "q":
                        dve.wait_ge(event("lam_exp", layer), 1)
                        tt(LAM[:, 4:5], LAM[:, 3:4], LAM[:, 2:3], ALU.subtract)
                        v.settle()
                        ts(LAM[:, 4:5], LAM[:, 4:5], -LAMBDA_INIT[layer], None, ALU.add)
                        if layer == 0:
                            dve.wait_ge(sem("cst_loaded"), 2 * 16)
                    norm_rope(step, ("q", "k").index(step), 24 if step == "q" else 40)
                elif step in ("cf0", "cf1"):
                    if step == "cf0":
                        wait_filled(dve, layer, "x2T", 1)
                    v.settle()
                    butterflies(step, YS[:, 0, :, :], YS[:, 1, :, :])
                    if step == "cf0":
                        multiply_spectra(0, 0)
                        split_to(first + LAST_SLAB["g0"] + 1, stage)
                        multiply_spectra(0, 1)
                        split_to(first + LAST_SLAB["g0"] + 2, stage)
                        even_odd_spectra(0)
                elif step in ("ci0", "ci1"):
                    o = int(step[2])
                    for tb in range(TB):
                        wait_filled(dve, layer, step, tb)
                        wait_drained(dve, layer, ("x1T", "x2T")[o], tb)
                        tt(XV[:, o, tb, :], XV[:, o, tb, :], bank(step, tb)[:, :], ALU.mult,
                           *drain_of(layer, step, tb))
                elif step[:2] == "sc":
                    h = int(step[2])
                    for c in range(2):
                        wait_filled(dve, layer, step, c)
                        v.do(vec.tensor_reduce(S_MAX[:, 2 * c:2 * c + 2],
                                               bank(step, c)[:, :].rearrange("p (t k) -> p t k", t=TB), AX_X, ALU.max))
                    v.settle()
                    ts(S_NEG, S_MAX, -DH ** -0.5, None, ALU.mult, None, event("neg_max", layer), h + 1)
                    if h == 2:
                        multiply_spectra(1, 0)
                    elif h == 3:
                        split_to(first + LAST_SLAB["g3"] + 1, stage)
                    for c in range(2):
                        wait_drained(dve, layer, step, c)
                    v.do(vec.reciprocal(S_FAC, S_SUM))
                    v.settle()
                    ts(S_FAC[:, 2:4], S_FAC[:, 2:4], LAM[:, 4:5], None, ALU.mult)
                    if h:
                        wait_filled(dve, layer, f"aT{h - 1}", 0)
                    v.settle()
                    for tb in range(TB):
                        ts(R["a"][:, tb, :], R["e"][:, tb, 1, :], S_FAC[:, 2 + tb:3 + tb], None, ALU.mult)
                    v.settle()
                    for tb in range(TB):
                        stt(R["a"][:, tb, :], R["e"][:, tb, 0, :], S_FAC[:, tb:tb + 1], R["a"][:, tb, :],
                            ALU.mult, ALU.add, event("a_ready", layer), 2 * h + tb + 1)
                elif step[:2] == "av" and step != "av":
                    h = int(step[2])
                    wait_filled(dve, layer, step, 0)
                    dve.wait_ge(event("o_rstd", layer), h + 1)
                    for tb in range(TB):
                        stt(QKV[:, 2, tb, h * DV:(h + 1) * DV], bank(step, 0)[:, tb * DV:(tb + 1) * DV],
                            STAT[:, 80 + 2 * (h % 2) + tb:81 + 2 * (h % 2) + tb], PAR[:, PAR_SUB:PAR_SUB + DV],
                            ALU.mult, ALU.mult, *(drain_of(layer, step, 0) if tb else (None, None)))
                elif step in ("yT", "yaT", "mT"):
                    at = 4 if step == "yaT" else 0
                    for i in range(len(BANKS[step])):
                        dve.wait_ge(event(f"{step}_hi", layer), i + 1)
                        tt(flat(HTL[:, at + 2 * i:at + 2 * i + 2, :]), bank(step, i)[:, :],
                           flat(HTH[:, at + 2 * i:at + 2 * i + 2, :]).bitcast(F32), ALU.subtract,
                           *drain_of(layer, step, i))
                elif step == "g3":
                    multiply_spectra(1, 1)
                    even_odd_spectra(1)
                elif step[:2] == "ph":
                    half = slice(int(step[2]) * 512, int(step[2]) * 512 + 512)
                    for tb in range(TB):
                        wait_filled(dve, layer, step, tb)
                        wait_drained(dve, layer, f"g{step[2]}", tb)
                        tt(GATES[:, tb, 0, half], GATES[:, tb, 0, half], bank(step, tb)[:, :], ALU.mult,
                           *drain_of(layer, step, tb))
                elif step[:2] == "pa":
                    half = slice(int(step[2]) * 512, int(step[2]) * 512 + 512)
                    for tb in range(TB):
                        wait_filled(dve, layer, step, tb)
                        wait_drained(dve, layer, f"g{2 + int(step[2])}", tb)
                        v.settle()
                        tt(TMP[:, 0:512], GATES[:, tb, 1, half], bank(step, tb)[:, :], ALU.mult,
                           *drain_of(layer, step, tb))
                        v.settle()
                        tt(GATES[:, tb, 0, half], GATES[:, tb, 0, half], TMP[:, 0:512], ALU.add,
                           event("merged", layer), 2 * int(step[2]) + tb + 1)
                elif step[:2] == "wo":
                    half = slice(int(step[2]) * 512, int(step[2]) * 512 + 512)
                    for tb in range(TB):
                        wait_filled(dve, layer, step, tb)
                        tt(X[:, tb, half], X[:, tb, half], bank(step, tb)[:, :], ALU.add,
                           *drain_of(layer, step, tb))

            stage = ("ffn", layer)
            first = FIRST[stage]
            split_to(first, stage)
            if layer == 1:
                dve.wait_ge(sem("wr_hi_ready"), 1)
                tt(R["wr_lo"][:, :, :], R["wr"][:, :, :], R["wr_hi"][:, :, :].bitcast(F32), ALU.subtract)
            diagonal("norm_ffn", "hf_ready")
            split_to(first + 1, stage)
            for i in range(4):
                dve.wait_ge(event("fht_hi", layer), 2 * i + 2)
                for j in range(2):
                    kd = 2 * i + j
                    stt(HTL[:, kd, :], bank("fht", i)[:, j * T:(j + 1) * T], PAR[:, PAR_GF + kd:PAR_GF + kd + 1],
                        HTH[:, kd, :].bitcast(F32), ALU.mult, ALU.subtract,
                        *(drain_of(layer, "fht", i) if j else (None, None)))
            if layer == 0:
                split_to(first + 2, stage)
            else:
                dve.wait_ge(sem("moe_loaded"), 48)
                for tb in range(TB):
                    stt(HG[:, tb, :], X[:, tb, :], STAT[:, 4 + tb:5 + tb], R["g_row"][:, :], ALU.mult, ALU.mult,
                        sem("h_scaled"), tb + 1)

            tbs = TB if layer == 0 else 1

            def mult(q, parity, width=CHUNK):
                dve.wait_ge(silu_done, q + 1)
                for tb in range(tbs):
                    ins = vec.tensor_tensor(R["act"][:, tb, 0:width], R["silu"][:, tb, 0:width],
                                            PS[tb if layer == 0 else parity][:, width:2 * width], ALU.mult)
                ins.then_inc(act_done, 1)

            def turned_lo(q):
                dve.wait_ge(act_hi_ready, q + 1)
                vec.tensor_tensor(R["act_lo"][:, :, 0:tbs * P],
                                  PS[2][:, 0:2 * tbs * P].rearrange("p (k t) -> p k t", k=2),
                                  R["act_hi"][:, :, 0:tbs * P].bitcast(F32), ALU.subtract).then_inc(act_lo_ready, 1)

            def gather_lo(b):
                for i in range(2):
                    dve.wait_ge(gathered, 4 * b + i + 3)
                    ins = vec.tensor_copy(HTL[:, 4 * i:4 * i + 4, 0:P],
                                          PS[(3, 1)[i]][:, :].rearrange("p (k t) -> p k t", k=4))
                ins.then_inc(g_lo_ready, 1)

            def select(b):
                for tb in range(TB):
                    ins = vec.tensor_scalar(R["psel"][:, tb, :], R["moec"][:, 0:P],
                                            R["pcol"][:, tb, bass.ds(b, 1)], None, ALU.is_equal)
                ins.then_inc(psel_ready, 1)
                vec.tensor_copy(R["wcur"][:, :], R["wcol"][:, :, bass.ds(b, 1)].rearrange("p a b -> p (a b)"))\
                   .then_inc(wcur_ready, 1)

            def y_lo():
                for h in range(2):
                    ins = vec.scalar_tensor_tensor(out=R["y_lo"][:, h * 512:(h + 1) * 512], in0=PS[4 + h][:, :],
                                                   scalar=R["wslot"][:, 0:1],
                                                   in1=R["y_hi"][:, h * 512:(h + 1) * 512].bitcast(F32),
                                                   op0=ALU.mult, op1=ALU.subtract)
                ins.then_inc(y_ready, 1)

            def add_scattered(b, i):
                tb, cols = i // 2, slice((i % 2) * 512, (i % 2) * 512 + 512)
                dve.wait_ge(scattered, 4 * b + i + 1)
                vec.tensor_tensor(X[:, tb, cols], X[:, tb, cols], PS[SCATTER_BANKS[i]][:, :], ALU.add)\
                   .then_inc(scatter_added, 1)

            def ffn_split(p, n0, width=SLAB):
                split(n0 + p, p % FFN_SLABS % RAW_SLOTS, (first + p) % SPLIT_SLOTS, width)

            def ffn_block(b, is_moe):
                n0 = dve.snap(FFN_SLABS * b + first) if is_moe else first
                qb = dve.snap((NCH + 1) * b + Q_FIRST[layer]) if is_moe else Q_FIRST[layer]
                if is_moe:
                    ffn_split(2, n0, 4 * CHUNK)
                ffn_split(3, n0, 4 * CHUNK)
                if is_moe:
                    dve.wait_ge(y_hi_ready, b + 1)
                    y_lo()
                ffn_split(4, n0)
                if is_moe:
                    add_scattered(b, 0)
                mult(qb, 0)
                ffn_split(5, n0)
                ffn_split(6, n0)

                def chunk(p, q, parity, n0, adds=False):
                    turned_lo(q - 1)
                    ffn_split(p + 3, n0)
                    if adds:
                        add_scattered(b, 1)
                    mult(q, parity)
                    ffn_split(p + 4, n0)
                    if adds:
                        add_scattered(b, 2)
                    ffn_split(p + 5, n0)
                    if adds:
                        add_scattered(b, 3)

                chunk(4, qb + 1, 1, n0, is_moe)
                chunk(7, qb + 2, 0, n0)
                with dve.Fori(1, 4) as i:
                    n0i, qi = dve.snap(n0 + 6 * i), dve.snap(qb + 2 * i)
                    chunk(4, qi + 1, 1, n0i)
                    chunk(7, qi + 2, 0, n0i)
                if is_moe:
                    dve.wait_ge(pselT_done, b + 1)
                    select(b + 1)
                turned_lo(qb + NCH - 2)
                ffn_split(31, n0, 8 * TAIL)
                mult(qb + NCH - 1, 1)
                ffn_split(32, n0, 8 * TAIL)
                ffn_split(33, n0)
                turned_lo(qb + NCH - 1)
                ffn_split(34, n0, D)
                mult(qb + NCH, 0, TAIL)
                ffn_split(35, n0, D)
                turned_lo(qb + NCH)
                if is_moe:
                    ffn_split(FFN_SLABS, n0, 4 * CHUNK)
                    gather_lo(b + 1)
                    ffn_split(FFN_SLABS + 1, n0, 4 * CHUNK)

            if layer == 0:
                ffn_block(0, False)
                dve.wait_ge(slab_used, first + FFN_SLABS)
                for i in range(4):
                    tb, half = i // 2, slice((i % 2) * 512, (i % 2) * 512 + 512)
                    tt(X[:, tb, half], X[:, tb, half], PS[4 + i][:, :], ALU.add,
                       event("ffn_added", 0), i + 1)
                done[0] = FIRST["mix", 1]
            else:
                router(dve, v, tt, ts, stt, lambda: gather_lo(0))
                nb = dve.value_load(R["nbi"][0:1, 0:1], min_val=NE, max_val=NBLK)
                with dve.Fori(0, nb) as b:
                    ffn_block(b, True)
                dve.wait_ge(y_hi_ready, nb + 1)
                y_lo()
                for i in range(4):
                    add_scattered(nb, i)

    @block.tensor
    def _(pe):
        mm = nc.tensor.matmul

        def three(out_, l_hi, l_lo, r_hi, r_lo, start, stop):
            mm(out_, l_hi, r_hi, start=start, stop=False)
            mm(out_, l_hi, r_lo, start=False, stop=False)
            return mm(out_, l_lo, r_hi, start=False, stop=stop)

        def bank_free(layer, step, i):
            b = BANKS[step][i]
            if DRAINS[layer, step, b] > 1:
                pe.wait_ge(drained[b], DRAINS[layer, step, b] - 1)

        def fill(layer, step, i, ins):
            ins.then_inc(filled[BANKS[step][i]], 1)

        def turn(dst, src):
            return nc.tensor.transpose(dst, src, IDENT[:, :])

        def w_parts(n_mod, lo, hi):
            return HI[:, n_mod, lo:hi], LO[:, n_mod, lo:hi]

        def project(layer, step, n, k0, nk, start, stop, turned_w, turned_by=None):
            pe.wait_ge(lo_ready, n + 1)
            s = n % SPLIT_SLOTS
            for k in range(nk):
                kd = k0 + k
                st, sp_ = start and k == 0, stop and k == nk - 1
                if turned_by and kd % 2 == 0:
                    wait_drained(pe, layer, turned_by, kd // 2)
                if turned_w:
                    for m in range(4):
                        w_hi, w_lo = w_parts(s, k * 512 + m * P, k * 512 + (m + 1) * P)
                        ins = three(bank(step, m)[:, 0:T], w_hi, w_lo, HTH[:, kd, :], HTL[:, kd, :], st, sp_)
                else:
                    w_hi, w_lo = w_parts(s, k * 512, (k + 1) * 512)
                    for tb in range(TB):
                        tok = slice(tb * P, (tb + 1) * P)
                        ins = three(bank(step, tb)[:, :], HTH[:, kd, tok], HTL[:, kd, tok], w_hi, w_lo, st, sp_)
            ins.then_inc(slab_used, 1)

        for layer in range(DEPTH):
            first = FIRST["mix", layer]
            if layer == 0:
                pe.wait_ge(sem("ident_loaded"), 16)
            else:
                pe.wait_ge(act_done, Q_FIRST[layer])
            for step, banks in plan(layer):
                if step in ("rt", "pos"):
                    continue
                if step in LAST_SLAB:
                    last = first + LAST_SLAB[step]
                    for i in range(len(banks)):
                        bank_free(layer, step, i)
                    if step in ("ph0", "pa0"):
                        for i in range(2):
                            wait_drained(pe, layer, "yT" if step == "ph0" else "yaT", i)
                    if step[:2] in ("ph", "pa"):
                        project(layer, step, last, 4 * (step[:2] == "pa"), 4, True, True, False)
                    else:
                        for part in range(2):
                            project(layer, step, last - 1 + part, 4 * part, 4, part == 0, part == 1,
                                    step in ("v", "x1", "x2"), {"v": "ht", "wo0": "mT"}.get(step))
                    continue
                own = layer + (step[0] == "n")
                if step in ("f1", "n1"):
                    pe.wait_ge(event("hidden_loaded", own), 4 * 16)
                elif step in ("f2", "n2"):
                    pe.wait_ge(event("sin_done", own), 1)
                elif step[:2] == "hf":
                    pe.wait_ge(event("sin_done", layer), 2)
                    pe.wait_ge(event("par_loaded", layer), 5 * 16)
                elif step[:2] == "ft":
                    pe.wait_ge(event("fpm", layer), 2 * int(step[2]) + 2)
                elif step == "ht":
                    pe.wait_ge(event("h_ready", layer), TB)
                    if layer:
                        pe.wait_ge(event("ffn_added", 0), 4)
                    if layer == 0:
                        pe.wait_ge(sem("cst_loaded"), 2 * 16)
                elif step in ("vT", "x1T", "x2T"):
                    pe.wait_ge(event("conv_done", layer), {"vT": 4, "x1T": 8, "x2T": 12}[step])
                elif step == "cf0":
                    for tb in range(TB):
                        wait_drained(pe, layer, "vT", tb)
                elif step == "cf1":
                    for tb in range(TB):
                        wait_drained(pe, layer, "ci0", tb)
                elif step[:2] == "ci":
                    pe.wait_ge(event("ys_ready", layer), int(step[2]) + 1)
                elif step in ("qT", "kT"):
                    pe.wait_ge(event(f"{step[0]}_roped", layer), TB)
                elif step == "sc0":
                    for i in range(2):
                        wait_drained(pe, layer, "qT", i)
                        wait_drained(pe, layer, "kT", i)
                elif step[:2] == "aT":
                    pe.wait_ge(event("a_ready", layer), 2 * int(step[2]) + 2)
                elif step[:2] == "av":
                    wait_drained(pe, layer, f"aT{step[2]}", 0)
                    for tb in range(TB):
                        wait_drained(pe, layer, "av", tb)
                elif step == "yT":
                    for tb in range(TB):
                        wait_drained(pe, layer, "ci1", tb)
                elif step == "yaT":
                    wait_drained(pe, layer, "av3", 0)
                elif step == "fht":
                    pe.wait_ge(event("hf_ready", layer), TB)
                for i in range(len(banks)):
                    bank_free(layer, step, i)
                    if step == "mT":
                        pe.wait_ge(event("merged", layer), 2 + i // 2 * 2)
                    dst = bank(step, i)
                    if step in ("f1", "n1"):
                        ins = mm(dst[0:FH, 0:T], R["wf1"][:, :], R["zT"][:, :], start=True, stop=True)
                    elif step in ("f2", "n2"):
                        ins = mm(dst[0:FH, 0:T], R["wf2"][:, :], R["hdn"][:, 0, :], start=True, stop=True)
                    elif step[:2] == "hf":
                        jt, part = i // 2, 2 * int(step[2]) + i % 2
                        ins = mm(dst[:, :], R["hdn"][:, 1, jt * P:(jt + 1) * P],
                                 R["wf3"][:, part * HW:(part + 1) * HW], start=True, stop=True)
                    elif step[:2] in ("ft", "cf"):
                        ri, par = i // 2, i % 2
                        src = R["fpm"][:, par, ri, :] if step[:2] == "ft" else \
                            XV[:, 0 if step == "cf1" else 2, par, :]
                        ins = mm(dst[:, :], DFT[:, 0, ri, par, :], src, start=True, stop=True)
                    elif step[:2] == "ci":
                        re, im = (YS[:, 0, 0, :], TMP[:, 512:1024]) if i == 0 else (TMP[:, 0:512], YS[:, 0, 1, :])
                        mm(dst[:, :], DFT[:, 1, 0, i, :], re, start=True, stop=False)
                        ins = mm(dst[:, :], DFT[:, 1, 1, i, :], im, start=False, stop=True)
                    elif step in ("ht", "fht", "mT"):
                        for j in range(4):
                            kd, tb = 2 * i + j // 2, j % 2
                            col, to = slice(kd * P, (kd + 1) * P), dst[:, j * P:(j + 1) * P]
                            if step == "mT":
                                ins = turn(to, GATES[:, tb, 0, col])
                            else:
                                ins = mm(to, X[:, tb, col], DIAG[:, tb, :], start=True, stop=True)
                    elif step in ("vT", "x1T", "x2T"):
                        c = ("vT", "x1T", "x2T").index(step)
                        for j in range(4):
                            ins = turn(dst[:, j * P:(j + 1) * P], CONV[:, c % 2, j, i * P:(i + 1) * P])
                    elif step in ("qT", "kT", "yT", "yaT"):
                        for j in range(4):
                            t, tb = 2 * i + j // 2, j % 2
                            col = slice(t * P, (t + 1) * P)
                            src = XV[:, 1, tb, col] if step == "yT" else \
                                QKV[:, {"qT": 0, "kT": 1, "yaT": 2}[step], tb, col]
                            ins = turn(dst[:, j * P:(j + 1) * P], src)
                    elif step[:2] == "sc":
                        h = int(step[2])
                        d = slice(i * DH, (i + 1) * DH)
                        for tb in range(TB):
                            ins = mm(dst[:, tb * T:(tb + 1) * T], QT[d, h, tb * P:(tb + 1) * P], KT[d, h, :],
                                     start=True, stop=True)
                    elif step[:2] == "aT":
                        for j in range(4):
                            kt, tb = j // 2, j % 2
                            ins = turn(dst[:, j * P:(j + 1) * P], R["a"][:, tb, kt * P:(kt + 1) * P])
                    elif step[:2] == "av":
                        h = int(step[2])
                        for j in range(4):
                            tb, kt = j // 2, j % 2
                            ins = mm(dst[:, tb * DV:(tb + 1) * DV], R["aT"][:, kt, tb * P:(tb + 1) * P],
                                     QKV[:, 2, kt, h * DV:(h + 1) * DV], start=kt == 0, stop=kt == 1)
                    fill(layer, step, i, ins)

            first = FIRST["ffn", layer]
            if layer == 1:
                bank_free(1, "rt", 0)
                pe.wait_ge(sem("wr_hi_ready"), 1)
                for i in range(4):
                    wait_drained(pe, layer, "fht", i)
                for tb in range(TB):
                    tok = slice(tb * P, (tb + 1) * P)
                    for kd in range(KD):
                        ins = three(bank("rt", 0)[:, tb * NE:(tb + 1) * NE], HTH[:, kd, tok], HTL[:, kd, tok],
                                    R["wr_hi"][:, kd, :], R["wr_lo"][:, kd, :], kd == 0, kd == KD - 1)
                fill(1, "rt", 0, ins)
                pe.wait_ge(sem("sel_ready"), 1)
                bank_free(1, "pos", 0)
                tri, ones = R["moec"][:, P:2 * P], R["moec"][:, 2 * P:3 * P]
                for i, terms in enumerate((((tri, 0),), ((ones, 0), (tri, 1)), ((ones, 0), (ones, 1)))):
                    for k, (m, tb) in enumerate(terms):
                        ins = mm(bank("pos", 0)[:, i * NE:(i + 1) * NE], m, R["sel"][:, tb, :],
                                 start=k == 0, stop=k == len(terms) - 1)
                fill(1, "pos", 0, ins)

            tbs = TB if layer == 0 else 1

            def gate_up(n, s, k0, nk, width, q, parity, turned_by=None):
                pe.wait_ge(lo_ready, n + 1)
                if layer == 0 and k0 == 0 and not (isinstance(q, int) and q == 0):
                    pe.wait_ge(act_done, q)
                for k in range(nk):
                    kd = k0 + k
                    if turned_by and kd % 2 == 0:
                        wait_drained(pe, layer, turned_by, kd // 2)
                    w_hi, w_lo = w_parts(s, k * 2 * width, (k + 1) * 2 * width)
                    for tb in range(tbs):
                        tok = slice(tb * P, (tb + 1) * P)
                        ins = three(PS[tb if layer == 0 else parity][:, 0:2 * width], HTH[:, kd, tok],
                                    HTL[:, kd, tok], w_hi, w_lo, kd == 0, kd == KD - 1)
                ins.then_inc(slab_used, 1)

            def turn_act(q, width=CHUNK):
                pe.wait_ge(act_done, q + 1)
                for k in range(2):
                    h = min(P, width - k * P)
                    for tb in range(tbs):
                        at = (k * tbs + tb) * P
                        ins = turn(PS[2][0:h, at:at + P], R["act"][:, tb, k * P:k * P + h])
                ins.then_inc(turned, 1)

            def down(n, s, q, start, stop=False, tiles=((0, P), (1, P))):
                pe.wait_ge(lo_ready, n + 1)
                pe.wait_ge(act_lo_ready, q + 1)
                for j, (k, h) in enumerate(tiles):
                    for tb in range(tbs):
                        tok = slice(tb * P, (tb + 1) * P)
                        for half in range(2):
                            at = j * D + half * 512
                            ins = three(PS[4 + 2 * tb + half][:, :], R["act_hi"][0:h, k, tok], R["act_lo"][0:h, k, tok],
                                        HI[0:h, s, at:at + 512], LO[0:h, s, at:at + 512],
                                        start and k == 0, stop and k == 1)
                ins.then_inc(slab_used, 1)

            def gather(b):
                pe.wait_ge(psel_ready, b + 1)
                for i, (src, bk) in enumerate(((R["hg_hi"], 6), (R["hg_hi"], 7), (R["hg_lo"], 3), (R["hg_lo"], 1))):
                    if isinstance(b, int):
                        pe.wait_ge(sem("hg_hi_ready") if i < 2 else sem("hg_lo_ready"), 1)
                    for k in range(4):
                        kd = 4 * (i % 2) + k
                        for tb in range(TB):
                            ins = mm(PS[bk][:, k * P:(k + 1) * P], src[:, tb, kd * P:(kd + 1) * P],
                                     R["psel"][:, tb, :], start=tb == 0, stop=tb == 1)
                    ins.then_inc(gathered, 1)

            def scatter(b):
                pe.wait_ge(y_ready, b + 1)
                for i, bk in enumerate(SCATTER_BANKS):
                    tb, cols = i // 2, slice((i % 2) * 512, (i % 2) * 512 + 512)
                    mm(PS[bk][:, :], R["pselT"][:, tb, :], R["y_hi"][:, cols], start=True, stop=False)
                    mm(PS[bk][:, :], R["pselT"][:, tb, :], R["y_lo"][:, cols], start=False, stop=True)\
                        .then_inc(scattered, 1)

            def ffn_block(b, is_moe):
                n0 = pe.snap(FFN_SLABS * b + first) if is_moe else first
                qb = pe.snap((NCH + 1) * b + Q_FIRST[layer]) if is_moe else Q_FIRST[layer]

                def slot(p):
                    return (first + p) % SPLIT_SLOTS
                if is_moe:
                    pe.wait_ge(g_hi_ready, b + 1)
                    pe.wait_ge(g_lo_ready, b + 1)
                for part in range(4):
                    gate_up(n0 + part, slot(part), 2 * part, 2, CHUNK, qb, 0, None if is_moe else "fht")
                if is_moe:
                    scatter(b)

                def pair(n0, qb, start):
                    for j in range(2):
                        p, q = 4 + 3 * j, qb + 1 + j
                        gate_up(n0 + p, slot(p), 0, 4, CHUNK, q, 1 - j)
                        if is_moe and start and j == 0:
                            pe.wait_ge(scatter_added, 4 * b + 1)
                        turn_act(q - 1)
                        gate_up(n0 + p + 1, slot(p + 1), 4, 4, CHUNK, q, 1 - j)
                        down(n0 + p + 2, slot(p + 2), q - 1, start and j == 0)

                pair(n0, qb, True)
                with pe.Fori(1, 4) as i:
                    pair(pe.snap(n0 + 6 * i), pe.snap(qb + 2 * i), False)
                if is_moe:
                    pe.wait_ge(wcur_ready, b + 1)
                    pe.wait_ge(scatter_added, 4 * b + 4)
                    for tb in range(TB):
                        turn(PS[3][:, tb * P:(tb + 1) * P], R["psel"][:, tb, :].bitcast(F32))
                    for tb in range(TB):
                        ins = mm(PS[3][:, 2 * P:2 * P + 1], R["psel"][:, tb, :].bitcast(F32), R["wcur"][:, tb:tb + 1],
                                 start=tb == 0, stop=tb == 1)
                    ins.then_inc(pselT_done, 1)
                q = qb + NCH - 1
                gate_up(n0 + 28, slot(28), 0, 4, CHUNK, q, 1)
                turn_act(q - 1)
                gate_up(n0 + 29, slot(29), 4, 4, CHUNK, q, 1)
                down(n0 + 30, slot(30), q - 1, False)
                gate_up(n0 + 31, slot(31), 0, 4, TAIL, q + 1, 0)
                turn_act(q)
                gate_up(n0 + 32, slot(32), 4, 4, TAIL, q + 1, 0)
                down(n0 + 33, slot(33), q, False)
                turn_act(q + 1, TAIL)
                if is_moe:
                    pe.wait_ge(pselT_ready, b + 1)
                    gather(b + 1)
                down(n0 + 34, slot(34), q + 1, False, tiles=((0, P),))
                down(n0 + 35, slot(35), q + 1, False, True, tiles=((1, TAIL - P),))

            if layer == 0:
                ffn_block(0, False)
            else:
                pe.wait_ge(psel_ready, 1)
                for half in range(2):
                    mm(PS[4 + half][:, :], R["pselT"][:, 0, :], HTH[:, 2 * half:2 * half + 2, :].rearrange("p a b -> p (a b)"),
                       start=True, stop=True)
                gather(0)
                pe.wait_ge(sem("blocks_known"), 1)
                nb = pe.value_load(R["nbi"][0:1, 0:1], min_val=NE, max_val=NBLK)
                with pe.Fori(0, nb) as b:
                    ffn_block(b, True)
                scatter(nb)

    ctx.close()


def constants():
    f = np.float32
    n = np.arange(P)
    angle = 2 * np.pi * (2 * n[:, None, None] + np.arange(TB)[None, :, None]) * (n + 0.5) / (2 * T)
    forward = np.stack([np.cos(angle), np.sin(angle)], axis=1)
    dft = np.stack([forward, forward.transpose(3, 1, 2, 0)], axis=1).reshape(P, 8 * P).astype(f)
    inv = (f(1.0) / (f(10000.0) ** (np.arange(0, DH, 2, dtype=f) / f(DH)))).astype(f)
    ang = np.arange(T, dtype=f)[:, None] * inv[None, :]
    rope = np.stack([np.cos(ang), np.sin(ang)]).astype(f).reshape(2, P, TB, DH // 2)
    cst = np.concatenate([np.eye(P, dtype=f), rope.transpose(1, 0, 2, 3).reshape(P, P)], axis=1)
    t = np.linspace(0.0, 1.0, T, dtype=f)[:, None]
    w = (f(2.0 * np.pi) * np.arange(T, dtype=f)[:, None] / f(T)).astype(f)
    bands = (FE - 1) // 2
    fr = np.linspace(1e-4, bands - 1, bands, dtype=f)[None, :]
    z = np.concatenate([t, np.cos(fr * w), -np.sin(fr * w)], axis=-1).astype(f)
    deltas = np.linspace(np.log(1e-2) / 1.5, np.log(1e-2) / 0.3, HW).astype(f)
    decay = np.exp(-t * np.abs(deltas)[None, :]).astype(f) / f(T)
    both = np.stack([decay, decay])
    both[1, 0] = 0
    both = both.reshape(2, P, TB, HW).transpose(1, 2, 0, 3).reshape(P, 4 * HW)
    moec = np.zeros((P, 3 * P + 64 + 8 + 4), f)
    moec[:, 0:P] = np.arange(P)
    moec[:, P:2 * P] = np.triu(np.ones((P, P)), 1)
    moec[:, 2 * P:3 * P] = 1
    moec[:, 3 * P:3 * P + 64] = np.tril(np.ones((NE, NE)), -1).reshape(1, 64)
    moec[:, 3 * P + 64:3 * P + 72] = np.arange(NE)
    zt = z.T.reshape(FE, P, TB).transpose(0, 2, 1).reshape(FE, T)
    return {"cst": cst, "dft": dft, "decay": both, "zt": zt, "moec": moec}


STREAMED = ["w_in", "w_hy_o", "w_at_o", "w_out", "w_dense_gate", "w_dense_up", "w_dense_down",
            "w_moe_gate", "w_moe_up", "w_moe_down"]


def kernel(**inputs):
    import concourse.bacc as bacc
    from concourse.bass_utils import run_bass_kernel_spmd

    a = {k: np.asarray(v) for k, v in inputs.items()}
    par = np.zeros((DEPTH, P, PAR_N), np.float32)
    for layer in range(DEPTH):
        par[layer, :, PAR_CONV:PAR_GM] = a["conv_w"][layer].reshape(3, 12, P).transpose(2, 1, 0).reshape(P, 36)
        par[layer, :, PAR_GM:PAR_GF] = a["norm_mix"][layer].reshape(KD, P).T
        par[layer, :, PAR_GF:PAR_QN] = a["norm_ffn"][layer].reshape(KD, P).T
        par[layer, :, PAR_QN:PAR_KN] = a["q_norm"][layer]
        par[layer, :, PAR_KN:PAR_SUB] = a["k_norm"][layer]
        par[layer, :, PAR_SUB:PAR_N] = a["subln_g"][layer]
    ins = dict(
        x=a["x"][0], par=par,
        lamv=np.concatenate([a["lam_q1"], a["lam_k1"], a["lam_q2"], a["lam_k2"]], axis=1),
        wf1=a["w_f1"], wf2=a["w_f2"],
        bf=np.stack([a["b_f1"], a["freq1"], a["b_f2"], a["freq2"]], axis=2),
        wf3=a["w_f3"], hyb=a["hy_bias"].reshape(DEPTH, 2 * HW), nffn=a["norm_ffn"][1:2], wr=a["w_router"][0],
        **constants())
    ins.update({k: a[k] for k in STREAMED if "moe" not in k})
    ins.update({k: a[k][0] for k in STREAMED if "moe" in k})

    nc = bacc.Bacc("TRN2", target_bir_lowering=False, num_devices=1)
    arrays, aps = {}, {}
    for name, value in ins.items():
        value = np.ascontiguousarray(value)
        arrays[f"in_{name}"] = value
        aps[name] = nc.dram_tensor(f"in_{name}", value.shape, mybir.dt.from_np(value.dtype), kind="ExternalInput").ap()
    out = nc.dram_tensor("out_x", (T, D), F32, kind="ExternalOutput").ap()
    trunk(nc, aps["x"], {k: aps[k] for k in STREAMED}, aps["par"], aps["lamv"], aps["wf1"], aps["wf2"], aps["bf"],
          aps["wf3"], aps["hyb"], aps["nffn"], aps["wr"], aps["cst"], aps["dft"], aps["decay"], aps["zt"],
          aps["moec"], out)
    result = run_bass_kernel_spmd(nc, [arrays], core_ids=[0])
    return result.results[0]["out_x"].reshape(1, T, D)
```
